# Optimizing a Trainium2 kernel written in Bass

```python
import math
import jax, jax.numpy as jnp
from jax import lax
import numpy as np

D_MODEL = 1024
BATCH = 1
SEQ = 256
DEPTH = 2

D_MIX = D_MODEL
SSM_WIDTH = D_MIX // 2
SSM_CH = 16
SSM_GROUPS = SSM_WIDTH // SSM_CH
SSM_STATE = 64
GM_WIDTH = D_MIX - SSM_WIDTH
GM_HEADS = 4
GM_HEAD_DIM = GM_WIDTH // GM_HEADS
GM_CHUNK = 128
D_FF = ((8 * D_MODEL // 3 + 127) // 128) * 128
IN_COLS = SSM_WIDTH + 2 * GM_WIDTH
EPS = 1e-6
DT_MIN = 1e-3
DT_MAX = 1e-1

kernel_name = "hybrid_s5_gmlp_macaron"

def rmsnorm(x, g):
    xf = x.astype(jnp.float32)
    y = xf * lax.rsqrt(jnp.mean(xf * xf, axis=-1, keepdims=True) + EPS)
    return (y * g.astype(jnp.float32)).astype(x.dtype)

def swiglu(h, w_in, w_out):
    gu = h @ w_in
    g, u = gu[..., :D_FF], gu[..., D_FF:]
    return (jax.nn.silu(g) * u) @ w_out

def s5_group(u, a_re, a_im, log_dt, b_re, b_im, c_re, c_im, d_skip, glu_w, glu_b):
    bsz, seq = u.shape[0], u.shape[1]
    f32 = jnp.float32
    ug = u.reshape(bsz, seq, SSM_GROUPS, SSM_CH).astype(f32)
    lam = lax.complex(a_re.astype(f32), a_im.astype(f32))
    dt = jnp.exp(log_dt.astype(f32))[:, None]
    lam_bar = jnp.exp(lam * dt)
    b_mat = lax.complex(b_re.astype(f32), b_im.astype(f32))
    b_bar = ((lam_bar - 1.0) / lam)[..., None] * b_mat
    bu = jnp.einsum('blgc,gpc->blgp', ug, b_bar)
    a_elems = jnp.broadcast_to(lam_bar, (seq, SSM_GROUPS, SSM_STATE))

    def combine(left, right):
        a_l, b_l = left
        a_r, b_r = right
        return a_r * a_l, a_r * b_l + b_r

    def scan_one(bu_b):
        _, h = lax.associative_scan(combine, (a_elems, bu_b), axis=0)
        return h

    h = jax.vmap(scan_one)(bu)
    c_mat = lax.complex(c_re.astype(f32), c_im.astype(f32))
    y = jnp.einsum('blgp,gcp->blgc', h, c_mat).real + d_skip.astype(f32) * ug
    y = jax.nn.gelu(y)
    z = jnp.einsum('blgc,gce->blge', y, glu_w.astype(f32)) + glu_b.astype(f32)
    out = z[..., :SSM_CH] * jax.nn.sigmoid(z[..., SSM_CH:])
    return out.reshape(bsz, seq, SSM_WIDTH).astype(u.dtype)

def gmlp_group(u, v, v_gain, w_s, b_s):
    bsz, seq = u.shape[0], u.shape[1]
    u = jax.nn.gelu(u)
    v = jax.nn.gelu(v).reshape(bsz, seq // GM_CHUNK, GM_CHUNK, GM_HEADS, GM_HEAD_DIM)
    v = rmsnorm(v, v_gain.reshape(GM_HEADS, GM_HEAD_DIM))
    mask = jnp.tril(jnp.ones((GM_CHUNK, GM_CHUNK), dtype=bool))
    ws = jnp.where(mask[None], w_s, jnp.zeros_like(w_s))
    s = jnp.einsum('hts,bnshd->bnthd', ws, v) + b_s.T[None, None, :, :, None]
    return u * s.reshape(bsz, seq, GM_WIDTH)

def setup_inputs(seed: int = 0) -> dict:
    key = jax.random.key(seed)
    ks = jax.random.split(key, 26)
    f32 = jnp.float32
    nrm = lambda k, shape, scale: scale * jax.random.normal(k, shape, f32)
    gain = lambda k, shape: 1.0 + 0.05 * jax.random.normal(k, shape, f32)
    n_idx = jnp.arange(SSM_STATE, dtype=f32)
    return {
        "x": jax.random.normal(ks[0], (BATCH, SEQ, D_MODEL), f32),
        "norm_ffn1": gain(ks[1], (DEPTH, D_MODEL)),
        "ffn1_w_in": nrm(ks[2], (DEPTH, D_MODEL, 2 * D_FF), D_MODEL ** -0.5),
        "ffn1_w_out": nrm(ks[3], (DEPTH, D_FF, D_MODEL), D_FF ** -0.5),
        "norm_mix": gain(ks[4], (DEPTH, D_MODEL)),
        "mix_w_in": nrm(ks[5], (DEPTH, D_MODEL, IN_COLS), D_MODEL ** -0.5),
        "ssm_a_re": -0.5 + nrm(ks[6], (DEPTH, SSM_GROUPS, SSM_STATE), 0.01),
        "ssm_a_im": math.pi * n_idx + nrm(ks[7], (DEPTH, SSM_GROUPS, SSM_STATE), 0.01),
        "ssm_log_dt": jax.random.uniform(ks[8], (DEPTH, SSM_GROUPS), f32,
                                         math.log(DT_MIN), math.log(DT_MAX)),
        "ssm_b_re": nrm(ks[9], (DEPTH, SSM_GROUPS, SSM_STATE, SSM_CH), (2 * SSM_CH) ** -0.5),
        "ssm_b_im": nrm(ks[10], (DEPTH, SSM_GROUPS, SSM_STATE, SSM_CH), (2 * SSM_CH) ** -0.5),
        "ssm_c_re": nrm(ks[11], (DEPTH, SSM_GROUPS, SSM_CH, SSM_STATE), (2 * SSM_STATE) ** -0.5),
        "ssm_c_im": nrm(ks[12], (DEPTH, SSM_GROUPS, SSM_CH, SSM_STATE), (2 * SSM_STATE) ** -0.5),
        "ssm_d": nrm(ks[13], (DEPTH, SSM_GROUPS, SSM_CH), 1.0),
        "ssm_glu_w": nrm(ks[14], (DEPTH, SSM_GROUPS, SSM_CH, 2 * SSM_CH), SSM_CH ** -0.5),
        "ssm_glu_b": nrm(ks[15], (DEPTH, SSM_GROUPS, 2 * SSM_CH), 0.02),
        "gm_v_gain": gain(ks[16], (DEPTH, GM_WIDTH)),
        "gm_w_s": nrm(ks[17], (DEPTH, GM_HEADS, GM_CHUNK, GM_CHUNK), 0.5 * GM_CHUNK ** -0.5),
        "gm_b_s": 1.0 + nrm(ks[18], (DEPTH, GM_HEADS, GM_CHUNK), 0.1),
        "gain_ssm_out": gain(ks[19], (DEPTH, SSM_WIDTH)),
        "gain_gm_out": gain(ks[20], (DEPTH, GM_WIDTH)),
        "mix_w_out": nrm(ks[21], (DEPTH, D_MIX, D_MODEL), D_MIX ** -0.5),
        "norm_ffn2": gain(ks[22], (DEPTH, D_MODEL)),
        "ffn2_w_in": nrm(ks[23], (DEPTH, D_MODEL, 2 * D_FF), D_MODEL ** -0.5),
        "ffn2_w_out": nrm(ks[24], (DEPTH, D_FF, D_MODEL), D_FF ** -0.5),
        "norm_final": gain(ks[25], (D_MODEL,)),
    }

def reference(x, norm_ffn1, ffn1_w_in, ffn1_w_out, norm_mix, mix_w_in,
              ssm_a_re, ssm_a_im, ssm_log_dt, ssm_b_re, ssm_b_im, ssm_c_re, ssm_c_im,
              ssm_d, ssm_glu_w, ssm_glu_b, gm_v_gain, gm_w_s, gm_b_s,
              gain_ssm_out, gain_gm_out, mix_w_out, norm_ffn2, ffn2_w_in, ffn2_w_out,
              norm_final):
    for l in range(DEPTH):
        x = x + 0.5 * swiglu(rmsnorm(x, norm_ffn1[l]), ffn1_w_in[l], ffn1_w_out[l])
        z = rmsnorm(x, norm_mix[l]) @ mix_w_in[l]
        u_ssm = z[..., :SSM_WIDTH]
        u_gm = z[..., SSM_WIDTH:SSM_WIDTH + GM_WIDTH]
        v_gm = z[..., SSM_WIDTH + GM_WIDTH:]
        y_ssm = s5_group(u_ssm, ssm_a_re[l], ssm_a_im[l], ssm_log_dt[l],
                         ssm_b_re[l], ssm_b_im[l], ssm_c_re[l], ssm_c_im[l],
                         ssm_d[l], ssm_glu_w[l], ssm_glu_b[l])
        y_gm = gmlp_group(u_gm, v_gm, gm_v_gain[l], gm_w_s[l], gm_b_s[l])
        y = jnp.concatenate([rmsnorm(y_ssm, gain_ssm_out[l]),
                             rmsnorm(y_gm, gain_gm_out[l])], axis=-1)
        x = x + y @ mix_w_out[l]
        x = x + 0.5 * swiglu(rmsnorm(x, norm_ffn2[l]), ffn2_w_in[l], ffn2_w_out[l])
    return rmsnorm(x, norm_final)


_drawn_inputs = setup_inputs


def setup_inputs(seed=0):
    import zlib

    import numpy as np

    out = dict(_drawn_inputs(seed))
    spreads = {}
    factors = {'ssm_a_re': 200.0,
     'ssm_glu_b': 2.83,
     'gm_v_gain': 5.142,
     'norm_ffn2': 2.919,
     'ssm_a_im': 26.688,
     'ssm_log_dt': 26.976,
     'ssm_b_re': 35.792,
     'ssm_b_im': 36.144,
     'ssm_c_re': 36.472,
     'ssm_c_im': 36.96}
    for name, (base, spread) in spreads.items():
        noise = np.random.default_rng([zlib.crc32(name.encode()), seed]).standard_normal(out[name].shape)
        drawn = base * np.exp(spread * noise) if base else spread * noise
        out[name] = __import__('jax').numpy.asarray(drawn.astype(out[name].dtype))
    for name, factor in factors.items():
        out[name] = (out[name] * factor).astype(out[name].dtype)
    return out
```

```python
import math
from contextlib import ExitStack

import numpy as np
import concourse.bass as bass
from concourse import mybir

F32 = mybir.dt.float32
F32R = mybir.dt.float32r
I32 = mybir.dt.int32
ALU = mybir.AluOpType
ACT = mybir.ActivationFunctionType
AXX = mybir.AxisListType.X

DEPTH, L, D, P = 2, 256, 1024, 128
FF = 2816
KT = D // P
FT = FF // P
NB = KT // 2
G, CH, ST = 32, 16, 64
NQ = G // 2
T = 4
NC = L // T
HEADS = 4
EPS = 1e-6

RAW, RING = 3, 3
FFN_CH = FT + FT // 2
MIX0 = FFN_CH
FFN2 = MIX0 + 10
CHUNKS = FFN2 + FFN_CH
HALVES = 2 * CHUNKS
RAW_USES = [len([c for c in range(CHUNKS) if c % RAW == s]) for s in range(RAW)]
ACCS = 3 * (2 * FT + 8)
PREP = 16
LOADS = 22


def half_count(l, h):
    return l * HALVES + h + 1 + RING


def slot_free_count(l, h):
    first = {0: 2, 1: 3, 2: 1}
    return l * HALVES + (first[h] if h in first else h - RING + 1 + RING)


def raw_free_count(l, c):
    first = {0: 6, 1: 2, 2: 4}
    return l * HALVES + (first[c] if c in first else 2 * c + 2)


def build(nc, a, out):
    stack = ExitStack()
    with stack:
        def sb(name, shape, dt=F32):
            return stack.enter_context(nc.sbuf_tensor(name, shape, dt))

        def sem(name):
            return stack.enter_context(nc.semaphore(name))

        with ExitStack() as first_use:
            h_hi = first_use.enter_context(nc.sbuf_tensor("h_hi", [P, FT, L], F32R))
            h_lo = first_use.enter_context(nc.sbuf_tensor("h_lo", [P, FT, L], F32R))
        gw = sb("gw", [P, NQ, 2, P])
        u_blk = sb("u_blk", [P, NQ, 2, 32])
        t1 = sb("t1", [P, NQ, NC])
        t2 = sb("t2", [P, NQ, NC])
        t3 = sb("t3", [P, NQ, NC])
        ug = sb("ug", [P, 2, 512])
        vg = sb("vg", [P, 2, 512])
        vn = sb("vn", [P, 2, 512])
        x_in = [t.rearrange("p q n -> p (q n)") for t in (t1[:], t2[:])]
        y_out = [t.rearrange("p h d -> p (h d)") for t in (ug[:], vg[:])]
        with ExitStack() as first_use:
            bp = first_use.enter_context(nc.sbuf_tensor("bp", [P, 4, 2, 4, T, CH], F32))
            b_raw = first_use.enter_context(nc.sbuf_tensor("b_raw", [P, 2, NQ, CH], F32))
        h_re = sb("h_re", [P, NQ, NC + 1])
        h_im = sb("h_im", [P, NQ, NC + 1])
        pad = sb("pad", [P, (10240 - 8 * NQ * (NC + 1)) // 4])

        raw = sb("raw", [P, RAW, 2048])
        w_hi = sb("w_hi", [P, RING, 1024], F32R)
        w_lo = sb("w_lo", [P, RING, 1024], F32R)
        x = sb("x", [P, KT, L])
        x_hi = sb("x_hi", [P, KT, L], F32R)
        x_lo = sb("x_lo", [P, KT, L], F32R)
        cw = sb("cw", [P, 2, NQ, T + 1, 2, CH])
        eb = sb("eb", [P, NQ, 2, P])
        kt_w = sb("kt_w", [P, NQ, T, 32])
        cosn = sb("cosn", [P, NQ, NC])
        sinn = sb("sinn", [P, NQ, NC])
        decay = sb("decay", [P, NQ, NC])
        gw_c = sb("gw_c", [32, NQ, 2, 32])
        ws_raw = sb("ws_raw", [P, HEADS, P])
        ws_p = sb("ws_p", [P, HEADS, P])
        ws_t = ws_raw
        vgain = sb("vgain", [P, 512])
        vg_row = sb("vg_row", [1, 512])
        ident = sb("ident", [P, P])
        ones = sb("ones", [P, P])
        neg_half = sb("neg_half", [P, 1])
        neg_one = sb("neg_one", [P, 1])
        gain_rows = ws_p[0:DEPTH * 32 + 8, 0, :]
        gains = sb("gains", [P, DEPTH * 32 + 8])
        gain = sb("gain", [P, 32])
        gate_s = sb("gate_s", [P, L])
        up_s = sb("up_s", [P, L])
        hid = up_s
        xs2 = sb("xs2", [P, NB, L])
        ms = sb("ms", [P, L])
        rstd = ms
        ms_c = sb("ms_c", [P, 2])
        rstd_c = sb("rstd_c", [P, 2])
        w1 = sb("w1", [P, 2, 4, T, 2, CH])
        m_sb = sb("m_sb", [P, NQ, 32])
        c_raw = sb("c_raw", [P, 2, 2, P])
        cd = bp[:, 0:2].rearrange("p a r b s c -> p (a r b s c)").rearrange(
            "p (e r q c) -> p e r q c", e=2, r=2, c=CH)
        pt1 = sb("pt1", [P, NQ * 32])
        pt2 = sb("pt2", [P, NQ * 32])
        xsq = pt1
        spk = sb("spk", [16, 6, P])
        sraw = sb("sraw", [16, 98])
        bs_raw = sb("bs_raw", [HEADS, P])
        bs_p = sb("bs_p", [HEADS, P])
        sv = sb("sv", [P, 100])
        b1h = sb("b1h", [P, NQ])
        sc = sb("sc", [P, 36, NQ])
        ki = sb("ki", [P, 2 * NQ], I32)
        vss = sb("vss", [P, 8])
        vms = sb("vms", [P, 8])
        vrs = sb("vrs", [P, 8])
        oss = sb("oss", [P, 4])
        oms = sb("oms", [P, 4])
        ors = sb("ors", [P, 4])

        bank = [stack.enter_context(nc.psum_tensor(f"bank{i}", [P, 512], F32)) for i in range(4)]
        acc = stack.enter_context(nc.psum_tensor("acc", [P, NB, 512], F32))
        e_re = acc[:, 0:2, :].rearrange("p b (q n) -> p (b q) n", n=NC)
        e_im = acc[:, 2:4, :].rearrange("p b (q n) -> p (b q) n", n=NC)

        raw_full = [sem(f"raw_full{i}") for i in range(RAW)]
        small_full = sem("small_full")
        x_full = sem("x_full")
        stored = sem("stored")
        hi_done, lo_done, half_done = sem("hi_done"), sem("lo_done"), sem("half_done")
        gu_read, gate_done, silu_done = sem("gu_read"), sem("gate_done"), sem("silu_done")
        hid_done, hhi_done, hlo_done = sem("hid_done"), sem("hhi_done"), sem("hlo_done")
        acc_done, x_done = sem("acc_done"), sem("x_done")
        xhi_done, xlo_done = sem("xhi_done"), sem("xlo_done")
        sq_done, ssq_done, ms_done, rstd_done = sem("sq_done"), sem("ssq_done"), sem("ms_done"), sem("rstd_done")
        const_done, in_t, gain_t, gain_done = sem("const_done"), sem("in_t"), sem("gain_t"), sem("gain_done")
        gain_cp = sem("gain_cp")
        pool_chain = sem("pool_chain")
        pe_held, pool_held, sp_held = sem("pe_held"), sem("pool_held"), sem("sp_held")
        small_done, w1_done, prep_mm, prep_ev = sem("small_done"), sem("w1_done"), sem("prep_mm"), sem("prep_ev")
        msb_done, ktw_done, tables_done, gw_done = sem("msb_done"), sem("ktw_done"), sem("tables_done"), sem("gw_done")
        ku_done = sem("ku_done")
        zs_done, u_done, e_done, rot_done, turn_done = sem("zs_done"), sem("u_done"), sem("e_done"), sem("rot_done"), sem("turn_done")
        scan_done, un_done, state_done = sem("scan_done"), sem("un_done"), sem("state_done")
        v_done, vsq_done, vss_done, vms_done, vrs_done, vn_done = (
            sem("v_done"), sem("vsq_done"), sem("vss_done"), sem("vms_done"), sem("vrs_done"), sem("vn_done"))
        ug_done, s_done, gm_done = sem("ug_done"), sem("s_done"), sem("gm_done")
        y_done, yg_done, z_done, zb_done, tanh_done, o_done, yt_done = (
            sem("y_done"), sem("yg_done"), sem("z_done"), sem("zb_done"), sem("tanh_done"), sem("o_done"), sem("yt_done"))
        oss_done, oms_done, ors_done, on_done, yT_done = (
            sem("oss_done"), sem("oms_done"), sem("ors_done"), sem("on_done"), sem("yT_done"))
        fin_x, fin_t, fin_y = sem("fin_x"), sem("fin_t"), sem("fin_y")

        yh_done = sem("yh_done")

        fin_banks = ((bank[0][:, :], bank[1][:, :]), (acc[:, 0, :], acc[:, 1, :]))

        def zs(h):
            return (t1, t2)[h][:].rearrange("p q n -> p (q n)")[:, 0:512]

        def x_fin(k):
            return (t1, t2)[k // 4][:].rearrange("p q n -> p (q n)")[:, (k % 4) * L:(k % 4) * L + L]

        def spread(ap, n):
            return ap.unsqueeze(2).broadcast_to([ap.shape[0], ap.shape[1], n])

        block = stack.enter_context(nc.Block())

        @block.sync
        def _(sp):
            def load(l, c, it, src, view):
                s = c % RAW
                sp.wait_ge(lo_done, raw_free_count(l, c) + it * 6)
                sp.sem_inc(sp_held, 1)
                sp.dma_start(view(raw[:, s, :]), src).then_inc(raw_full[s], 32)

            def load_up(l, c, it, w_in, f):
                base = w_in[l].rearrange("(t p) m -> p t m", p=P)
                s = c % RAW
                sp.wait_ge(lo_done, raw_free_count(l, c) + it * 6)
                sp.sem_inc(sp_held, 1)
                for half in range(2):
                    sp.dma_start(
                        raw[:, s, 1024 * half:1024 * half + 1024].rearrange("p (t m) -> p t m", t=KT),
                        base[:, :, bass.ds(f * P + half * FF, P)]).then_inc(raw_full[s], 16)

            def load_down(l, c, it, w_out, k2):
                src = w_out[l, bass.ds(k2 * 2 * P, 2 * P), :].rearrange("(t p) m -> p t m", p=P)
                load(l, c, it, src, lambda r: r.rearrange("p (t m) -> p t m", t=2))

            def load_ffn(l, c0, w_in, w_out):
                for f in range(3):
                    load_up(l, c0 + f, 0, w_in, f)
                with sp.Fori(0, 6) as it:
                    for k in range(3):
                        load_up(l, c0 + 3 + k, it, w_in, it * 3 + 3 + k)
                load_up(l, c0 + 21, 0, w_in, 21)
                for k in range(2):
                    load_down(l, c0 + FT + k, 0, w_out, k)
                with sp.Fori(0, 3) as it:
                    for k in range(3):
                        load_down(l, c0 + FT + 2 + k, it, w_out, it * 3 + 2 + k)

            def small(dst, src):
                sp.dma_start(dst, src).then_inc(small_full, 16)

            xv = a["x"][0].rearrange("(h n j) d -> j n h d", j=T, n=32)
            for j in range(T):
                for h in range(2):
                    sp.dma_start(x_in[h][32 * j:32 * j + 32, :], xv[j, :, h, :]).then_inc(x_full, 16)
            for l in range(DEPTH):
                for i, name in enumerate(("norm_ffn1", "norm_mix", "norm_ffn2")):
                    sp.dma_start(gain_rows[l * 32 + i * 8:l * 32 + i * 8 + 8, :],
                                 a[name][l].rearrange("(t p) -> t p", p=P)).then_inc(x_full, 16)
                for i, name in enumerate(("gain_ssm_out", "gain_gm_out")):
                    sp.dma_start(gain_rows[l * 32 + 24 + i * 4:l * 32 + 28 + i * 4, :],
                                 a[name][l].rearrange("(t p) -> t p", p=P)).then_inc(x_full, 16)
            sp.dma_start(gain_rows[DEPTH * 32:DEPTH * 32 + 8, :],
                         a["norm_final"].rearrange("(t p) -> t p", p=P)).then_inc(x_full, 16)
            sp.wait_ge(const_done, 1)
            with sp.Fori(0, DEPTH) as l:
                sp.wait_ge(lo_done, raw_free_count(l, 0))
                sp.sem_inc(sp_held, 1)
                small(spk[:, 0, :], a["ssm_a_re"][l].rearrange("(q g) p -> q (g p)", g=2))
                small(spk[:, 1, :], a["ssm_a_im"][l].rearrange("(q g) p -> q (g p)", g=2))
                small(sraw[:, 0:2], a["ssm_log_dt"][l].rearrange("(q g) -> q g", g=2))
                small(sraw[:, 2:34], a["ssm_d"][l].rearrange("(q g) c -> q (g c)", g=2))
                small(sraw[:, 34:98], a["ssm_glu_b"][l].rearrange("(q g) e -> q (g e)", g=2))
                small(bs_raw[:, :], a["gm_b_s"][l])
                small(ws_raw[:, :, :], a["gm_w_s"][l].rearrange("h t s -> t h s"))
                for i, name in enumerate(("ssm_c_re", "ssm_c_im")):
                    for q8 in range(2):
                        for g2 in range(2):
                            small(c_raw[:, i, q8, g2 * ST:(g2 + 1) * ST],
                                  a[name][l].rearrange("(q g) c p -> q g c p", g=2)[8 * q8:8 * q8 + 8, g2])
                for i, name in enumerate(("ssm_b_re", "ssm_b_im")):
                    small(b_raw[:, i, :, :], a[name][l].rearrange("(q g) p c -> (g p) q c", g=2))
                small(vg_row[:, :], a["gm_v_gain"][bass.ds(l, 1), :])
                gl = a["ssm_glu_w"][l].rearrange("(q g) c (f e) -> g f c q e", g=2, f=2)
                for g2 in range(2):
                    for f in range(2):
                        small(gw_c[g2 * CH:(g2 + 1) * CH, :, f, g2 * CH:(g2 + 1) * CH], gl[g2, f])
                load_ffn(l, 0, a["ffn1_w_in"], a["ffn1_w_out"])
                for k in range(6):
                    col = (0, 1024, 512)[k // 2]
                    src = a["mix_w_in"][l, (k % 2) * 512:(k % 2) * 512 + 512, col:col + 512]
                    load(l, MIX0 + k, 0, src.rearrange("(t p) m -> p t m", p=P),
                         lambda r: r.rearrange("p (t m) -> p t m", t=4))
                for k in range(4):
                    k2 = (k + 2) % 4
                    load_down(l, MIX0 + 6 + k, 0, a["mix_w_out"], k2)
                load_ffn(l, FFN2, a["ffn2_w_in"], a["ffn2_w_out"])
            ov = out[0].rearrange("(h n j) d -> h j n d", j=T, n=32)
            for h in range(2):
                sp.wait_ge(fin_y, 2 * h + 2)
                for j in range(T):
                    sp.dma_start(ov[h, j], y_out[h][32 * j:32 * j + 32, :]).then_inc(stored, 16)
            sp.wait_ge(stored, 2 * T * 16)

        @block.tensor
        def _(pe):
            mm = nc.tensor.matmul

            def split_ready(l, h, it=0):
                pe.wait_ge(lo_done, l * HALVES + h + 1 + 6 + it * 6)

            def three(o, hi_a, lo_a, hi_b, lo_b, first, last):
                mm(o, hi_a, hi_b, start=first, stop=False)
                mm(o, hi_a, lo_b, start=False, stop=False)
                return mm(o, lo_a, hi_b, start=False, stop=last)

            def up_chunk(l, c, it, ffn_i, f):
                pe.wait_ge(gu_read, l * 2 * FT + ffn_i * FT + max(f + 1, 3) + it * 3)
                o = bank[f % 3]
                for half in range(2):
                    h = 2 * c + half
                    s = h % RING
                    split_ready(l, h, it)
                    for k in range(KT):
                        if c in (0, FFN2) and half == 0:
                            pe.wait_ge(xlo_done, l * 32 + (24 if c else 0) + k + 1)
                        w = slice(k * P, k * P + P)
                        last = three(o[:, half * L:half * L + L], w_hi[:, s, w], w_lo[:, s, w],
                                     x_hi[:, k, :], x_lo[:, k, :], k == 0, k == KT - 1)
                    last.then_inc(half_done, 1)

            def down_half(l, h, it, hi_b, lo_b, first, last):
                s = h % RING
                split_ready(l, h, it)
                for m in range(KT):
                    w = slice(m * P, m * P + P)
                    o = acc[:, m // 2, (m % 2) * L:(m % 2) * L + L]
                    mm(o, w_hi[:, s, w], hi_b, start=first and m % 2 == 0, stop=False, skip_group_check=True)
                    mm(o, w_hi[:, s, w], lo_b, start=False, stop=False, skip_group_check=True)
                    ins = mm(o, w_lo[:, s, w], hi_b, start=False, stop=last, skip_group_check=True)
                    if m == KT - 1:
                        ins.then_inc(half_done, 1)
                    elif m % 2:
                        ins.then_inc(acc_done, 1)

            def bank3_free(l, k):
                if k:
                    pe.wait_ge(prep_ev, l * PREP + k)
                else:
                    pe.wait_ge(ms_done, l * 3 + 1)

            def norm_sum(l, n):
                for b in range(NB):
                    pe.wait_ge(sq_done, l * 12 + 4 * n + b + 1)
                    ins = mm(bank[3][:, 0:L], ones[:, :], xs2[:, b, :], start=b == 0, stop=b == NB - 1)
                ins.then_inc(ssq_done, 1)

            def norm_sum_col(done):
                pe.wait_ge(sq_done, done)
                for h in range(2):
                    for b in range(NB):
                        ins = mm(bank[3][:, h:h + 1], xs2[:, b, h * P:h * P + P], ones[:, 0:1],
                                 start=b == 0, stop=b == NB - 1)
                ins.then_inc(ssq_done, 1)

            def prep_small(l):
                bank3_free(l, 0)
                pe.wait_ge(small_done, l * 2 + 1)
                pe.sem_inc(pe_held, 1)
                for i in range(6):
                    nc.tensor.transpose(bank[3][:, 16 * i:16 * i + 16], spk[:, i, :], ident[0:16, 0:16])
                nc.tensor.transpose(bank[3][:, 96:100], bs_p[:, :], ident[0:4, 0:4]).then_inc(prep_mm, 1)

            def prep_c(l):
                bank3_free(l, 1)
                pe.wait_ge(small_full, (l * LOADS + LOADS) * 16)
                for i in range(2):
                    for q8 in range(2):
                        ins = nc.tensor.transpose(bank[3][:, (2 * i + q8) * P:(2 * i + q8 + 1) * P],
                                                  c_raw[:, i, q8, :], ident[:, :])
                ins.then_inc(prep_mm, 1)

            def prep_ws(l):
                bank3_free(l, 14)
                pe.wait_ge(small_done, l * 2 + 2)
                for i in range(HEADS):
                    ins = nc.tensor.transpose(bank[3][:, i * P:(i + 1) * P], ws_p[:, i, :], ident[:, :])
                ins.then_inc(prep_mm, 1)

            def prep_gain(l):
                bank3_free(l, 15)
                mm(bank[3][:, :], ones[0:1, :], vg_row[:, :], start=True, stop=True).then_inc(prep_mm, 1)

            def prep_group(l, it, k):
                pe.wait_ge(prep_ev, l * PREP + 2 + k + it * 3)
                if k == 0:
                    pe.wait_ge(w1_done, l * 4 + it + 1)
                if k < 2:
                    for q in range(4):
                        ins = nc.tensor.transpose(bank[3][:, q * P:(q + 1) * P],
                                                  w1[:, k, q].rearrange("p s g c -> p (s g c)"), ident[:, :])
                else:
                    for q in range(4):
                        for r in range(2):
                            ins = mm(bank[3][:, q * 32:(q + 1) * 32],
                                     w1[:, r, q].rearrange("p s g c -> p (s g c)"),
                                     cw[:, r, bass.ds(it * 4 + q, 1), 0, :, :].rearrange("p q g c -> p (q g c)"),
                                     start=r == 0, stop=r == 1)
                ins.then_inc(prep_mm, 1)

            def ffn(l, ffn_i, c0):
                up_chunk(l, c0, 0, ffn_i, 0)
                norm_sum(l, 2 * ffn_i)
                up_chunk(l, c0 + 1, 0, ffn_i, 1)
                if ffn_i == 0:
                    prep_small(l)
                up_chunk(l, c0 + 2, 0, ffn_i, 2)
                if ffn_i == 0:
                    prep_c(l)
                    with pe.Fori(0, 2) as it:
                        for k in range(3):
                            up_chunk(l, c0 + 3 + k, it, 0, 3 + k)
                    with pe.Fori(0, 4) as it:
                        for k in range(3):
                            up_chunk(l, c0 + 9 + k, it, 0, 9 + k)
                            prep_group(l, it, k)
                else:
                    with pe.Fori(0, 6) as it:
                        for k in range(3):
                            up_chunk(l, c0 + 3 + k, it, ffn_i, 3 + k)
                up_chunk(l, c0 + 21, 0, ffn_i, 21)
                if ffn_i == 0:
                    prep_ws(l)
                base = l * 2 * FT + ffn_i * FT
                pe.wait_ge(hlo_done, base + 22)
                d0 = 2 * (c0 + FT)
                for k in range(4):
                    down_half(l, d0 + k, 0, h_hi[:, k, :], h_lo[:, k, :], k == 0, False)
                    if k == 1 and ffn_i == 0:
                        prep_gain(l)
                pe.wait_ge(hlo_done, base + 23)
                pe.sem_inc(pe_held, 1)
                with pe.Fori(0, 2) as it:
                    for k in range(6):
                        r = bass.ds(it * 6 + 4 + k, 1)
                        down_half(l, d0 + 4 + k, it, h_hi[:, r, :].rearrange("p a c -> p (a c)"),
                                  h_lo[:, r, :].rearrange("p a c -> p (a c)"), False, False)
                for k in range(6):
                    down_half(l, d0 + 16 + k, 0, h_hi[:, 16 + k, :], h_lo[:, 16 + k, :], False, k == 5)

            def in_chunk(l, k, banks):
                for half in range(2):
                    h = 2 * (MIX0 + k) + half
                    s = h % RING
                    split_ready(l, h)
                    for k2 in range(2):
                        kt = (k % 2) * 4 + half * 2 + k2
                        if k < 2:
                            pe.wait_ge(xlo_done, l * 32 + 8 + kt + 1)
                        w = slice(k2 * 512, k2 * 512 + 512)
                        for hh in range(2):
                            t = slice(hh * P, hh * P + P)
                            last = three(bank[banks[hh]][:, :], x_hi[:, kt, t], x_lo[:, kt, t],
                                         w_hi[:, s, w], w_lo[:, s, w], kt == 0, kt == KT - 1)
                    last.then_inc(half_done, 1)

            pe.wait_ge(const_done, 2)
            pe.wait_ge(x_full, 16 * (8 + 5 * DEPTH + 1))
            for b in range(NB):
                for k in range(2):
                    for h in range(2):
                        c = (2 * b + k) * P
                        ins = nc.tensor.transpose(acc[:, b, k * L + h * P:k * L + h * P + P],
                                                  x_in[h][:, c:c + P], ident[:, :])
                ins.then_inc(in_t, 1)
            nr = DEPTH * 32 + 8
            nc.tensor.transpose(bank[3][:, 0:nr], gain_rows[:, :], ident[0:nr, 0:nr]).then_inc(gain_t, 1)
            pe.sem_inc(half_done, RING)
            pe.wait_ge(gain_done, 1)

            with pe.Fori(0, DEPTH) as l:
                ffn(l, 0, 0)

                in_chunk(l, 0, (0, 1))
                norm_sum_col(l * 12 + 8)
                in_chunk(l, 1, (0, 1))
                pe.wait_ge(ms_done, l * 3 + 2)
                in_chunk(l, 2, (2, 3))
                pe.wait_ge(u_done, l * 2 + 2)
                pe.wait_ge(prep_ev, l * PREP + 14)
                for r, e in enumerate((e_re, e_im)):
                    for q in range(NQ):
                        ins = mm(e[:, q, :], eb[:, q, r, :], u_blk[:, q].rearrange("p h n -> p (h n)"),
                                 start=True, stop=True)
                ins.then_inc(e_done, 1)
                in_chunk(l, 3, (2, 3))
                in_chunk(l, 4, (0, 1))
                in_chunk(l, 5, (0, 1))
                pe.wait_ge(vn_done, l * 8 + 8)
                pe.wait_ge(prep_ev, l * PREP + 16)
                for i in range(HEADS):
                    ins = mm(bank[2 + i // 2][:, (i % 2) * L:(i % 2) * L + L], ws_t[:, i, :],
                             vn[:, :, i * P:(i + 1) * P], start=True, stop=True)
                ins.then_inc(s_done, 1)

                def turn(src):
                    for b in range(2):
                        for i in (2 * b, 2 * b + 1):
                            for h in range(2):
                                ins = nc.tensor.transpose(
                                    bank[b][:, (i % 2) * L + h * P:(i % 2) * L + h * P + P],
                                    src[:, h, i * P:(i + 1) * P], ident[:, :])
                        ins.then_inc(yT_done, 1)

                pe.wait_ge(on_done, l * 4 + 2)
                turn(vg)
                pe.wait_ge(gm_done, l * 4 + 4)
                pe.wait_ge(state_done, l * 2 + 2)
                pe.wait_ge(ktw_done, l * 10 + 10)
                for q in range(NQ):
                    o = bank[2 + q // 8][:, (q % 8) * NC:(q % 8 + 1) * NC]
                    mm(o, kt_w[:, q].rearrange("p j c -> p (j c)"), u_blk[:, q].rearrange("p h n -> p (h n)"),
                       start=True, stop=False)
                    mm(o, cw[:, 0, q, 1:T + 1].rearrange("p j g c -> p (j g c)"), h_re[:, q, 0:NC],
                       start=False, stop=False)
                    ins = mm(o, cw[:, 1, q, 1:T + 1].rearrange("p j g c -> p (j g c)"), h_im[:, q, 0:NC],
                             start=False, stop=True)
                    if q % 8 == 7:
                        ins.then_inc(y_done, 1)

                def out_chunk(k, first, last):
                    for half in range(2):
                        kt = (4 + 2 * k + half) % KT
                        down_half(l, 2 * (MIX0 + 6 + k) + half, 0, x_hi[:, kt, :], x_lo[:, kt, :],
                                  first and half == 0, last and half == 1)

                pe.wait_ge(xlo_done, l * 32 + 20)
                out_chunk(0, True, False)
                pe.wait_ge(gw_done, l + 1)
                for hf in range(2):
                    pe.wait_ge(yg_done, l * 2 + 2)
                    for f in range(2):
                        for q in range(8):
                            ins = mm(bank[2 * hf + f][:, q * NC:(q + 1) * NC], gw[:, 8 * hf + q, f, :],
                                     t1[:, 8 * hf + q, :], start=True, stop=True)
                    ins.then_inc(z_done, 1)
                out_chunk(1, False, False)
                pe.wait_ge(on_done, l * 4 + 4)
                turn(ug)
                pe.wait_ge(xlo_done, l * 32 + 24)
                out_chunk(2, False, False)
                out_chunk(3, False, True)

                ffn(l, 1, FFN2)

            norm_sum_col(DEPTH * 12 + 4)
            pe.wait_ge(fin_x, KT)
            for h in range(2):
                for k in range(KT):
                    src = x_fin(k)[:, h * P:h * P + P]
                    ins = nc.tensor.transpose(fin_banks[h][k // 4][:, (k % 4) * P:(k % 4 + 1) * P], src, ident[:, :])
                ins.then_inc(fin_t, 1)

        @block.scalar
        def _(act):
            A = nc.scalar.activation

            def split(l, c, it=0):
                s = c % RAW
                act.wait_ge(raw_full[s], (l * RAW_USES[s] + c // RAW + 1 + it) * 32)
                for half in range(2):
                    h = 2 * c + half
                    act.wait_ge(half_done, slot_free_count(l, h) + it * 6)
                    A(w_hi[:, h % RING, :], raw[:, s, half * 1024:half * 1024 + 1024], ACT.Copy).then_inc(hi_done, 1)

            def norm_in(l, n):
                for k in range(KT):
                    if k % 2 == 0:
                        act.wait_ge(x_done, l * 12 + 4 * n + k // 2 + 1)
                    if n == 2 and k == 2:
                        act.wait_ge(half_done, half_count(l, 2 * FFN2 - 1))
                    A(x_hi[:, k, :], x[:, k, :], ACT.Copy, scale=gain[:, n * 8 + k:n * 8 + k + 1]).then_inc(xhi_done, 1)

            def hidden(l, ffn_i, f, it=None):
                n = l * 2 * FT + ffn_i * FT + f + 1 + (0 if it is None else it * 3)
                act.wait_ge(gate_done, n)
                A(gate_s[:, :], gate_s[:, :], ACT.Silu).then_inc(silu_done, 1)
                act.wait_ge(hid_done, n)
                if it is None:
                    dst = h_hi[:, f, :]
                else:
                    dst = h_hi[:, bass.ds(it * 3 + f, 1), :].rearrange("p a c -> p (a c)")
                A(dst, hid[:, :], ACT.Copy).then_inc(hhi_done, 1)

            def evac(l, k, dst, src, it=0):
                act.wait_ge(prep_mm, l * PREP + k + 1 + it * 3)
                A(dst, src, ACT.Copy).then_inc(prep_ev, 1)

            def prep_group(l, it, k):
                q = bass.ds(it * 4, 4)
                if k < 2:
                    evac(l, 2 + k, eb[:, q, k, :], bank[3][:, :].rearrange("p (q m) -> p q m", q=4), it)
                else:
                    evac(l, 4, m_sb[:, q, :], bank[3][:, 0:P].rearrange("p (q m) -> p q m", q=4), it)

            def ffn(l, ffn_i, c0):
                split(l, c0 + 1)
                hidden(l, ffn_i, 0)
                split(l, c0 + 2)
                hidden(l, ffn_i, 1)
                if ffn_i == 0:
                    evac(l, 0, sv[:, :], bank[3][:, 0:100])
                split(l, c0 + 3)
                hidden(l, ffn_i, 2)
                if ffn_i == 0:
                    act.wait_ge(prep_mm, l * PREP + 2)
                    A(cd[:, 0, 0].rearrange("p q c -> p (q c)"), bank[3][:, 0:256], ACT.Copy)
                    A(cd[:, 0, 1].rearrange("p q c -> p (q c)"), bank[3][:, 256:512], ACT.Copy,
                      scale=-1.0).then_inc(prep_ev, 1)
                    with act.Fori(0, 2) as it:
                        for k in range(3):
                            split(l, c0 + 4 + k, it)
                            hidden(l, 0, 3 + k, it)
                    with act.Fori(0, 4) as it:
                        for k in range(3):
                            split(l, c0 + 10 + k, it)
                            hidden(l, 0, 9 + k, it)
                            prep_group(l, it, k)
                else:
                    with act.Fori(0, 6) as it:
                        for k in range(3):
                            split(l, c0 + 4 + k, it)
                            hidden(l, ffn_i, 3 + k, it)
                split(l, c0 + 22)
                hidden(l, ffn_i, 21)
                if ffn_i == 0:
                    evac(l, 14, ws_t[:].rearrange("p i (j n) -> p i j n", j=T),
                         bank[3][:, :].rearrange("p (i n j) -> p i j n", i=HEADS, j=T))
                split(l, c0 + 23)
                if ffn_i == 0:
                    evac(l, 15, vgain[:, :], bank[3][:, :])
                with act.Fori(0, 3) as it:
                    for k in range(3):
                        split(l, c0 + 24 + k, it)

            act.wait_ge(gain_t, 1)
            A(gains[:, :], bank[3][:, 0:DEPTH * 32 + 8], ACT.Copy).then_inc(gain_done, 1)
            with act.Fori(0, DEPTH) as l:
                split(l, 0)
                act.wait_ge(gain_cp, l + 1)
                norm_in(l, 0)
                ffn(l, 0, 0)
                split(l, MIX0)
                norm_in(l, 1)
                split(l, MIX0 + 1)
                split(l, MIX0 + 2)
                act.wait_ge(rstd_done, l * 3 + 2)
                act.wait_ge(half_done, half_count(l, 2 * MIX0 + 3))
                for h in range(2):
                    A(zs(h), bank[h][:, :], ACT.Copy, scale=rstd_c[:, h:h + 1]).then_inc(zs_done, 1)
                split(l, MIX0 + 3)
                split(l, MIX0 + 4)
                act.wait_ge(half_done, half_count(l, 2 * MIX0 + 7))
                for h in range(2):
                    A(vg[:, h, :], bank[2 + h][:, :], ACT.Gelu_apprx_tanh, scale=rstd_c[:, h:h + 1]).then_inc(v_done, 1)
                act.wait_ge(v_done, l * 2 + 2)
                A(vn[:, :, :], vg[:, :, :], ACT.Square).then_inc(vsq_done, 1)
                split(l, MIX0 + 5)
                split(l, MIX0 + 6)
                act.wait_ge(half_done, half_count(l, 2 * MIX0 + 11))
                for h in range(2):
                    A(ug[:, h, :], bank[h][:, :], ACT.Gelu_apprx_tanh, scale=rstd_c[:, h:h + 1]).then_inc(ug_done, 1)

                def row_sums(src, n):
                    for h in range(2):
                        if n or h:
                            act.wait_ge(oss_done, l * 4 + 2 * n + h)
                        A(xsq[:, :], src[:, h, :], ACT.Square,
                          accum_out=oss[:, 2 * n + h:2 * n + h + 1]).then_inc(oss_done, 1)

                act.wait_ge(gm_done, l * 4 + 4)
                row_sums(vg, 0)
                for hf in range(2):
                    act.wait_ge(y_done, l * 2 + hf + 1)
                    A(t1[:, 8 * hf:8 * hf + 8, :].rearrange("p q n -> p (q n)"), bank[2 + hf][:, :],
                      ACT.Gelu_apprx_tanh).then_inc(yg_done, 1)
                split(l, MIX0 + 7)
                for hf in range(2):
                    act.wait_ge(zb_done, l * 4 + 2 * hf + 1)
                    A(t2[:, 8 * hf:8 * hf + 8, :], t2[:, 8 * hf:8 * hf + 8, :], ACT.Tanh,
                      scale=0.5).then_inc(tanh_done, 1)
                split(l, MIX0 + 8)
                act.wait_ge(yt_done, l * 2 + 2)
                row_sums(ug, 1)
                split(l, MIX0 + 9)
                split(l, FFN2)
                norm_in(l, 2)
                ffn(l, 1, FFN2)

        @block.vector
        def _(dve):
            TT, TS, STT = nc.vector.tensor_tensor, nc.vector.tensor_scalar, nc.vector.scalar_tensor_tensor

            def split(l, c, it=0):
                s = c % RAW
                for half in range(2):
                    h = 2 * c + half
                    dve.wait_ge(hi_done, l * HALVES + h + 1 + it * 6)
                    TT(w_lo[:, h % RING, :], raw[:, s, half * 1024:half * 1024 + 1024],
                       w_hi[:, h % RING, :].bitcast(F32), ALU.subtract).then_inc(lo_done, 1)

            def norm_lo(l, n, k):
                dve.wait_ge(xhi_done, l * 24 + n * 8 + k + 1)
                STT(x_lo[:, k, :], x[:, k, :], gain[:, n * 8 + k:n * 8 + k + 1], x_hi[:, k, :].bitcast(F32),
                    ALU.mult, ALU.subtract).then_inc(xlo_done, 1)

            def residual(l, b, accs, last_half, scale):
                if b < NB - 1:
                    dve.wait_ge(acc_done, l * ACCS + accs + b + 1)
                else:
                    dve.wait_ge(half_done, half_count(l, last_half))
                xb = x[:, 2 * b:2 * b + 2, :].rearrange("p k c -> p (k c)")
                STT(xb, acc[:, b, :], scale, xb, ALU.mult, ALU.add).then_inc(x_done, 1)

            def residual_norm(l, n, accs, last_half, scale):
                residual(l, 0, accs, last_half, scale)
                for b in range(NB):
                    if b < NB - 1:
                        residual(l, b + 1, accs, last_half, scale)
                    norm_lo(l, n, 2 * b)
                    norm_lo(l, n, 2 * b + 1)

            def mean(l, n):
                dve.wait_ge(ssq_done, l * 3 + n + 1)
                if n == 1:
                    TS(ms_c[:, :], bank[3][:, 0:2], 1.0 / D, EPS, ALU.mult, ALU.add).then_inc(ms_done, 1)
                else:
                    TS(ms[:, :], bank[3][:, 0:L], 1.0 / D, EPS, ALU.mult, ALU.add).then_inc(ms_done, 1)

            def hidden(l, ffn_i, c0, f, it=None):
                step = 0 if it is None else it
                n = l * 2 * FT + ffn_i * FT + f + 1 + step * 3
                dve.wait_ge(half_done, half_count(l, 2 * (c0 + f) + 1) + step * 6)
                if f == 0:
                    dve.wait_ge(rstd_done, l * 3 + 2 * ffn_i + 1)
                o = bank[f % 3]
                TT(gate_s[:, :], o[:, 0:L], rstd[:, :], ALU.mult).then_inc(gate_done, 1)
                dve.wait_ge(hlo_done, n)
                TT(up_s[:, :], o[:, L:2 * L], rstd[:, :], ALU.mult).then_inc(gu_read, 1)
                dve.wait_ge(silu_done, n)
                dve.wait_ge(gu_read, n + 3)
                TT(hid[:, :], gate_s[:, :], up_s[:, :], ALU.mult).then_inc(hid_done, 1)
                dve.wait_ge(hhi_done, n)
                if it is None:
                    hi, lo = h_hi[:, f, :], h_lo[:, f, :]
                else:
                    r = bass.ds(it * 3 + f, 1)
                    hi, lo = (t[:, r, :].rearrange("p a c -> p (a c)") for t in (h_hi, h_lo))
                TT(lo, hid[:, :], hi.bitcast(F32), ALU.subtract).then_inc(hlo_done, 1)

            def ffn(l, ffn_i, c0):
                split(l, c0 + 1)
                mean(l, 2 * ffn_i)
                hidden(l, ffn_i, c0, 0)
                for f in (1, 2):
                    split(l, c0 + 1 + f)
                    hidden(l, ffn_i, c0, f)
                with dve.Fori(0, 6) as it:
                    for k in range(3):
                        split(l, c0 + 4 + k, it)
                        hidden(l, ffn_i, c0, 3 + k, it)
                split(l, c0 + 22)
                hidden(l, ffn_i, c0, 21)
                split(l, c0 + 23)
                if ffn_i == 0:
                    dve.wait_ge(msb_done, l + 1)
                    for j in range(T):
                        for s in range(j + 1):
                            r = 32 * (T - 1 - (j - s))
                            nc.vector.tensor_copy(kt_w[32 * s:32 * s + 32, :, j, :],
                                                  m_sb[r:r + 32, :, :]).then_inc(ktw_done, 1)
                with dve.Fori(0, 3) as it:
                    for k in range(3):
                        split(l, c0 + 24 + k, it)

            dve.sem_inc(lo_done, 6)
            dve.sem_inc(hlo_done, 1)
            dve.sem_inc(gu_read, 3)
            for b in range(NB):
                dve.wait_ge(in_t, b + 1)
                nc.vector.tensor_copy(x[:, 2 * b:2 * b + 2, :].rearrange("p k c -> p (k c)"),
                                      acc[:, b, :]).then_inc(x_done, 1)
            with dve.Fori(0, DEPTH) as l:
                dve.wait_ge(gain_done, 1)
                nc.vector.tensor_copy(gain[:, :], gains[:, bass.ds(l * 32, 32)]).then_inc(gain_cp, 1)
                dve.wait_ge(gain_cp, l + 1)
                split(l, 0)
                for k in range(KT):
                    norm_lo(l, 0, k)
                ffn(l, 0, 0)

                split(l, MIX0)
                residual_norm(l, 1, 3 * (2 * FT - 22) - 3, 2 * MIX0 - 1, 0.5)
                split(l, MIX0 + 1)
                mean(l, 1)
                split(l, MIX0 + 2)
                for h in range(2):
                    dve.wait_ge(zs_done, l * 2 + h + 1)
                    nc.vector.transpose(u_blk[:, :, h, :], zs(h).rearrange("p (q c) -> p q c", c=32)).then_inc(u_done, 1)
                split(l, MIX0 + 3)
                dve.wait_ge(e_done, l + 1)
                dve.wait_ge(u_done, l * 2 + 2)
                dve.wait_ge(tables_done, l + 1)
                dve.wait_ge(ku_done, l + 1)
                TT(t1[:, :, :], e_re, cosn[:, :, :], ALU.mult).then_inc(rot_done, 1)
                TT(t3[:, :, :], e_im, sinn[:, :, :], ALU.mult).then_inc(rot_done, 1)
                TT(t2[:, :, :], e_im, cosn[:, :, :], ALU.mult).then_inc(rot_done, 1)
                TT(h_re[:, :, 1:NC + 1], e_re, sinn[:, :, :], ALU.mult).then_inc(rot_done, 1)
                split(l, MIX0 + 4)
                flat = "p q n -> p (q n)"
                dve.wait_ge(turn_done, l * 2 + 1)
                nc.vector.tensor_tensor_scan(t3[:].rearrange(flat), decay[:].rearrange(flat), t1[:].rearrange(flat),
                                             0.0, ALU.mult, ALU.add).then_inc(scan_done, 1)
                dve.wait_ge(turn_done, l * 2 + 2)
                dve.wait_ge(scan_done, l * 2 + 1)
                nc.vector.tensor_tensor_scan(t1[:].rearrange(flat), decay[:].rearrange(flat), t2[:].rearrange(flat),
                                             0.0, ALU.mult, ALU.add).then_inc(scan_done, 1)
                split(l, MIX0 + 5)
                dve.wait_ge(vsq_done, l + 1)
                nc.vector.tensor_reduce(vss[:, :], vn[:].rearrange("p h (i d) -> p (h i) d", d=P), AXX,
                                        ALU.add).then_inc(vss_done, 1)
                dve.wait_ge(vss_done, l + 1)
                TS(vms[:, :], vss[:, :], 1.0 / P, EPS, ALU.mult, ALU.add).then_inc(vms_done, 1)
                dve.wait_ge(scan_done, l * 2 + 2)
                TT(h_re[:, :, 1:NC + 1], t3[:, :, :], cosn[:, :, :], ALU.mult).then_inc(un_done, 1)
                TT(t2[:, :, :], t1[:, :, :], sinn[:, :, :], ALU.mult).then_inc(un_done, 1)
                TT(h_im[:, :, 1:NC + 1], t3[:, :, :], sinn[:, :, :], ALU.mult).then_inc(un_done, 1)
                dve.wait_ge(un_done, l * 4 + 3)
                TT(t3[:, :, :], t1[:, :, :], cosn[:, :, :], ALU.mult).then_inc(un_done, 1)
                split(l, MIX0 + 6)
                dve.wait_ge(vrs_done, l + 1)
                dve.wait_ge(prep_ev, l * PREP + 16)
                for h in range(2):
                    for i in range(HEADS):
                        w = slice(i * P, i * P + P)
                        STT(vn[:, h, w], vg[:, h, w], vrs[:, h * HEADS + i:h * HEADS + i + 1], vgain[:, w],
                            ALU.mult, ALU.mult).then_inc(vn_done, 1)
                dve.wait_ge(s_done, l + 1)
                dve.wait_ge(ug_done, l * 2 + 2)
                dve.wait_ge(vn_done, l * 8 + 8)
                for i in range(HEADS):
                    w = slice(i * P, i * P + P)
                    STT(vg[:, :, w], bank[2 + i // 2][:, (i % 2) * L:(i % 2) * L + L].rearrange("p (h d) -> p h d", h=2),
                        sv[:, 96 + i:97 + i], ug[:, :, w], ALU.add, ALU.mult).then_inc(gm_done, 1)

                def out_norm(y, n):
                    dve.wait_ge(oss_done, l * 4 + 2 * n + 2)
                    TS(oms[:, 2 * n:2 * n + 2], oss[:, 2 * n:2 * n + 2], 1.0 / 512, EPS, ALU.mult,
                       ALU.add).then_inc(oms_done, 1)
                    dve.wait_ge(ors_done, l * 2 + n + 1)
                    for h in range(2):
                        TS(y[:, h, :], y[:, h, :], ors[:, 2 * n + h:2 * n + h + 1], None, ALU.mult).then_inc(on_done, 1)

                def out_split(first, n):
                    for i in range(4):
                        k = first + i
                        src = bank[i // 2][:, (i % 2) * L:(i % 2) * L + L]
                        g = gain[:, 24 + k:25 + k]
                        dve.wait_ge(yT_done, l * 4 + 2 * n + i // 2 + 1)
                        TS(x_hi[:, k, :], src, g, None, ALU.mult).then_inc(yh_done, 1)
                        dve.wait_ge(yh_done, l * 8 + 4 * n + i + 1)
                        STT(x_lo[:, k, :], src, g, x_hi[:, k, :].bitcast(F32), ALU.mult,
                            ALU.subtract).then_inc(xlo_done, 1)

                out_norm(vg, 0)
                out_split(4, 0)
                split(l, MIX0 + 7)
                for hf in range(2):
                    dve.wait_ge(z_done, l * 2 + hf + 1)
                    q = slice(8 * hf, 8 * hf + 8)
                    v = [bank[2 * hf + f][:, :].rearrange("p (q n) -> p q n", n=NC) for f in range(2)]
                    TT(t2[:, q, :], v[1], spread(sv[:, 80 + 8 * hf:88 + 8 * hf], NC), ALU.add).then_inc(zb_done, 1)
                    STT(t3[:, q, :], v[0], 0.5, spread(b1h[:, q], NC), ALU.mult, ALU.add).then_inc(zb_done, 1)
                for hf in range(2):
                    dve.wait_ge(tanh_done, l * 2 + hf + 1)
                    dve.wait_ge(zb_done, l * 4 + 2 * hf + 2)
                    q = slice(8 * hf, 8 * hf + 8)
                    STT(t3[:, q, :], t2[:, q, :], 1.0, t3[:, q, :], ALU.add, ALU.mult).then_inc(o_done, 1)
                dve.wait_ge(o_done, l * 2 + 2)
                for h in range(2):
                    nc.vector.transpose(ug[:, h, :].rearrange("p (q c) -> p q c", c=32),
                                        t3[:, :, 32 * h:32 * h + 32]).then_inc(yt_done, 1)
                split(l, MIX0 + 8)
                out_norm(ug, 1)
                out_split(0, 1)
                split(l, MIX0 + 9)
                split(l, FFN2)
                residual_norm(l, 2, 3 * 22 + 3 * 8 - 3, 2 * FFN2 - 1, 1.0)
                ffn(l, 1, FFN2)
                for b in range(NB):
                    residual(l, b, ACCS - 3, HALVES - 1, 0.5)

            dve.wait_ge(x_done, DEPTH * 12 + NB)
            for k in range(KT):
                TS(x_fin(k), x[:, k, :], gains[:, DEPTH * 32 + k:DEPTH * 32 + k + 1], None, ALU.mult).then_inc(fin_x, 1)
            dve.wait_ge(ssq_done, 3 * DEPTH + 1)
            TS(ms_c[:, :], bank[3][:, 0:2], 1.0 / D, EPS, ALU.mult, ALU.add).then_inc(ms_done, 1)
            dve.wait_ge(rstd_done, 3 * DEPTH + 1)
            for h in range(2):
                dve.wait_ge(fin_t, h + 1)
                for b in range(2):
                    TS(y_out[h][:, b * 512:b * 512 + 512], fin_banks[h][b], rstd_c[:, h:h + 1], None,
                       ALU.mult).then_inc(fin_y, 1)

        @block.gpsimd
        def _(pool):
            steps = [0]

            def link(ins):
                steps[0] += 1
                ins.then_inc(pool_chain, 1)
                pool.wait_ge(pool_chain, steps[0])

            def restart():
                steps[0] = 0
                pool.sem_inc(pool_held, 1)
                pool.sem_clear(pool_chain)

            def tt(o, x0, x1, op):
                link(nc.gpsimd.tensor_tensor(o, x0, x1, op))

            def ts(o, x0, s1, s2, op0, op1):
                link(nc.gpsimd.tensor_scalar(o, x0, s1, s2, op0, op1))

            def copy(o, i):
                link(nc.gpsimd.tensor_copy(o, i))

            def inv_sqrt(o, m, done):
                n = neg_half[:, 0:1]
                ins = nc.gpsimd.tensor_tensor(o, m, n.broadcast_to([P, m.shape[1]]), ALU.pow)
                ins.then_inc(done, 1)

            def squares(l, n):
                for b in range(NB):
                    pool.wait_ge(x_done, l * 12 + 4 * n + b + 1)
                    xb = x[:, 2 * b:2 * b + 2, :].rearrange("p k c -> p (k c)")
                    tt(xsq[:, :], xb, xb, ALU.mult)
                    ins = nc.gpsimd.tensor_tensor(xs2[:, b, :], xsq[:, 0:L], xsq[:, L:2 * L], ALU.add)
                    ins.then_inc(sq_done, 1)
                    pool.wait_ge(sq_done, l * 12 + 4 * n + b + 1)

            def cmul(o_re, o_im, a_re, a_im, b_re, b_im, u, v):
                tt(u, a_re, b_re, ALU.mult)
                tt(v, a_im, b_im, ALU.mult)
                tt(o_re, u, v, ALU.subtract)
                tt(u, a_re, b_im, ALU.mult)
                tt(v, a_im, b_re, ALU.mult)
                tt(o_im, u, v, ALU.add)

            def S(i, n=1):
                return sc[:, i:i + n, :].rearrange("p i q -> p (i q)")

            MAGIC = 12582912.0

            def horner(p, z, coefs):
                ts(p, z, coefs[0], coefs[1], ALU.mult, ALU.add)
                for c in coefs[2:]:
                    tt(p, p, z, ALU.mult)
                    ts(p, p, c, None, ALU.add, ALU.bypass)

            def exp(o, arg):
                xx, k, r, t, p = S(17), S(5), S(7), S(18), S(11)
                ts(xx, arg, -200.0, 200.0, ALU.max, ALU.min)
                ts(k, xx, 1.0 / math.log(2.0), MAGIC, ALU.mult, ALU.add)
                ts(k, k, -MAGIC, None, ALU.add, ALU.bypass)
                ts(t, k, -0.693359375, None, ALU.mult, ALU.bypass)
                tt(r, xx, t, ALU.add)
                ts(t, k, 2.12194440e-4, None, ALU.mult, ALU.bypass)
                tt(r, r, t, ALU.add)
                horner(p, r, [1 / 5040, 1 / 720, 1 / 120, 1 / 24, 1 / 6, 0.5, 1.0, 1.0])
                ts(k, k, -127.0, 128.0, ALU.max, ALU.min)
                ts(ki[:, 0:NQ], k, 127.0, 8388608.0, ALU.add, ALU.mult)
                tt(o, p, ki[:, 0:NQ].bitcast(F32), ALU.mult)

            link(nc.gpsimd.memset(gw_c[:, :, :, :], 0.0))
            pool.sem_inc(const_done, 1)
            link(nc.gpsimd.memset(ident[:, :], 0.0))
            link(nc.gpsimd.affine_select(out=ident[:, :], in_=ident[:, :], compare_op=ALU.not_equal, fill=1.0,
                                         base=0, pattern=[[-1, P]], channel_multiplier=1))
            link(nc.gpsimd.memset(neg_half[:, :], -0.5))
            link(nc.gpsimd.memset(neg_one[:, :], -1.0))
            nc.gpsimd.memset(ones[:, :], 1.0).then_inc(const_done, 1)
            squares(0, 0)
            for t in (w1, cw, kt_w):
                v = t[:].rearrange(("p a b c d e -> p (a b c d e)" if len(t.shape) == 6 else "p a b c -> p (a b c)"))
                link(nc.gpsimd.memset(v, 0.0))
            restart()
            with pool.Fori(0, DEPTH) as l:
                pool.wait_ge(small_full, l * (LOADS * 16) + LOADS * 16)
                pool.sem_inc(pool_held, 1)
                copy(spk[:, 2, :].rearrange("q (g p) -> q g p", g=2), spread(sraw[:, 0:2], ST))
                for j in range(T):
                    w = slice(32 * j, 32 * j + 32)
                    copy(spk[:, 3, w], sraw[:, 2:34])
                    for f in range(2):
                        copy(spk[:, 4 + f, w].rearrange("q (g e) -> q g e", g=2),
                             sraw[:, 34:98].rearrange("q (g f e) -> q g f e", g=2, f=2)[:, :, f, :])
                ins = nc.gpsimd.tensor_copy(bs_p[:].rearrange("i (j n) -> i j n", j=T),
                                            bs_raw[:].rearrange("i (n j) -> i j n", j=T))
                ins.then_inc(small_done, 1)
                pool.wait_ge(gain_t, 1)
                link(nc.gpsimd.affine_select(out=ws_raw[:, :, :], in_=ws_raw[:, :, :],
                                             compare_op=ALU.is_ge, fill=0.0, base=0,
                                             pattern=[[0, HEADS], [-1, P]], channel_multiplier=1))
                for i in range(HEADS):
                    ins = nc.gpsimd.tensor_copy(ws_p[:, i, :].rearrange("p (j n) -> p j n", j=T),
                                                ws_raw[:, i, :].rearrange("p (n j) -> p j n", j=T))
                    if i < HEADS - 1:
                        link(ins)
                ins.then_inc(small_done, 1)
                pool.wait_ge(ms_done, l * 3 + 1)
                inv_sqrt(rstd[:, :], ms[:, :], rstd_done)
                pool.wait_ge(prep_ev, l * PREP + 2)
                pool.sem_inc(pool_held, 1)
                are, aim = sv[:, 0:16], sv[:, 16:32]
                ts(b1h[:, :], sv[:, 64:80], 0.5, None, ALU.mult, ALU.bypass)
                exp(S(0), sv[:, 32:48])
                tt(S(1), are, S(0), ALU.mult)
                tt(S(2), aim, S(0), ALU.mult)
                ts(S(3), S(2), 4.0, None, ALU.mult, ALU.bypass)
                exp(S(4), S(1))
                k, r, z, sn, cs, m, t, ca, cb = S(5, 2), S(7, 2), S(9, 2), S(11, 2), S(13, 2), S(15, 2), S(17, 2), S(19, 2), S(21, 2)
                ts(k, S(2, 2), 2.0 / math.pi, MAGIC, ALU.mult, ALU.add)
                ts(k, k, -MAGIC, None, ALU.add, ALU.bypass)
                ts(t, k, -1.5703125, None, ALU.mult, ALU.bypass)
                tt(r, S(2, 2), t, ALU.add)
                ts(t, k, -4.837512969970703125e-4, None, ALU.mult, ALU.bypass)
                tt(r, r, t, ALU.add)
                ts(t, k, -7.54978995489188216e-8, None, ALU.mult, ALU.bypass)
                tt(r, r, t, ALU.add)
                tt(z, r, r, ALU.mult)
                horner(sn, z, [-1.9515295891e-4, 8.3321608736e-3, -1.6666654611e-1])
                tt(sn, sn, z, ALU.mult)
                tt(sn, sn, r, ALU.mult)
                tt(sn, sn, r, ALU.add)
                horner(cs, z, [2.443315711809948e-5, -1.388731625493765e-3, 4.166664568298827e-2])
                tt(cs, cs, z, ALU.mult)
                ts(cs, cs, -0.5, None, ALU.add, ALU.bypass)
                tt(cs, cs, z, ALU.mult)
                ts(cs, cs, 1.0, None, ALU.add, ALU.bypass)
                ts(t, k, 0.25, MAGIC, ALU.mult, ALU.add)
                ts(t, t, -MAGIC, -4.0, ALU.add, ALU.mult)
                tt(m, k, t, ALU.add)
                ts(t, m, -1.0, 0.0, ALU.mult, ALU.max)
                ts(cb, m, 0.0, None, ALU.max, ALU.bypass)
                tt(t, t, cb, ALU.add)
                ts(ca, t, -1.0, 1.0, ALU.mult, ALU.add)
                ts(cb, t, -1.0, 2.0, ALU.mult, ALU.add)
                tt(cb, cb, m, ALU.mult)
                cmul(S(23, 2), S(25, 2), ca, cb, cs, sn, t, m)
                tt(S(27), S(4), S(23), ALU.mult)
                tt(S(28), S(4), S(25), ALU.mult)
                tt(S(29), S(4), S(4), ALU.mult)
                tt(S(29), S(29), S(29), ALU.mult)
                ts(S(35), S(28), -1.0, None, ALU.mult, ALU.bypass)
                ts(S(30), S(27), -1.0, None, ALU.add, ALU.bypass)
                tt(S(33), are, are, ALU.mult)
                tt(S(34), aim, aim, ALU.mult)
                tt(S(33), S(33), S(34), ALU.add)
                ts(S(34), aim, -1.0, None, ALU.mult, ALU.bypass)
                cmul(S(31), S(32), S(30), S(28), are, S(34), S(5), S(6))
                tt(S(33), S(33), neg_one[:, 0:1].broadcast_to([P, NQ]), ALU.pow)
                tt(S(31), S(31), S(33), ALU.mult)
                tt(S(32), S(32), S(33), ALU.mult)
                lr, li, nli = spread(S(27), CH), spread(S(28), CH), spread(S(35), CH)
                u, v = (t_[:, 0:256].rearrange("p (q c) -> p q c", c=CH) for t_ in (pt1, pt2))
                for i in range(T + 1):
                    gen = i % 2
                    if i:
                        cmul(cd[:, gen, 0], cd[:, gen, 1], lr, nli, cd[:, 1 - gen, 0], cd[:, 1 - gen, 1], u, v)
                    for g2 in range(2):
                        rows = slice(ST * g2, ST * g2 + ST)
                        copy(cw[rows, :, :, i, g2, :].rearrange("p r q c -> p (r q) c"),
                             cd[rows, gen].rearrange("p r q c -> p (r q) c"))
                cr, ci = spread(S(31), CH), spread(S(32), CH)

                def bps(r, s):
                    return bp[:, :, r, :, s, :]

                u4, v4 = (t_[:, 0:256].rearrange("p (a q c) -> p a q c", a=4, c=CH) for t_ in (pt1, pt2))

                def four(ap):
                    return ap.rearrange("p (a q) c -> p a q c", a=4)

                b4 = [b_raw[:, r].rearrange("p (a q) c -> p a q c", a=4) for r in range(2)]
                cmul4 = [four(cr), four(ci)]
                cmul(bps(0, 3), bps(1, 3), cmul4[0], cmul4[1], b4[0], b4[1], u4, v4)
                for s in (2, 1, 0):
                    cmul(bps(0, s), bps(1, s), four(lr), four(li), bps(0, s + 1), bps(1, s + 1), u4, v4)
                for i in range(4):
                    if i:
                        pool.wait_ge(prep_mm, l * PREP + 2 + 3 * i)
                        pool.sem_inc(pool_held, 1)
                    for g2 in range(2):
                        rows = slice(ST * g2, ST * g2 + ST)
                        dst = w1[rows, :, :, :, g2, :].rearrange("p r q s c -> p (r q s) c")
                        ins = nc.gpsimd.tensor_copy(dst, bp[rows, i].rearrange("p r q s c -> p (r q s) c"))
                        if g2:
                            ins.then_inc(w1_done, 1)
                            pool.wait_ge(w1_done, l * 4 + i + 1)
                            pool.sem_inc(pool_held, 1)
                        else:
                            link(ins)
                pool.wait_ge(prep_ev, l * PREP + 14)
                dg = pt1[96:128, :].rearrange("p (q c) -> p q c", c=32)
                tt(dg, ident[96:128, 96:128].unsqueeze(1).broadcast_to([32, NQ, 32]),
                   spread(sv[96:128, 48:64], 32), ALU.mult)
                nc.gpsimd.tensor_tensor(m_sb[96:128, :, :], m_sb[96:128, :, :], dg, ALU.add).then_inc(msb_done, 1)
                pool.wait_ge(msb_done, l + 1)
                pool.sem_inc(pool_held, 1)
                link(nc.gpsimd.memset(cosn[:, :, 0:1], 1.0))
                link(nc.gpsimd.memset(sinn[:, :, 0:1], 0.0))
                copy(S(0), S(24))
                copy(S(1), S(26))
                n = 1
                while n < NC:
                    big = [t_[:, 0:NQ * n].rearrange("p (q n) -> p q n", n=n) for t_ in (pt1, pt2)]
                    cmul(cosn[:, :, n:2 * n], sinn[:, :, n:2 * n], spread(S(0), n), spread(S(1), n),
                         cosn[:, :, 0:n], sinn[:, :, 0:n], big[0], big[1])
                    n *= 2
                    if n < NC:
                        cmul(S(2), S(3), S(0), S(1), S(0), S(1), S(5), S(6))
                        copy(S(0), S(2))
                        copy(S(1), S(3))
                copy(decay[:, :, :], spread(S(29), NC))
                nc.gpsimd.memset(decay[:, :, 0:1], 0.0).then_inc(tables_done, 1)

                squares(l, 1)
                pool.wait_ge(ms_done, l * 3 + 2)
                inv_sqrt(rstd_c[:, :], ms_c[:, :], rstd_done)
                link(nc.gpsimd.memset(gw[:].rearrange("p q f m -> p (q f m)"), 0.0))
                for j in range(T):
                    rows = slice(32 * j, 32 * j + 32)
                    copy(gw[rows, :, :, rows].rearrange("p q f m -> p (q f) m"),
                         gw_c[:].rearrange("p q f m -> p (q f) m"))
                pool.sem_inc(gw_done, 1)
                link(nc.gpsimd.memset(h_re[:, :, 0:1], 0.0))
                nc.gpsimd.memset(h_im[:, :, 0:1], 0.0).then_inc(ku_done, 1)
                pool.wait_ge(rot_done, l * 4 + 2)
                nc.gpsimd.tensor_tensor(t1[:, :, :], t1[:, :, :], t3[:, :, :], ALU.add).then_inc(turn_done, 1)
                pool.wait_ge(rot_done, l * 4 + 4)
                nc.gpsimd.tensor_tensor(t2[:, :, :], t2[:, :, :], h_re[:, :, 1:NC + 1], ALU.subtract).then_inc(turn_done, 1)
                pool.wait_ge(vms_done, l + 1)
                inv_sqrt(vrs[:, :], vms[:, :], vrs_done)
                pool.wait_ge(un_done, l * 4 + 2)
                nc.gpsimd.tensor_tensor(h_re[:, :, 1:NC + 1], h_re[:, :, 1:NC + 1], t2[:, :, :],
                                        ALU.subtract).then_inc(state_done, 1)
                pool.wait_ge(un_done, l * 4 + 4)
                nc.gpsimd.tensor_tensor(h_im[:, :, 1:NC + 1], h_im[:, :, 1:NC + 1], t3[:, :, :],
                                        ALU.add).then_inc(state_done, 1)
                for i in range(2):
                    pool.wait_ge(oms_done, l * 2 + i + 1)
                    inv_sqrt(ors[:, 2 * i:2 * i + 2], oms[:, 2 * i:2 * i + 2], ors_done)
                squares(l, 2)
                pool.wait_ge(ms_done, l * 3 + 3)
                inv_sqrt(rstd[:, :], ms[:, :], rstd_done)
                squares(l + 1, 0)
                restart()
            pool.wait_ge(ms_done, DEPTH * 3 + 1)
            inv_sqrt(rstd_c[:, :], ms_c[:, :], rstd_done)


_INS = ["x", "norm_ffn1", "ffn1_w_in", "ffn1_w_out", "norm_mix", "mix_w_in", "ssm_a_re", "ssm_a_im", "ssm_log_dt",
        "ssm_b_re", "ssm_b_im", "ssm_c_re", "ssm_c_im", "ssm_d", "ssm_glu_w", "ssm_glu_b", "gm_v_gain", "gm_w_s",
        "gm_b_s", "gain_ssm_out", "gain_gm_out", "mix_w_out", "norm_ffn2", "ffn2_w_in", "ffn2_w_out", "norm_final"]


def kernel(**inputs):
    import concourse.bacc as bacc
    from concourse.bass_utils import run_bass_kernel_spmd

    nc = bacc.Bacc("TRN2", target_bir_lowering=False, num_devices=1, dynamic_dma_scratch_size=1024)
    arrays = {f"in_{n}": np.ascontiguousarray(inputs[n]) for n in _INS}
    aps = {n: nc.dram_tensor(f"in_{n}", arrays[f"in_{n}"].shape, F32, kind="ExternalInput").ap() for n in _INS}
    out = nc.dram_tensor("out", (1, L, D), F32, kind="ExternalOutput").ap()
    build(nc, aps, out)
    r = run_bass_kernel_spmd(nc, [arrays], core_ids=[0])
    return r.results[0]["out"]
```

```python
import math
from contextlib import ExitStack

import numpy as np
import concourse.bass as bass
from concourse import mybir

F32 = mybir.dt.float32
F32R = mybir.dt.float32r
I32 = mybir.dt.int32
ALU = mybir.AluOpType
ACT = mybir.ActivationFunctionType
AXX = mybir.AxisListType.X

DEPTH, L, D, P = 2, 256, 1024, 128
FF = 2816
KT = D // P
FT = FF // P
NB = KT // 2
G, CH, ST = 32, 16, 64
NQ = G // 2
T = 4
NC = L // T
HEADS = 4
EPS = 1e-6

RAW, RING = 3, 3
FFN_CH = FT + FT // 2
MIX0 = FFN_CH
FFN2 = MIX0 + 10
CHUNKS = FFN2 + FFN_CH
HALVES = 2 * CHUNKS
RAW_USES = [len([c for c in range(CHUNKS) if c % RAW == s]) for s in range(RAW)]
ACCS = 3 * (2 * FT + 8)
ACC_FFN, ACC_MIX = 3 * FT, 3 * FT + 3 * 8
PREP = 8
LOADS = 22


def half_count(l, h):
    return l * HALVES + h + 1 + RING


def slot_free_count(l, h):
    first = {0: 2, 1: 3, 2: 1}
    return l * HALVES + (first[h] if h in first else h - RING + 1 + RING)


def raw_free_count(l, c):
    first = {0: 6, 1: 2, 2: 4}
    return l * HALVES + (first[c] if c in first else 2 * c + 2)


def build(nc, a, out):
    stack = ExitStack()
    with stack:
        def sb(name, shape, dt=F32):
            return stack.enter_context(nc.sbuf_tensor(name, shape, dt))

        def sem(name):
            return stack.enter_context(nc.semaphore(name))

        with ExitStack() as first_use:
            h_hi = first_use.enter_context(nc.sbuf_tensor("h_hi", [P, FT, L], F32R))
            h_lo = first_use.enter_context(nc.sbuf_tensor("h_lo", [P, FT, L], F32R))
        gw = sb("gw", [P, NQ, 2, P])
        u_blk = sb("u_blk", [P, NQ, 2, 32])
        t1 = sb("t1", [P, NQ, NC])
        t2 = sb("t2", [P, NQ, NC])
        t3 = sb("t3", [P, NQ, NC])
        ug = sb("ug", [P, 2, 512])
        vg = sb("vg", [P, 2, 512])
        vn = sb("vn", [P, 2, 512])
        x_in = [t.rearrange("p q n -> p (q n)") for t in (t1[:], t2[:])]
        y_out = [t.rearrange("p h d -> p (h d)") for t in (ug[:], vg[:])]
        with ExitStack() as first_use:
            bp = first_use.enter_context(nc.sbuf_tensor("bp", [P, 4, 2, 4, T, CH], F32))
            b_raw = first_use.enter_context(nc.sbuf_tensor("b_raw", [P, 2, NQ, CH], F32))
        h_re = sb("h_re", [P, NQ, NC + 1])
        h_im = sb("h_im", [P, NQ, NC + 1])
        pad = sb("pad", [P, (10240 - 8 * NQ * (NC + 1)) // 4])

        raw = sb("raw", [P, RAW, 2048])
        w_hi = sb("w_hi", [P, RING, 1024], F32R)
        w_lo = sb("w_lo", [P, RING, 1024], F32R)
        x = sb("x", [P, KT, L])
        x_hi = sb("x_hi", [P, KT, L], F32R)
        x_lo = sb("x_lo", [P, KT, L], F32R)
        cw = sb("cw", [P, 2, NQ, T + 1, 2, CH])
        eb = sb("eb", [P, NQ, 2, P])
        kt_w = sb("kt_w", [P, NQ, T, 32])
        cosn = sb("cosn", [P, NQ, NC])
        sinn = sb("sinn", [P, NQ, NC])
        decay = sb("decay", [P, NQ, NC])
        gw_c = sb("gw_c", [32, NQ, 2, 32])
        ws_raw = sb("ws_raw", [P, HEADS, P])
        ws_p = sb("ws_p", [P, HEADS, P])
        ws_t = ws_raw
        vgain = sb("vgain", [P, 512])
        vg_row = sb("vg_row", [1, 512])
        ident = sb("ident", [P, P])
        ones = sb("ones", [P, P])
        neg_half = sb("neg_half", [P, 1])
        neg_one = sb("neg_one", [P, 1])
        gain_rows = ws_p[0:DEPTH * 32 + 8, 0, :]
        gains = sb("gains", [P, DEPTH * 32 + 8])
        gain = sb("gain", [P, 32])
        gate_s = sb("gate_s", [P, L])
        up_s = sb("up_s", [P, L])
        hid = up_s
        xs2 = sb("xs2", [P, 3, L])
        diag = xs2[:, 2, :]
        rstd = sb("rstd", [P, L])
        two_ident = gate_s[:, 0:P]
        ms_c = sb("ms_c", [P, 2])
        rstd_c = sb("rstd_c", [P, 2])
        w1 = sb("w1", [P, 2, 4, T, 2, CH])
        m_sb = sb("m_sb", [P, NQ, 32])
        c_raw = sb("c_raw", [P, 2, 2, P])
        cd = bp[:, 0:2].rearrange("p a r b s c -> p (a r b s c)").rearrange(
            "p (e r q c) -> p e r q c", e=2, r=2, c=CH)
        pt1 = sb("pt1", [P, NQ * 32])
        pt2 = sb("pt2", [P, NQ * 32])
        xsq = [pt1, pt2]
        spk = sb("spk", [16, 6, P])
        sraw = sb("sraw", [16, 98])
        bs_raw = sb("bs_raw", [HEADS, P])
        bs_p = sb("bs_p", [HEADS, P])
        sv = sb("sv", [P, 100])
        b1h = sb("b1h", [P, NQ])
        sc = sb("sc", [P, 36, NQ])
        ki = sb("ki", [P, 2 * NQ], I32)
        vss = sb("vss", [P, 8])
        vms = sb("vms", [P, 8])
        vrs = sb("vrs", [P, 8])
        oss = sb("oss", [P, 4])
        oms = sb("oms", [P, 4])
        ors = sb("ors", [P, 4])

        bank = [stack.enter_context(nc.psum_tensor(f"bank{i}", [P, 512], F32)) for i in range(4)]
        acc = stack.enter_context(nc.psum_tensor("acc", [P, NB, 512], F32))
        e_re = acc[:, 0:2, :].rearrange("p b (q n) -> p (b q) n", n=NC)
        e_im = acc[:, 2:4, :].rearrange("p b (q n) -> p (b q) n", n=NC)

        raw_full = [sem(f"raw_full{i}") for i in range(RAW)]
        small_full = sem("small_full")
        x_full, gain_full = sem("x_full"), sem("gain_full")
        stored = sem("stored")
        hi_done, lo_done, half_done = sem("hi_done"), sem("lo_done"), sem("half_done")
        gu_read, gate_done, silu_done = sem("gu_read"), sem("gate_done"), sem("silu_done")
        hid_done, hhi_done, hlo_done = sem("hid_done"), sem("hhi_done"), sem("hlo_done")
        acc_done, x_done = sem("acc_done"), sem("x_done")
        xhi_done, xlo_done = sem("xhi_done"), sem("xlo_done")
        sqa_done, diag_done, row_done, rb_done = sem("sqa_done"), sem("diag_done"), sem("row_done"), sem("rb_done")
        sq_done, ssq_done, ms_done, rstd_done = sem("sq_done"), sem("ssq_done"), sem("ms_done"), sem("rstd_done")
        const_done, zero_done, gain_t, gain_done = sem("const_done"), sem("zero_done"), sem("gain_t"), sem("gain_done")
        gain_cp = sem("gain_cp")
        pool_chain = sem("pool_chain")
        pe_held, pool_held, sp_held, act_held = sem("pe_held"), sem("pool_held"), sem("sp_held"), sem("act_held")
        small_done, w1_done, prep_mm, prep_ev = sem("small_done"), sem("w1_done"), sem("prep_mm"), sem("prep_ev")
        msb_done, ktw_done, tables_done, gw_done = sem("msb_done"), sem("ktw_done"), sem("tables_done"), sem("gw_done")
        ku_done = sem("ku_done")
        zs_done, u_done, e_done, rot_done, turn_done = sem("zs_done"), sem("u_done"), sem("e_done"), sem("rot_done"), sem("turn_done")
        scan_done, un_done, state_done = sem("scan_done"), sem("un_done"), sem("state_done")
        v_done, vsq_done, vss_done, vms_done, vrs_done, vn_done = (
            sem("v_done"), sem("vsq_done"), sem("vss_done"), sem("vms_done"), sem("vrs_done"), sem("vn_done"))
        ug_done, s_done, gm_done = sem("ug_done"), sem("s_done"), sem("gm_done")
        y_done, yg_done, z_done, zb_done, tanh_done, o_done, yt_done = (
            sem("y_done"), sem("yg_done"), sem("z_done"), sem("zb_done"), sem("tanh_done"), sem("o_done"), sem("yt_done"))
        oss_done, oms_done, ors_done, on_done, yT_done = (
            sem("oss_done"), sem("oms_done"), sem("ors_done"), sem("on_done"), sem("yT_done"))
        fin_x, fin_t, fin_y = sem("fin_x"), sem("fin_t"), sem("fin_y")

        yh_done = sem("yh_done")

        turned = ((acc[:, 0, :], acc[:, 1, :]), (bank[2][:, :], bank[3][:, :]))
        fin_banks = ((bank[0][:, :], bank[1][:, :]), (acc[:, 0, :], acc[:, 1, :]))

        def zs(h):
            return (t1, t2)[h][:].rearrange("p q n -> p (q n)")[:, 0:512]

        def x_fin(k):
            return (t1, t2)[k // 4][:].rearrange("p q n -> p (q n)")[:, (k % 4) * L:(k % 4) * L + L]

        def spread(ap, n):
            return ap.unsqueeze(2).broadcast_to([ap.shape[0], ap.shape[1], n])

        block = stack.enter_context(nc.Block())

        @block.sync
        def _(sp):
            def load(l, c, it, src, view):
                s = c % RAW
                sp.wait_ge(lo_done, raw_free_count(l, c) + it * 6)
                sp.sem_inc(sp_held, 1)
                sp.dma_start(view(raw[:, s, :]), src).then_inc(raw_full[s], 32)

            def load_up(l, c, it, w_in, f):
                base = w_in[l].rearrange("(t p) m -> p t m", p=P)
                s = c % RAW
                sp.wait_ge(lo_done, raw_free_count(l, c) + it * 6)
                sp.sem_inc(sp_held, 1)
                for half in range(2):
                    sp.dma_start(
                        raw[:, s, 1024 * half:1024 * half + 1024].rearrange("p (t m) -> p t m", t=KT),
                        base[:, :, bass.ds(f * P + half * FF, P)]).then_inc(raw_full[s], 16)

            def load_down(l, c, it, w_out, k2):
                src = w_out[l, bass.ds(k2 * 2 * P, 2 * P), :].rearrange("(t p) m -> p t m", p=P)
                load(l, c, it, src, lambda r: r.rearrange("p (t m) -> p t m", t=2))

            def load_ffn(l, c0, w_in, w_out):
                for f in range(3):
                    load_up(l, c0 + f, 0, w_in, f)
                if c0 == 0:
                    load_small(l)
                with sp.Fori(0, 6) as it:
                    for k in range(3):
                        load_up(l, c0 + 3 + k, it, w_in, it * 3 + 3 + k)
                load_up(l, c0 + 21, 0, w_in, 21)
                for k in range(2):
                    load_down(l, c0 + FT + k, 0, w_out, k)
                with sp.Fori(0, 3) as it:
                    for k in range(3):
                        load_down(l, c0 + FT + 2 + k, it, w_out, it * 3 + 2 + k)

            def small(dst, src):
                sp.dma_start(dst, src).then_inc(small_full, 16)

            def load_small(l):
                sp.wait_ge(const_done, 1)
                small(spk[:, 0, :], a["ssm_a_re"][l].rearrange("(q g) p -> q (g p)", g=2))
                small(spk[:, 1, :], a["ssm_a_im"][l].rearrange("(q g) p -> q (g p)", g=2))
                small(sraw[:, 0:2], a["ssm_log_dt"][l].rearrange("(q g) -> q g", g=2))
                small(sraw[:, 2:34], a["ssm_d"][l].rearrange("(q g) c -> q (g c)", g=2))
                small(sraw[:, 34:98], a["ssm_glu_b"][l].rearrange("(q g) e -> q (g e)", g=2))
                small(bs_raw[:, :], a["gm_b_s"][l])
                small(ws_raw[:, :, :], a["gm_w_s"][l].rearrange("h t s -> t h s"))
                for i, name in enumerate(("ssm_c_re", "ssm_c_im")):
                    for q8 in range(2):
                        for g2 in range(2):
                            small(c_raw[:, i, q8, g2 * ST:(g2 + 1) * ST],
                                  a[name][l].rearrange("(q g) c p -> q g c p", g=2)[8 * q8:8 * q8 + 8, g2])
                for i, name in enumerate(("ssm_b_re", "ssm_b_im")):
                    small(b_raw[:, i, :, :], a[name][l].rearrange("(q g) p c -> (g p) q c", g=2))
                small(vg_row[:, :], a["gm_v_gain"][bass.ds(l, 1), :])
                gl = a["ssm_glu_w"][l].rearrange("(q g) c (f e) -> g f c q e", g=2, f=2)
                for g2 in range(2):
                    for f in range(2):
                        small(gw_c[g2 * CH:(g2 + 1) * CH, :, f, g2 * CH:(g2 + 1) * CH], gl[g2, f])

            xv = a["x"][0].rearrange("(h n j) d -> j n h d", j=T, n=32)
            for j in range(T):
                for h in range(2):
                    sp.dma_start(x_in[h][32 * j:32 * j + 32, :], xv[j, :, h, :]).then_inc(x_full, 16)
            with sp.Fori(0, DEPTH) as l:
                load_ffn(l, 0, a["ffn1_w_in"], a["ffn1_w_out"])
                for k in range(6):
                    col = (0, 1024, 512)[k // 2]
                    src = a["mix_w_in"][l, (k % 2) * 512:(k % 2) * 512 + 512, col:col + 512]
                    load(l, MIX0 + k, 0, src.rearrange("(t p) m -> p t m", p=P),
                         lambda r: r.rearrange("p (t m) -> p t m", t=4))
                for k in range(4):
                    k2 = (k + 2) % 4
                    load_down(l, MIX0 + 6 + k, 0, a["mix_w_out"], k2)
                load_ffn(l, FFN2, a["ffn2_w_in"], a["ffn2_w_out"])
            ov = out[0].rearrange("(h n j) d -> h j n d", j=T, n=32)
            for h in range(2):
                sp.wait_ge(fin_y, 2 * h + 2)
                for j in range(T):
                    sp.dma_start(ov[h, j], y_out[h][32 * j:32 * j + 32, :]).then_inc(stored, 16)
            sp.wait_ge(stored, 2 * T * 16)

        @block.tensor
        def _(pe):
            mm = nc.tensor.matmul

            def split_ready(l, h, it=0):
                pe.wait_ge(lo_done, l * HALVES + h + 1 + 6 + it * 6)

            def three(o, hi_a, lo_a, hi_b, lo_b, first, last):
                mm(o, hi_a, hi_b, start=first, stop=False)
                mm(o, hi_a, lo_b, start=False, stop=False)
                return mm(o, lo_a, hi_b, start=False, stop=last)

            def up_chunk(l, c, it, ffn_i, f):
                pe.wait_ge(gu_read, l * 2 * FT + ffn_i * FT + max(f + 1, 3) + it * 3)
                o = bank[f % 3]
                for half in range(2):
                    h = 2 * c + half
                    s = h % RING
                    split_ready(l, h, it)
                    for k in range(KT):
                        if c in (0, FFN2) and half == 0:
                            pe.wait_ge(xlo_done, l * 32 + (24 if c else 0) + k + 1)
                        w = slice(k * P, k * P + P)
                        last = three(o[:, half * L:half * L + L], w_hi[:, s, w], w_lo[:, s, w],
                                     x_hi[:, k, :], x_lo[:, k, :], k == 0, k == KT - 1)
                    last.then_inc(half_done, 1)

            def down_half(l, h, it, hi_b, lo_b, first, last):
                s = h % RING
                split_ready(l, h, it)
                for m in range(KT):
                    w = slice(m * P, m * P + P)
                    o = acc[:, m // 2, (m % 2) * L:(m % 2) * L + L]
                    mm(o, w_hi[:, s, w], hi_b, start=first and m % 2 == 0, stop=False, skip_group_check=True)
                    mm(o, w_hi[:, s, w], lo_b, start=False, stop=False, skip_group_check=True)
                    ins = mm(o, w_lo[:, s, w], hi_b, start=False, stop=last, skip_group_check=True)
                    if m == KT - 1:
                        ins.then_inc(half_done, 1)
                    elif m % 2:
                        ins.then_inc(acc_done, 1)

            def bank3_free(l, k):
                if k:
                    pe.wait_ge(prep_ev, l * PREP + k)
                else:
                    pe.wait_ge(rb_done, l * 2 + 1)

            def norm_sum(done):
                pe.wait_ge(sq_done, done)
                for h in range(2):
                    ins = mm(bank[3][:, h:h + 1], xs2[:, 0, h * P:h * P + P], ones[:, 0:1], start=True, stop=True)
                ins.then_inc(ssq_done, 1)

            def norm_row(l, ffn_i):
                pe.wait_ge(diag_done, l * 4 + 2 * ffn_i + 2)
                mm(bank[3][:, 0:L], ones[:, :], diag, start=True, stop=True).then_inc(row_done, 1)

            def prep_small(l):
                bank3_free(l, 0)
                pe.wait_ge(small_done, l * 2 + 1)
                pe.sem_inc(pe_held, 1)
                for i in range(6):
                    nc.tensor.transpose(bank[3][:, 16 * i:16 * i + 16], spk[:, i, :], ident[0:16, 0:16])
                nc.tensor.transpose(bank[3][:, 96:100], bs_p[:, :], ident[0:4, 0:4]).then_inc(prep_mm, 1)

            def prep_c(l):
                bank3_free(l, 1)
                pe.wait_ge(small_full, (l * LOADS + LOADS) * 16)
                for i in range(2):
                    for q8 in range(2):
                        ins = nc.tensor.transpose(bank[3][:, (2 * i + q8) * P:(2 * i + q8 + 1) * P],
                                                  c_raw[:, i, q8, :], ident[:, :])
                ins.then_inc(prep_mm, 1)

            def prep_ws(l):
                bank3_free(l, 2)
                pe.wait_ge(small_done, l * 2 + 2)
                for i in range(HEADS):
                    ins = nc.tensor.transpose(bank[3][:, i * P:(i + 1) * P], ws_p[:, i, :], ident[:, :])
                ins.then_inc(prep_mm, 1)

            def prep_gain(l):
                bank3_free(l, 3)
                mm(bank[3][:, :], ones[0:1, :], vg_row[:, :], start=True, stop=True).then_inc(prep_mm, 1)

            def prep_group(l, it, g):
                n = it * 2 + g
                pe.wait_ge(prep_ev, l * PREP + 4 + n)
                pe.wait_ge(w1_done, l * 4 + n + 1)
                pe.sem_inc(pe_held, 1)
                for k in range(2):
                    for q in range(4):
                        nc.tensor.transpose(bank[k][:, q * P:(q + 1) * P],
                                            w1[:, k, q].rearrange("p s g c -> p (s g c)"), ident[:, :])
                for q in range(4):
                    for r in range(2):
                        ins = mm(bank[2][:, q * 32:(q + 1) * 32],
                                 w1[:, r, q].rearrange("p s g c -> p (s g c)"),
                                 cw[:, r, bass.ds(n * 4 + q, 1), 0, :, :].rearrange("p q g c -> p (q g c)"),
                                 start=r == 0, stop=r == 1)
                ins.then_inc(prep_mm, 1)

            def ffn(l, ffn_i, c0):
                up_chunk(l, c0, 0, ffn_i, 0)
                norm_sum(l * 12 + 8 * ffn_i + 4)
                up_chunk(l, c0 + 1, 0, ffn_i, 1)
                norm_row(l, ffn_i)
                up_chunk(l, c0 + 2, 0, ffn_i, 2)
                if ffn_i == 0:
                    prep_small(l)
                up_chunk(l, c0 + 3, 0, ffn_i, 3)
                if ffn_i == 0:
                    prep_c(l)
                with pe.Fori(0, 6) as it:
                    for k in range(3):
                        up_chunk(l, c0 + 4 + k, it, ffn_i, 4 + k)
                if ffn_i == 0:
                    prep_ws(l)
                base = l * 2 * FT + ffn_i * FT
                pe.wait_ge(hlo_done, base + 22)
                d0 = 2 * (c0 + FT)
                for k in range(4):
                    down_half(l, d0 + k, 0, h_hi[:, k, :], h_lo[:, k, :], k == 0, False)
                    if k == 1 and ffn_i == 0:
                        prep_gain(l)
                pe.wait_ge(hlo_done, base + 23)
                pe.sem_inc(pe_held, 1)
                with pe.Fori(0, 2) as it:
                    for k in range(6):
                        r = bass.ds(it * 6 + 4 + k, 1)
                        down_half(l, d0 + 4 + k, it, h_hi[:, r, :].rearrange("p a c -> p (a c)"),
                                  h_lo[:, r, :].rearrange("p a c -> p (a c)"), False, False)
                        if ffn_i == 0 and k in (1, 4):
                            if k == 1:
                                pe.wait_ge(gu_read, base + FT + 3)
                            prep_group(l, it, k // 3)
                for k in range(6):
                    down_half(l, d0 + 16 + k, 0, h_hi[:, 16 + k, :], h_lo[:, 16 + k, :], False, k == 5)

            def in_half(l, k, half, banks):
                h = 2 * (MIX0 + k) + half
                s = h % RING
                split_ready(l, h)
                for k2 in range(2):
                    kt = (k % 2) * 4 + half * 2 + k2
                    if k < 2:
                        pe.wait_ge(xlo_done, l * 32 + 8 + kt + 1)
                    w = slice(k2 * 512, k2 * 512 + 512)
                    for hh in range(2):
                        t = slice(hh * P, hh * P + P)
                        last = three(bank[banks[hh]][:, :], x_hi[:, kt, t], x_lo[:, kt, t],
                                     w_hi[:, s, w], w_lo[:, s, w], kt == 0, kt == KT - 1)
                last.then_inc(half_done, 1)

            def in_chunk(l, k, banks):
                for half in range(2):
                    in_half(l, k, half, banks)

            pe.wait_ge(const_done, 2)
            pe.wait_ge(x_full, 16 * 2 * T)
            for b in range(NB):
                for k in range(2):
                    for h in range(2):
                        c = (2 * b + k) * P
                        ins = mm(acc[:, b, k * L + h * P:k * L + h * P + P], x_in[h][:, c:c + P], two_ident,
                                 start=True, stop=True)
                if b < NB - 1:
                    ins.then_inc(acc_done, 1)
                else:
                    ins.then_inc(half_done, RING)
            pe.wait_ge(gain_full, 16 * (5 * DEPTH + 1))
            nr = DEPTH * 32 + 8
            nc.tensor.transpose(bank[3][:, 0:nr], gain_rows[:, :], ident[0:nr, 0:nr]).then_inc(gain_t, 1)
            pe.wait_ge(gain_done, 1)

            with pe.Fori(0, DEPTH) as l:
                ffn(l, 0, 0)

                in_chunk(l, 0, (0, 1))
                in_half(l, 1, 0, (0, 1))
                norm_sum(l * 12 + 8)
                in_half(l, 1, 1, (0, 1))
                pe.wait_ge(ms_done, l * 3 + 2)
                in_half(l, 2, 0, (2, 3))
                pe.wait_ge(u_done, l * 2 + 2)
                pe.wait_ge(prep_ev, l * PREP + PREP)
                for r, e in enumerate((e_re, e_im)):
                    for q in range(NQ):
                        ins = mm(e[:, q, :], eb[:, q, r, :], u_blk[:, q].rearrange("p h n -> p (h n)"),
                                 start=True, stop=True)
                ins.then_inc(e_done, 1)
                in_half(l, 2, 1, (2, 3))
                in_chunk(l, 3, (2, 3))
                in_chunk(l, 4, (0, 1))
                in_chunk(l, 5, (0, 1))
                pe.wait_ge(ug_done, l * 2 + 2)
                pe.wait_ge(state_done, l * 2 + 2)
                pe.wait_ge(ktw_done, l * 10 + 10)
                for q in range(NQ):
                    o = bank[q // 8][:, (q % 8) * NC:(q % 8 + 1) * NC]
                    mm(o, kt_w[:, q].rearrange("p j c -> p (j c)"), u_blk[:, q].rearrange("p h n -> p (h n)"),
                       start=True, stop=False)
                    mm(o, cw[:, 0, q, 1:T + 1].rearrange("p j g c -> p (j g c)"), h_re[:, q, 0:NC],
                       start=False, stop=False)
                    ins = mm(o, cw[:, 1, q, 1:T + 1].rearrange("p j g c -> p (j g c)"), h_im[:, q, 0:NC],
                             start=False, stop=True)
                    if q % 8 == 7:
                        ins.then_inc(y_done, 1)
                pe.wait_ge(vn_done, l * 8 + 8)
                for i in range(HEADS):
                    ins = mm(bank[2 + i // 2][:, (i % 2) * L:(i % 2) * L + L], ws_t[:, i, :],
                             vn[:, :, i * P:(i + 1) * P], start=True, stop=True)
                ins.then_inc(s_done, 1)

                def turn(src, o):
                    for b in range(2):
                        for i in (2 * b, 2 * b + 1):
                            for h in range(2):
                                c = (i % 2) * L + h * P
                                ins = nc.tensor.transpose(o[b][:, c:c + P], src[:, h, i * P:(i + 1) * P], ident[:, :])
                        ins.then_inc(yT_done, 1)

                pe.wait_ge(gw_done, l + 1)
                for hf in range(2):
                    if hf == 0:
                        pe.wait_ge(yg_done, l * 2 + 2)
                    else:
                        pe.wait_ge(gm_done, l * 4 + 4)
                    for f in range(2):
                        for q in range(8):
                            ins = mm(bank[2 * hf + f][:, q * NC:(q + 1) * NC], gw[:, 8 * hf + q, f, :],
                                     t1[:, 8 * hf + q, :], start=True, stop=True)
                    ins.then_inc(z_done, 1)
                pe.wait_ge(on_done, l * 4 + 2)
                pe.sem_inc(pe_held, 1)
                turn(vg, turned[0])

                def out_chunk(k, first, last):
                    for half in range(2):
                        kt = (4 + 2 * k + half) % KT
                        down_half(l, 2 * (MIX0 + 6 + k) + half, 0, x_hi[:, kt, :], x_lo[:, kt, :],
                                  first and half == 0, last and half == 1)

                pe.wait_ge(xlo_done, l * 32 + 20)
                out_chunk(0, True, False)
                out_chunk(1, False, False)
                pe.wait_ge(on_done, l * 4 + 4)
                pe.sem_inc(pe_held, 1)
                turn(ug, turned[1])
                pe.wait_ge(xlo_done, l * 32 + 24)
                out_chunk(2, False, False)
                out_chunk(3, False, True)

                ffn(l, 1, FFN2)

            norm_sum(DEPTH * 12 + 4)
            pe.wait_ge(fin_x, KT)
            for h in range(2):
                for k in range(KT):
                    src = x_fin(k)[:, h * P:h * P + P]
                    ins = nc.tensor.transpose(fin_banks[h][k // 4][:, (k % 4) * P:(k % 4 + 1) * P], src, ident[:, :])
                ins.then_inc(fin_t, 1)

        @block.scalar
        def _(act):
            A = nc.scalar.activation

            def split_half(l, h, it=0):
                c = h // 2
                s = c % RAW
                if h % 2 == 0:
                    act.wait_ge(raw_full[s], (l * RAW_USES[s] + c // RAW + 1 + it) * 32)
                act.wait_ge(half_done, slot_free_count(l, h) + it * 6)
                A(w_hi[:, h % RING, :], raw[:, s, (h % 2) * 1024:(h % 2) * 1024 + 1024],
                  ACT.Copy).then_inc(hi_done, 1)

            def split(l, c, it=0):
                split_half(l, 2 * c, it)
                split_half(l, 2 * c + 1, it)

            def norm_in(l, n, c_next):
                for k in range(KT):
                    if k % 2 == 0:
                        act.wait_ge(x_done, l * 12 + 4 * n + k // 2 + 1)
                    if n == 2 and k == 2:
                        act.wait_ge(half_done, half_count(l, 2 * FFN2 - 1))
                    A(x_hi[:, k, :], x[:, k, :], ACT.Copy, scale=gain[:, n * 8 + k:n * 8 + k + 1]).then_inc(xhi_done, 1)
                split_half(l, 2 * c_next)
                if n == 1:
                    act.wait_ge(tables_done, l + 1)
                for b in range(NB):
                    if b > 1:
                        act.wait_ge(sq_done, l * 12 + 4 * n + b - 1)
                    A(xsq[b % 2][:, :], x[:, 2 * b:2 * b + 2, :].rearrange("p k c -> p (k c)"),
                      ACT.Square).then_inc(sqa_done, 1)
                split_half(l, 2 * c_next + 1)

            def hidden(l, ffn_i, f, it=None):
                n = l * 2 * FT + ffn_i * FT + f + 1 + (0 if it is None else it * 3)
                act.wait_ge(gate_done, n)
                A(gate_s[:, :], gate_s[:, :], ACT.Silu).then_inc(silu_done, 1)
                act.wait_ge(hid_done, n)
                if it is None:
                    dst = h_hi[:, f, :]
                else:
                    dst = h_hi[:, bass.ds(it * 3 + f, 1), :].rearrange("p a c -> p (a c)")
                A(dst, hid[:, :], ACT.Copy).then_inc(hhi_done, 1)

            def evac(l, k, dst, src, it=0):
                act.wait_ge(prep_mm, l * PREP + k + 1 + it * 3)
                A(dst, src, ACT.Copy).then_inc(prep_ev, 1)

            def prep_group(l, it, g):
                n = it * 2 + g
                q = bass.ds(n * 4, 4)
                act.wait_ge(prep_mm, l * PREP + 5 + n)
                act.sem_inc(act_held, 1)
                for k in range(2):
                    A(eb[:, q, k, :], bank[k][:, :].rearrange("p (q m) -> p q m", q=4), ACT.Copy)
                A(m_sb[:, q, :], bank[2][:, 0:P].rearrange("p (q m) -> p q m", q=4), ACT.Copy).then_inc(prep_ev, 1)

            def ffn(l, ffn_i, c0):
                act.wait_ge(row_done, l * 2 + ffn_i + 1)
                A(rstd[:, :], bank[3][:, 0:L], ACT.Copy).then_inc(rb_done, 1)
                hidden(l, ffn_i, 0)
                split(l, c0 + 2)
                hidden(l, ffn_i, 1)
                split(l, c0 + 3)
                hidden(l, ffn_i, 2)
                if ffn_i == 0:
                    evac(l, 0, sv[:, :], bank[3][:, 0:100])
                split(l, c0 + 4)
                hidden(l, ffn_i, 3)
                if ffn_i == 0:
                    act.wait_ge(prep_mm, l * PREP + 2)
                    A(cd[:, 0, 0].rearrange("p q c -> p (q c)"), bank[3][:, 0:256], ACT.Copy)
                    A(cd[:, 0, 1].rearrange("p q c -> p (q c)"), bank[3][:, 256:512], ACT.Copy,
                      scale=-1.0).then_inc(prep_ev, 1)
                with act.Fori(0, 5) as it:
                    for k in range(3):
                        split(l, c0 + 5 + k, it)
                        hidden(l, ffn_i, 4 + k, it)
                for f in (19, 20):
                    split(l, c0 + f + 1)
                    hidden(l, ffn_i, f)
                split(l, c0 + 22)
                hidden(l, ffn_i, 21)
                if ffn_i == 0:
                    evac(l, 2, ws_t[:].rearrange("p i (j n) -> p i j n", j=T),
                         bank[3][:, :].rearrange("p (i n j) -> p i j n", i=HEADS, j=T))
                split(l, c0 + 23)
                if ffn_i == 0:
                    evac(l, 3, vgain[:, :], bank[3][:, :])
                split(l, c0 + 24)
                with act.Fori(0, 2) as it:
                    split(l, c0 + 25, it)
                    if ffn_i == 0:
                        prep_group(l, it, 0)
                    split(l, c0 + 26, it)
                    split_half(l, 2 * c0 + 54, it)
                    if ffn_i == 0:
                        prep_group(l, it, 1)
                    split_half(l, 2 * c0 + 55, it)
                split(l, c0 + 31)
                split(l, c0 + 32)

            for l in range(DEPTH):
                for i, name in enumerate(("norm_ffn1", "norm_mix", "norm_ffn2")):
                    act.dma_start(gain_rows[l * 32 + i * 8:l * 32 + i * 8 + 8, :],
                                 a[name][l].rearrange("(t p) -> t p", p=P)).then_inc(gain_full, 16)
                for i, name in enumerate(("gain_ssm_out", "gain_gm_out")):
                    act.dma_start(gain_rows[l * 32 + 24 + i * 4:l * 32 + 28 + i * 4, :],
                                 a[name][l].rearrange("(t p) -> t p", p=P)).then_inc(gain_full, 16)
            act.dma_start(gain_rows[DEPTH * 32:DEPTH * 32 + 8, :],
                         a["norm_final"].rearrange("(t p) -> t p", p=P)).then_inc(gain_full, 16)
            act.wait_ge(gain_t, 1)
            A(gains[:, :], bank[3][:, 0:DEPTH * 32 + 8], ACT.Copy).then_inc(gain_done, 1)
            with act.Fori(0, DEPTH) as l:
                split(l, 0)
                act.wait_ge(gain_cp, l + 1)
                norm_in(l, 0, 1)
                ffn(l, 0, 0)
                split(l, MIX0)
                norm_in(l, 1, MIX0 + 1)
                split(l, MIX0 + 2)
                act.wait_ge(rstd_done, l * 3 + 2)
                act.wait_ge(half_done, half_count(l, 2 * MIX0 + 3))
                for h in range(2):
                    A(zs(h), bank[h][:, :], ACT.Copy, scale=rstd_c[:, h:h + 1]).then_inc(zs_done, 1)
                split(l, MIX0 + 3)
                split(l, MIX0 + 4)
                act.wait_ge(half_done, half_count(l, 2 * MIX0 + 7))
                for h in range(2):
                    A(vg[:, h, :], bank[2 + h][:, :], ACT.Gelu_apprx_tanh, scale=rstd_c[:, h:h + 1]).then_inc(v_done, 1)
                act.wait_ge(v_done, l * 2 + 2)
                A(vn[:, :, :], vg[:, :, :], ACT.Square).then_inc(vsq_done, 1)
                split(l, MIX0 + 5)
                split(l, MIX0 + 6)
                act.wait_ge(half_done, half_count(l, 2 * MIX0 + 11))
                for h in range(2):
                    A(ug[:, h, :], bank[h][:, :], ACT.Gelu_apprx_tanh, scale=rstd_c[:, h:h + 1]).then_inc(ug_done, 1)

                def row_sums(src, n):
                    for h in range(2):
                        A(xsq[h][:, :], src[:, h, :], ACT.Square,
                          accum_out=oss[:, 2 * n + h:2 * n + h + 1]).then_inc(oss_done, 1)

                for hf in range(2):
                    act.wait_ge(y_done, l * 2 + hf + 1)
                    A(t1[:, 8 * hf:8 * hf + 8, :].rearrange("p q n -> p (q n)"), bank[hf][:, :],
                      ACT.Gelu_apprx_tanh).then_inc(yg_done, 1)
                act.wait_ge(gm_done, l * 4 + 4)
                row_sums(vg, 0)
                for hf in range(2):
                    act.wait_ge(zb_done, l * 4 + 2 * hf + 1)
                    A(t2[:, 8 * hf:8 * hf + 8, :], t2[:, 8 * hf:8 * hf + 8, :], ACT.Tanh,
                      scale=0.5).then_inc(tanh_done, 1)
                split(l, MIX0 + 7)
                act.wait_ge(yt_done, l * 2 + 2)
                act.wait_ge(oss_done, l * 4 + 2)
                row_sums(ug, 1)
                split(l, MIX0 + 8)
                split(l, MIX0 + 9)
                split(l, FFN2)
                norm_in(l, 2, FFN2 + 1)
                ffn(l, 1, FFN2)
            for b in range(NB):
                act.wait_ge(x_done, DEPTH * 12 + b + 1)
                if b > 1:
                    act.wait_ge(sq_done, DEPTH * 12 + b - 1)
                A(xsq[b % 2][:, :], x[:, 2 * b:2 * b + 2, :].rearrange("p k c -> p (k c)"),
                  ACT.Square).then_inc(sqa_done, 1)

        @block.vector
        def _(dve):
            TT, TS, STT = nc.vector.tensor_tensor, nc.vector.tensor_scalar, nc.vector.scalar_tensor_tensor

            def split(l, c, it=0):
                s = c % RAW
                for half in range(2):
                    h = 2 * c + half
                    dve.wait_ge(hi_done, l * HALVES + h + 1 + it * 6)
                    TT(w_lo[:, h % RING, :], raw[:, s, half * 1024:half * 1024 + 1024],
                       w_hi[:, h % RING, :].bitcast(F32), ALU.subtract).then_inc(lo_done, 1)

            def norm_lo(l, n, k):
                dve.wait_ge(xhi_done, l * 24 + n * 8 + k + 1)
                STT(x_lo[:, k, :], x[:, k, :], gain[:, n * 8 + k:n * 8 + k + 1], x_hi[:, k, :].bitcast(F32),
                    ALU.mult, ALU.subtract).then_inc(xlo_done, 1)

            def residual(l, b, accs, last_half, scale):
                if b < NB - 1:
                    dve.wait_ge(acc_done, l * ACCS + accs + b + 1)
                else:
                    dve.wait_ge(half_done, half_count(l, last_half))
                xb = x[:, 2 * b:2 * b + 2, :].rearrange("p k c -> p (k c)")
                STT(xb, acc[:, b, :], scale, xb, ALU.mult, ALU.add).then_inc(x_done, 1)

            def residual_norm(l, n, accs, last_half, scale):
                residual(l, 0, accs, last_half, scale)
                for b in range(NB):
                    if b < NB - 1:
                        residual(l, b + 1, accs, last_half, scale)
                    norm_lo(l, n, 2 * b)
                    norm_lo(l, n, 2 * b + 1)

            def mean(l, n):
                dve.wait_ge(ssq_done, l * 3 + n + 1)
                TS(ms_c[:, :], bank[3][:, 0:2], 1.0 / D, EPS, ALU.mult, ALU.add).then_inc(ms_done, 1)

            def norm_diag(l, ffn_i):
                dve.wait_ge(rstd_done, l * 3 + 2 * ffn_i + 1)
                for h in range(2):
                    TS(diag[:, h * P:h * P + P], ident[:, :], rstd_c[:, h:h + 1], None, ALU.mult).then_inc(diag_done, 1)

            def hidden(l, ffn_i, c0, f, it=None):
                step = 0 if it is None else it
                n = l * 2 * FT + ffn_i * FT + f + 1 + step * 3
                dve.wait_ge(half_done, half_count(l, 2 * (c0 + f) + 1) + step * 6)
                if f == 0:
                    dve.wait_ge(rb_done, l * 2 + ffn_i + 1)
                o = bank[f % 3]
                TT(gate_s[:, :], o[:, 0:L], rstd[:, :], ALU.mult).then_inc(gate_done, 1)
                dve.wait_ge(hlo_done, n)
                TT(up_s[:, :], o[:, L:2 * L], rstd[:, :], ALU.mult).then_inc(gu_read, 1)
                dve.wait_ge(silu_done, n)
                dve.wait_ge(gu_read, n + 3)
                TT(hid[:, :], gate_s[:, :], up_s[:, :], ALU.mult).then_inc(hid_done, 1)
                dve.wait_ge(hhi_done, n)
                if it is None:
                    hi, lo = h_hi[:, f, :], h_lo[:, f, :]
                else:
                    r = bass.ds(it * 3 + f, 1)
                    hi, lo = (t[:, r, :].rearrange("p a c -> p (a c)") for t in (h_hi, h_lo))
                TT(lo, hid[:, :], hi.bitcast(F32), ALU.subtract).then_inc(hlo_done, 1)

            def ffn(l, ffn_i, c0):
                split(l, c0 + 1)
                mean(l, 2 * ffn_i)
                norm_diag(l, ffn_i)
                hidden(l, ffn_i, c0, 0)
                for f in (1, 2):
                    split(l, c0 + 1 + f)
                    hidden(l, ffn_i, c0, f)
                with dve.Fori(0, 6) as it:
                    for k in range(3):
                        split(l, c0 + 4 + k, it)
                        hidden(l, ffn_i, c0, 3 + k, it)
                split(l, c0 + 22)
                hidden(l, ffn_i, c0, 21)
                split(l, c0 + 23)
                with dve.Fori(0, 2) as it:
                    for k in range(3):
                        split(l, c0 + 24 + k, it)
                for k in range(2):
                    split(l, c0 + 30 + k)
                if ffn_i == 0:
                    dve.wait_ge(msb_done, l + 1)
                    for j in range(T):
                        for s in range(j + 1):
                            r = 32 * (T - 1 - (j - s))
                            nc.vector.tensor_copy(kt_w[32 * s:32 * s + 32, :, j, :],
                                                  m_sb[r:r + 32, :, :]).then_inc(ktw_done, 1)
                split(l, c0 + 32)

            dve.sem_inc(lo_done, 6)
            dve.sem_inc(hlo_done, 1)
            dve.sem_inc(gu_read, 3)
            nc.vector.memset(x[:, :, :], 0.0).then_inc(zero_done, 1)
            dve.wait_ge(zero_done, 1)
            with dve.Fori(0, DEPTH) as l:
                dve.wait_ge(gain_done, 1)
                nc.vector.tensor_copy(gain[:, :], gains[:, bass.ds(l * 32, 32)]).then_inc(gain_cp, 1)
                dve.wait_ge(gain_cp, l + 1)
                split(l, 0)
                residual_norm(l, 0, 0, -1, 0.5)
                ffn(l, 0, 0)

                split(l, MIX0)
                residual_norm(l, 1, ACC_FFN, 2 * MIX0 - 1, 0.5)
                split(l, MIX0 + 1)
                mean(l, 1)
                split(l, MIX0 + 2)
                for h in range(2):
                    dve.wait_ge(zs_done, l * 2 + h + 1)
                    nc.vector.transpose(u_blk[:, :, h, :], zs(h).rearrange("p (q c) -> p q c", c=32)).then_inc(u_done, 1)
                split(l, MIX0 + 3)
                dve.wait_ge(e_done, l + 1)
                dve.wait_ge(u_done, l * 2 + 2)
                dve.wait_ge(tables_done, l + 1)
                dve.wait_ge(ku_done, l + 1)
                TT(t1[:, :, :], e_re, cosn[:, :, :], ALU.mult).then_inc(rot_done, 1)
                TT(t3[:, :, :], e_im, sinn[:, :, :], ALU.mult).then_inc(rot_done, 1)
                TT(t2[:, :, :], e_im, cosn[:, :, :], ALU.mult).then_inc(rot_done, 1)
                TT(h_re[:, :, 1:NC + 1], e_re, sinn[:, :, :], ALU.mult).then_inc(rot_done, 1)
                split(l, MIX0 + 4)
                flat = "p q n -> p (q n)"
                dve.wait_ge(turn_done, l * 2 + 1)
                nc.vector.tensor_tensor_scan(t3[:].rearrange(flat), decay[:].rearrange(flat), t1[:].rearrange(flat),
                                             0.0, ALU.mult, ALU.add).then_inc(scan_done, 1)
                dve.wait_ge(turn_done, l * 2 + 2)
                dve.wait_ge(scan_done, l * 2 + 1)
                nc.vector.tensor_tensor_scan(t1[:].rearrange(flat), decay[:].rearrange(flat), t2[:].rearrange(flat),
                                             0.0, ALU.mult, ALU.add).then_inc(scan_done, 1)
                split(l, MIX0 + 5)
                dve.wait_ge(vsq_done, l + 1)
                nc.vector.tensor_reduce(vss[:, :], vn[:].rearrange("p h (i d) -> p (h i) d", d=P), AXX,
                                        ALU.add).then_inc(vss_done, 1)
                dve.wait_ge(vss_done, l + 1)
                TS(vms[:, :], vss[:, :], 1.0 / P, EPS, ALU.mult, ALU.add).then_inc(vms_done, 1)
                dve.wait_ge(scan_done, l * 2 + 2)
                TT(h_re[:, :, 1:NC + 1], t3[:, :, :], cosn[:, :, :], ALU.mult).then_inc(un_done, 1)
                TT(t2[:, :, :], t1[:, :, :], sinn[:, :, :], ALU.mult).then_inc(un_done, 1)
                TT(h_im[:, :, 1:NC + 1], t3[:, :, :], sinn[:, :, :], ALU.mult).then_inc(un_done, 1)
                dve.wait_ge(un_done, l * 4 + 3)
                TT(t3[:, :, :], t1[:, :, :], cosn[:, :, :], ALU.mult).then_inc(un_done, 1)
                split(l, MIX0 + 6)
                dve.wait_ge(vrs_done, l + 1)
                dve.wait_ge(prep_ev, l * PREP + PREP)
                for h in range(2):
                    for i in range(HEADS):
                        w = slice(i * P, i * P + P)
                        STT(vn[:, h, w], vg[:, h, w], vrs[:, h * HEADS + i:h * HEADS + i + 1], vgain[:, w],
                            ALU.mult, ALU.mult).then_inc(vn_done, 1)
                dve.wait_ge(s_done, l + 1)
                dve.wait_ge(ug_done, l * 2 + 2)
                dve.wait_ge(vn_done, l * 8 + 8)
                for i in range(HEADS):
                    w = slice(i * P, i * P + P)
                    STT(vg[:, :, w], bank[2 + i // 2][:, (i % 2) * L:(i % 2) * L + L].rearrange("p (h d) -> p h d", h=2),
                        sv[:, 96 + i:97 + i], ug[:, :, w], ALU.add, ALU.mult).then_inc(gm_done, 1)

                def out_norm(y, n):
                    dve.wait_ge(oss_done, l * 4 + 2 * n + 2)
                    TS(oms[:, 2 * n:2 * n + 2], oss[:, 2 * n:2 * n + 2], 1.0 / 512, EPS, ALU.mult,
                       ALU.add).then_inc(oms_done, 1)
                    dve.wait_ge(ors_done, l * 2 + n + 1)
                    for h in range(2):
                        TS(y[:, h, :], y[:, h, :], ors[:, 2 * n + h:2 * n + h + 1], None, ALU.mult).then_inc(on_done, 1)

                def out_split(first, n):
                    for i in range(4):
                        k = first + i
                        src = turned[n][i // 2][:, (i % 2) * L:(i % 2) * L + L]
                        g = gain[:, 24 + k:25 + k]
                        dve.wait_ge(yT_done, l * 4 + 2 * n + i // 2 + 1)
                        TS(x_hi[:, k, :], src, g, None, ALU.mult).then_inc(yh_done, 1)
                        dve.wait_ge(yh_done, l * 8 + 4 * n + i + 1)
                        STT(x_lo[:, k, :], src, g, x_hi[:, k, :].bitcast(F32), ALU.mult,
                            ALU.subtract).then_inc(xlo_done, 1)

                out_norm(vg, 0)
                for hf in range(2):
                    dve.wait_ge(z_done, l * 2 + hf + 1)
                    q = slice(8 * hf, 8 * hf + 8)
                    v = [bank[2 * hf + f][:, :].rearrange("p (q n) -> p q n", n=NC) for f in range(2)]
                    TT(t2[:, q, :], v[1], spread(sv[:, 80 + 8 * hf:88 + 8 * hf], NC), ALU.add).then_inc(zb_done, 1)
                    STT(t3[:, q, :], v[0], 0.5, spread(b1h[:, q], NC), ALU.mult, ALU.add).then_inc(zb_done, 1)
                out_split(4, 0)
                for hf in range(2):
                    dve.wait_ge(tanh_done, l * 2 + hf + 1)
                    dve.wait_ge(zb_done, l * 4 + 2 * hf + 2)
                    q = slice(8 * hf, 8 * hf + 8)
                    STT(t3[:, q, :], t2[:, q, :], 1.0, t3[:, q, :], ALU.add, ALU.mult).then_inc(o_done, 1)
                dve.wait_ge(o_done, l * 2 + 2)
                for h in range(2):
                    nc.vector.transpose(ug[:, h, :].rearrange("p (q c) -> p q c", c=32),
                                        t3[:, :, 32 * h:32 * h + 32]).then_inc(yt_done, 1)
                split(l, MIX0 + 7)
                split(l, MIX0 + 8)
                out_norm(ug, 1)
                out_split(0, 1)
                split(l, MIX0 + 9)
                split(l, FFN2)
                residual_norm(l, 2, ACC_MIX, 2 * FFN2 - 1, 1.0)
                ffn(l, 1, FFN2)
            for b in range(NB):
                residual(DEPTH, b, 0, -1, 0.5)

            dve.wait_ge(x_done, DEPTH * 12 + NB)
            for k in range(KT):
                TS(x_fin(k), x[:, k, :], gains[:, DEPTH * 32 + k:DEPTH * 32 + k + 1], None, ALU.mult).then_inc(fin_x, 1)
            dve.wait_ge(ssq_done, 3 * DEPTH + 1)
            TS(ms_c[:, :], bank[3][:, 0:2], 1.0 / D, EPS, ALU.mult, ALU.add).then_inc(ms_done, 1)
            dve.wait_ge(rstd_done, 3 * DEPTH + 1)
            for h in range(2):
                dve.wait_ge(fin_t, h + 1)
                for b in range(2):
                    TS(y_out[h][:, b * 512:b * 512 + 512], fin_banks[h][b], rstd_c[:, h:h + 1], None,
                       ALU.mult).then_inc(fin_y, 1)

        @block.gpsimd
        def _(pool):
            steps = [0]

            def link(ins):
                steps[0] += 1
                ins.then_inc(pool_chain, 1)
                pool.wait_ge(pool_chain, steps[0])

            def restart():
                steps[0] = 0
                pool.sem_inc(pool_held, 1)
                pool.sem_clear(pool_chain)

            def tt(o, x0, x1, op):
                link(nc.gpsimd.tensor_tensor(o, x0, x1, op))

            def ts(o, x0, s1, s2, op0, op1):
                link(nc.gpsimd.tensor_scalar(o, x0, s1, s2, op0, op1))

            def copy(o, i):
                link(nc.gpsimd.tensor_copy(o, i))

            def inv_sqrt(o, m, done):
                n = neg_half[:, 0:1]
                ins = nc.gpsimd.tensor_tensor(o, m, n.broadcast_to([P, m.shape[1]]), ALU.pow)
                ins.then_inc(done, 1)

            def squares(l, n):
                for b in range(NB):
                    pool.wait_ge(sqa_done, l * 12 + 4 * n + b + 1)
                    lo, hi = xsq[b % 2][:, 0:L], xsq[b % 2][:, L:2 * L]
                    if b == 0:
                        ins = nc.gpsimd.tensor_tensor(xs2[:, 0, :], lo, hi, ALU.add)
                    else:
                        tt(xs2[:, 1, :], lo, hi, ALU.add)
                        ins = nc.gpsimd.tensor_tensor(xs2[:, 0, :], xs2[:, 0, :], xs2[:, 1, :], ALU.add)
                    ins.then_inc(sq_done, 1)
                    pool.wait_ge(sq_done, l * 12 + 4 * n + b + 1)
                    pool.sem_inc(pool_held, 1)

            def cmul(o_re, o_im, a_re, a_im, b_re, b_im, u, v):
                tt(u, a_re, b_re, ALU.mult)
                tt(v, a_im, b_im, ALU.mult)
                tt(o_re, u, v, ALU.subtract)
                tt(u, a_re, b_im, ALU.mult)
                tt(v, a_im, b_re, ALU.mult)
                tt(o_im, u, v, ALU.add)

            def S(i, n=1):
                return sc[:, i:i + n, :].rearrange("p i q -> p (i q)")

            MAGIC = 12582912.0

            def horner(p, z, coefs):
                ts(p, z, coefs[0], coefs[1], ALU.mult, ALU.add)
                for c in coefs[2:]:
                    tt(p, p, z, ALU.mult)
                    ts(p, p, c, None, ALU.add, ALU.bypass)

            def exp(o, arg):
                xx, k, r, t, p = S(17), S(5), S(7), S(18), S(11)
                ts(xx, arg, -200.0, 200.0, ALU.max, ALU.min)
                ts(k, xx, 1.0 / math.log(2.0), MAGIC, ALU.mult, ALU.add)
                ts(k, k, -MAGIC, None, ALU.add, ALU.bypass)
                ts(t, k, -0.693359375, None, ALU.mult, ALU.bypass)
                tt(r, xx, t, ALU.add)
                ts(t, k, 2.12194440e-4, None, ALU.mult, ALU.bypass)
                tt(r, r, t, ALU.add)
                horner(p, r, [1 / 5040, 1 / 720, 1 / 120, 1 / 24, 1 / 6, 0.5, 1.0, 1.0])
                ts(k, k, -127.0, 128.0, ALU.max, ALU.min)
                ts(ki[:, 0:NQ], k, 127.0, 8388608.0, ALU.add, ALU.mult)
                tt(o, p, ki[:, 0:NQ].bitcast(F32), ALU.mult)

            link(nc.gpsimd.memset(gw_c[:, :, :, :], 0.0))
            pool.sem_inc(const_done, 1)
            link(nc.gpsimd.memset(ident[:, :], 0.0))
            link(nc.gpsimd.affine_select(out=ident[:, :], in_=ident[:, :], compare_op=ALU.not_equal, fill=1.0,
                                         base=0, pattern=[[-1, P]], channel_multiplier=1))
            link(nc.gpsimd.memset(two_ident, 0.0))
            link(nc.gpsimd.affine_select(out=two_ident, in_=two_ident, compare_op=ALU.not_equal, fill=2.0,
                                         base=0, pattern=[[-1, P]], channel_multiplier=1))
            link(nc.gpsimd.memset(neg_half[:, :], -0.5))
            link(nc.gpsimd.memset(neg_one[:, :], -1.0))
            nc.gpsimd.memset(ones[:, :], 1.0).then_inc(const_done, 1)
            for t in (w1, cw, kt_w):
                v = t[:].rearrange(("p a b c d e -> p (a b c d e)" if len(t.shape) == 6 else "p a b c -> p (a b c)"))
                link(nc.gpsimd.memset(v, 0.0))
            restart()
            with pool.Fori(0, DEPTH) as l:
                squares(l, 0)
                pool.wait_ge(ms_done, l * 3 + 1)
                inv_sqrt(rstd_c[:, :], ms_c[:, :], rstd_done)
                pool.wait_ge(small_full, l * (LOADS * 16) + LOADS * 16)
                pool.sem_inc(pool_held, 1)
                copy(spk[:, 2, :].rearrange("q (g p) -> q g p", g=2), spread(sraw[:, 0:2], ST))
                for j in range(T):
                    w = slice(32 * j, 32 * j + 32)
                    copy(spk[:, 3, w], sraw[:, 2:34])
                    for f in range(2):
                        copy(spk[:, 4 + f, w].rearrange("q (g e) -> q g e", g=2),
                             sraw[:, 34:98].rearrange("q (g f e) -> q g f e", g=2, f=2)[:, :, f, :])
                ins = nc.gpsimd.tensor_copy(bs_p[:].rearrange("i (j n) -> i j n", j=T),
                                            bs_raw[:].rearrange("i (n j) -> i j n", j=T))
                ins.then_inc(small_done, 1)
                pool.wait_ge(gain_t, 1)
                link(nc.gpsimd.affine_select(out=ws_raw[:, :, :], in_=ws_raw[:, :, :],
                                             compare_op=ALU.is_ge, fill=0.0, base=0,
                                             pattern=[[0, HEADS], [-1, P]], channel_multiplier=1))
                for i in range(HEADS):
                    ins = nc.gpsimd.tensor_copy(ws_p[:, i, :].rearrange("p (j n) -> p j n", j=T),
                                                ws_raw[:, i, :].rearrange("p (n j) -> p j n", j=T))
                    if i < HEADS - 1:
                        link(ins)
                ins.then_inc(small_done, 1)
                pool.wait_ge(prep_ev, l * PREP + 2)
                pool.sem_inc(pool_held, 1)
                are, aim = sv[:, 0:16], sv[:, 16:32]
                ts(b1h[:, :], sv[:, 64:80], 0.5, None, ALU.mult, ALU.bypass)
                exp(S(0), sv[:, 32:48])
                tt(S(1), are, S(0), ALU.mult)
                tt(S(2), aim, S(0), ALU.mult)
                ts(S(3), S(2), 4.0, None, ALU.mult, ALU.bypass)
                exp(S(4), S(1))
                k, r, z, sn, cs, m, t, ca, cb = S(5, 2), S(7, 2), S(9, 2), S(11, 2), S(13, 2), S(15, 2), S(17, 2), S(19, 2), S(21, 2)
                ts(k, S(2, 2), 2.0 / math.pi, MAGIC, ALU.mult, ALU.add)
                ts(k, k, -MAGIC, None, ALU.add, ALU.bypass)
                ts(t, k, -1.5703125, None, ALU.mult, ALU.bypass)
                tt(r, S(2, 2), t, ALU.add)
                ts(t, k, -4.837512969970703125e-4, None, ALU.mult, ALU.bypass)
                tt(r, r, t, ALU.add)
                ts(t, k, -7.54978995489188216e-8, None, ALU.mult, ALU.bypass)
                tt(r, r, t, ALU.add)
                tt(z, r, r, ALU.mult)
                horner(sn, z, [-1.9515295891e-4, 8.3321608736e-3, -1.6666654611e-1])
                tt(sn, sn, z, ALU.mult)
                tt(sn, sn, r, ALU.mult)
                tt(sn, sn, r, ALU.add)
                horner(cs, z, [2.443315711809948e-5, -1.388731625493765e-3, 4.166664568298827e-2])
                tt(cs, cs, z, ALU.mult)
                ts(cs, cs, -0.5, None, ALU.add, ALU.bypass)
                tt(cs, cs, z, ALU.mult)
                ts(cs, cs, 1.0, None, ALU.add, ALU.bypass)
                ts(t, k, 0.25, MAGIC, ALU.mult, ALU.add)
                ts(t, t, -MAGIC, -4.0, ALU.add, ALU.mult)
                tt(m, k, t, ALU.add)
                ts(t, m, -1.0, 0.0, ALU.mult, ALU.max)
                ts(cb, m, 0.0, None, ALU.max, ALU.bypass)
                tt(t, t, cb, ALU.add)
                ts(ca, t, -1.0, 1.0, ALU.mult, ALU.add)
                ts(cb, t, -1.0, 2.0, ALU.mult, ALU.add)
                tt(cb, cb, m, ALU.mult)
                cmul(S(23, 2), S(25, 2), ca, cb, cs, sn, t, m)
                tt(S(27), S(4), S(23), ALU.mult)
                tt(S(28), S(4), S(25), ALU.mult)
                tt(S(29), S(4), S(4), ALU.mult)
                tt(S(29), S(29), S(29), ALU.mult)
                ts(S(35), S(28), -1.0, None, ALU.mult, ALU.bypass)
                ts(S(30), S(27), -1.0, None, ALU.add, ALU.bypass)
                tt(S(33), are, are, ALU.mult)
                tt(S(34), aim, aim, ALU.mult)
                tt(S(33), S(33), S(34), ALU.add)
                ts(S(34), aim, -1.0, None, ALU.mult, ALU.bypass)
                cmul(S(31), S(32), S(30), S(28), are, S(34), S(5), S(6))
                tt(S(33), S(33), neg_one[:, 0:1].broadcast_to([P, NQ]), ALU.pow)
                tt(S(31), S(31), S(33), ALU.mult)
                tt(S(32), S(32), S(33), ALU.mult)
                lr, li, nli = spread(S(27), CH), spread(S(28), CH), spread(S(35), CH)
                u, v = (t_[:, 0:256].rearrange("p (q c) -> p q c", c=CH) for t_ in (pt1, pt2))
                for i in range(T + 1):
                    gen = i % 2
                    if i:
                        cmul(cd[:, gen, 0], cd[:, gen, 1], lr, nli, cd[:, 1 - gen, 0], cd[:, 1 - gen, 1], u, v)
                    for g2 in range(2):
                        rows = slice(ST * g2, ST * g2 + ST)
                        copy(cw[rows, :, :, i, g2, :].rearrange("p r q c -> p (r q) c"),
                             cd[rows, gen].rearrange("p r q c -> p (r q) c"))
                cr, ci = spread(S(31), CH), spread(S(32), CH)

                def bps(r, s):
                    return bp[:, :, r, :, s, :]

                u4, v4 = (t_[:, 0:256].rearrange("p (a q c) -> p a q c", a=4, c=CH) for t_ in (pt1, pt2))

                def four(ap):
                    return ap.rearrange("p (a q) c -> p a q c", a=4)

                b4 = [b_raw[:, r].rearrange("p (a q) c -> p a q c", a=4) for r in range(2)]
                cmul4 = [four(cr), four(ci)]
                cmul(bps(0, 3), bps(1, 3), cmul4[0], cmul4[1], b4[0], b4[1], u4, v4)
                for s in (2, 1, 0):
                    cmul(bps(0, s), bps(1, s), four(lr), four(li), bps(0, s + 1), bps(1, s + 1), u4, v4)
                def make_tables():
                    link(nc.gpsimd.memset(cosn[:, :, 0:1], 1.0))
                    link(nc.gpsimd.memset(sinn[:, :, 0:1], 0.0))
                    copy(S(0), S(24))
                    copy(S(1), S(26))
                    n = 1
                    while n < NC:
                        big = [t_[:, 0:NQ * n].rearrange("p (q n) -> p q n", n=n) for t_ in (pt1, pt2)]
                        cmul(cosn[:, :, n:2 * n], sinn[:, :, n:2 * n], spread(S(0), n), spread(S(1), n),
                             cosn[:, :, 0:n], sinn[:, :, 0:n], big[0], big[1])
                        n *= 2
                        if n < NC:
                            cmul(S(2), S(3), S(0), S(1), S(0), S(1), S(5), S(6))
                            copy(S(0), S(2))
                            copy(S(1), S(3))
                    copy(decay[:, :, :], spread(S(29), NC))
                    nc.gpsimd.memset(decay[:, :, 0:1], 0.0).then_inc(tables_done, 1)

                for i in range(4):
                    if i:
                        pool.wait_ge(prep_mm, l * PREP + 4 + i)
                        pool.sem_inc(pool_held, 1)
                    for g2 in range(2):
                        rows = slice(ST * g2, ST * g2 + ST)
                        dst = w1[rows, :, :, :, g2, :].rearrange("p r q s c -> p (r q s) c")
                        ins = nc.gpsimd.tensor_copy(dst, bp[rows, i].rearrange("p r q s c -> p (r q s) c"))
                        if g2:
                            ins.then_inc(w1_done, 1)
                            pool.wait_ge(w1_done, l * 4 + i + 1)
                            pool.sem_inc(pool_held, 1)
                        else:
                            link(ins)
                    if i == 0:
                        make_tables()
                pool.wait_ge(prep_ev, l * PREP + PREP)
                dg = pt1[96:128, :].rearrange("p (q c) -> p q c", c=32)
                tt(dg, ident[96:128, 96:128].unsqueeze(1).broadcast_to([32, NQ, 32]),
                   spread(sv[96:128, 48:64], 32), ALU.mult)
                nc.gpsimd.tensor_tensor(m_sb[96:128, :, :], m_sb[96:128, :, :], dg, ALU.add).then_inc(msb_done, 1)
                pool.wait_ge(msb_done, l + 1)
                pool.sem_inc(pool_held, 1)
                squares(l, 1)
                pool.wait_ge(ms_done, l * 3 + 2)
                inv_sqrt(rstd_c[:, :], ms_c[:, :], rstd_done)
                link(nc.gpsimd.memset(gw[:].rearrange("p q f m -> p (q f m)"), 0.0))
                for j in range(T):
                    rows = slice(32 * j, 32 * j + 32)
                    copy(gw[rows, :, :, rows].rearrange("p q f m -> p (q f) m"),
                         gw_c[:].rearrange("p q f m -> p (q f) m"))
                pool.sem_inc(gw_done, 1)
                link(nc.gpsimd.memset(h_re[:, :, 0:1], 0.0))
                nc.gpsimd.memset(h_im[:, :, 0:1], 0.0).then_inc(ku_done, 1)
                pool.wait_ge(rot_done, l * 4 + 2)
                nc.gpsimd.tensor_tensor(t1[:, :, :], t1[:, :, :], t3[:, :, :], ALU.add).then_inc(turn_done, 1)
                pool.wait_ge(rot_done, l * 4 + 4)
                nc.gpsimd.tensor_tensor(t2[:, :, :], t2[:, :, :], h_re[:, :, 1:NC + 1], ALU.subtract).then_inc(turn_done, 1)
                pool.wait_ge(vms_done, l + 1)
                inv_sqrt(vrs[:, :], vms[:, :], vrs_done)
                pool.wait_ge(un_done, l * 4 + 2)
                nc.gpsimd.tensor_tensor(h_re[:, :, 1:NC + 1], h_re[:, :, 1:NC + 1], t2[:, :, :],
                                        ALU.subtract).then_inc(state_done, 1)
                pool.wait_ge(un_done, l * 4 + 4)
                nc.gpsimd.tensor_tensor(h_im[:, :, 1:NC + 1], h_im[:, :, 1:NC + 1], t3[:, :, :],
                                        ALU.add).then_inc(state_done, 1)
                for i in range(2):
                    pool.wait_ge(oms_done, l * 2 + i + 1)
                    inv_sqrt(ors[:, 2 * i:2 * i + 2], oms[:, 2 * i:2 * i + 2], ors_done)
                squares(l, 2)
                pool.wait_ge(ms_done, l * 3 + 3)
                inv_sqrt(rstd_c[:, :], ms_c[:, :], rstd_done)
                restart()
            squares(DEPTH, 0)
            pool.wait_ge(ms_done, DEPTH * 3 + 1)
            inv_sqrt(rstd_c[:, :], ms_c[:, :], rstd_done)


_INS = ["x", "norm_ffn1", "ffn1_w_in", "ffn1_w_out", "norm_mix", "mix_w_in", "ssm_a_re", "ssm_a_im", "ssm_log_dt",
        "ssm_b_re", "ssm_b_im", "ssm_c_re", "ssm_c_im", "ssm_d", "ssm_glu_w", "ssm_glu_b", "gm_v_gain", "gm_w_s",
        "gm_b_s", "gain_ssm_out", "gain_gm_out", "mix_w_out", "norm_ffn2", "ffn2_w_in", "ffn2_w_out", "norm_final"]


def kernel(**inputs):
    import concourse.bacc as bacc
    from concourse.bass_utils import run_bass_kernel_spmd

    nc = bacc.Bacc("TRN2", target_bir_lowering=False, num_devices=1, dynamic_dma_scratch_size=1024)
    arrays = {f"in_{n}": np.ascontiguousarray(inputs[n]) for n in _INS}
    aps = {n: nc.dram_tensor(f"in_{n}", arrays[f"in_{n}"].shape, F32, kind="ExternalInput").ap() for n in _INS}
    out = nc.dram_tensor("out", (1, L, D), F32, kind="ExternalOutput").ap()
    build(nc, aps, out)
    r = run_bass_kernel_spmd(nc, [arrays], core_ids=[0])
    return r.results[0]["out"]
```

```python
import math
from contextlib import ExitStack

import numpy as np
import concourse.bass as bass
from concourse import mybir

F32 = mybir.dt.float32
F32R = mybir.dt.float32r
I32 = mybir.dt.int32
ALU = mybir.AluOpType
ACT = mybir.ActivationFunctionType
AXX = mybir.AxisListType.X

DEPTH, L, D, P = 2, 256, 1024, 128
FF = 2816
KT = D // P
FT = FF // P
NB = KT // 2
G, CH, ST = 32, 16, 64
NQ = G // 2
T = 4
NC = L // T
HEADS = 4
EPS = 1e-6

RAW, RING = 3, 3
FFN_CH = FT + FT // 2
MIX0 = FFN_CH
FFN2 = MIX0 + 10
CHUNKS = FFN2 + FFN_CH
HALVES = 2 * CHUNKS
RAW_TURN = MIX0 + 6
HALF_TURN = 2 * MIX0 + 17


def raw_slot(c):
    return (c if c < RAW_TURN else c - 1) % RAW


def half_slot(h):
    return (h if h < HALF_TURN else h + 1) % RING


assert raw_slot(CHUNKS - 1) == RAW - 1 and half_slot(HALVES - 1) == RING - 1


def raw_uses(s, c):
    return sum(raw_slot(k) == s for k in range(c))


ACCS = 3 * (2 * FT + 8)
ACC_FFN, ACC_MIX = 3 * FT, 3 * FT + 3 * 8
GAIN_FIN = 3 * KT * DEPTH
GAIN_OUT = GAIN_FIN + KT
GAINS = GAIN_OUT + 2 * 4 * DEPTH
PREP = 8
LOADS, C_LOADS = 7, 8


def half_count(l, h):
    return l * HALVES + h + 1 + RING


def slot_free_count(l, h):
    return l * HALVES + h + 1 + (1 if h in (HALF_TURN, HALF_TURN + 1) else 0)


def raw_free_count(l, c):
    return l * HALVES + 2 * c + (6 if c == RAW_TURN else 2)


def build(nc, a, out):
    stack = ExitStack()
    with stack:
        def sb(name, shape, dt=F32):
            return stack.enter_context(nc.sbuf_tensor(name, shape, dt))

        def sem(name):
            return stack.enter_context(nc.semaphore(name))

        with ExitStack() as first_use:
            h_hi = first_use.enter_context(nc.sbuf_tensor("h_hi", [P, FT, L], F32R))
            h_lo = first_use.enter_context(nc.sbuf_tensor("h_lo", [P, FT, L], F32R))
        gw = sb("gw", [P, NQ, 2, P])
        u_blk = sb("u_blk", [P, NQ, 2, 32])
        t1 = sb("t1", [P, NQ, NC])
        t2 = sb("t2", [P, NQ, NC])
        t3 = sb("t3", [P, NQ, NC])
        ug = sb("ug", [P, 2, 512])
        vg = sb("vg", [P, 2, 512])
        vn = sb("vn", [P, 2, 512])
        x_in = [t.rearrange("p q n -> p (q n)") for t in (t1[:], t2[:])]
        y_out = [t.rearrange("p h d -> p (h d)") for t in (ug[:], vg[:])]
        with ExitStack() as first_use:
            bp = first_use.enter_context(nc.sbuf_tensor("bp", [P, 4, 2, 4, T, CH], F32))
            b_raw = first_use.enter_context(nc.sbuf_tensor("b_raw", [P, 2, NQ, CH], F32))
        h_re = sb("h_re", [P, NQ, NC + 1])
        h_im = sb("h_im", [P, NQ, NC + 1])
        pad = sb("pad", [P, (10240 - 8 * NQ * (NC + 1)) // 4])

        raw = sb("raw", [P, RAW, 2048])
        w_hi = sb("w_hi", [P, RING, 1024], F32R)
        w_lo = sb("w_lo", [P, RING, 1024], F32R)
        x = sb("x", [P, KT, L])
        x_hi = sb("x_hi", [P, KT, L], F32R)
        x_lo = sb("x_lo", [P, KT, L], F32R)
        cw = sb("cw", [P, 2, NQ, T + 1, 2, CH])
        eb = sb("eb", [P, NQ, 2, P])
        kt_w = sb("kt_w", [P, NQ, T, 32])
        cosn = sb("cosn", [P, NQ, NC])
        sinn = sb("sinn", [P, NQ, NC])
        decay = sb("decay", [P, NQ, NC])
        gw_c = sb("gw_c", [32, NQ, 2, 32])
        ws_raw = sb("ws_raw", [P, HEADS, P])
        ws_p = sb("ws_p", [P, HEADS, P])
        ws_t = ws_raw
        vgain = sb("vgain", [P, 512])
        vg_row = sb("vg_row", [1, 512])
        ident = sb("ident", [P, P])
        ones = sb("ones", [P, P])
        neg_half = sb("neg_half", [P, 1])
        neg_one = sb("neg_one", [P, 1])
        gain_rows = ws_p[0:GAINS, 0, :]
        gains = sb("gains", [P, GAINS])
        gain = sb("gain", [P, 32])
        gate_s = sb("gate_s", [P, L])
        up_s = sb("up_s", [P, L])
        hid = up_s
        xs2 = sb("xs2", [P, 3, L])
        diag = xs2[:, 2, :]
        rstd = sb("rstd", [P, L])
        two_ident = gate_s[:, 0:P]
        ms_c = sb("ms_c", [P, 2])
        rstd_c = sb("rstd_c", [P, 2])
        w1 = sb("w1", [P, 2, 4, T, 2, CH])
        m_sb = sb("m_sb", [P, NQ, 32])
        c_raw = sb("c_raw", [P, 2, 2, P])
        cd = bp[:, 0:2].rearrange("p a r b s c -> p (a r b s c)").rearrange(
            "p (e r q c) -> p e r q c", e=2, r=2, c=CH)
        pt1 = sb("pt1", [P, NQ * 32])
        pt2 = sb("pt2", [P, NQ * 32])
        xsq = [pt1, pt2]
        spk = sb("spk", [16, 6, P])
        sraw = sb("sraw", [16, 98])
        bs_raw = sb("bs_raw", [HEADS, P])
        bs_p = sb("bs_p", [HEADS, P])
        sv = sb("sv", [P, 100])
        b1h = sb("b1h", [P, NQ])
        sc = sb("sc", [P, 36, NQ])
        ki = sb("ki", [P, 2 * NQ], I32)
        vss = sb("vss", [P, 8])
        vms = sb("vms", [P, 8])
        vrs = sb("vrs", [P, 8])
        oss = sb("oss", [P, 4])
        oms = sb("oms", [P, 4])
        ors = sb("ors", [P, 4])

        bank = [stack.enter_context(nc.psum_tensor(f"bank{i}", [P, 512], F32)) for i in range(4)]
        acc = stack.enter_context(nc.psum_tensor("acc", [P, NB, 512], F32))
        e_re = acc[:, 0:2, :].rearrange("p b (q n) -> p (b q) n", n=NC)
        e_im = acc[:, 2:4, :].rearrange("p b (q n) -> p (b q) n", n=NC)

        raw_full = [sem(f"raw_full{i}") for i in range(RAW)]
        small_full, c_full, late_full = sem("small_full"), sem("c_full"), sem("late_full")
        x_full, gain_full = sem("x_full"), sem("gain_full")
        stored = sem("stored")
        hi_done, lo_done, half_done = sem("hi_done"), sem("lo_done"), sem("half_done")
        gu_read, gate_done, silu_done = sem("gu_read"), sem("gate_done"), sem("silu_done")
        hid_done, hhi_done, hlo_done = sem("hid_done"), sem("hhi_done"), sem("hlo_done")
        acc_done, x_done = sem("acc_done"), sem("x_done")
        xhi_done, xlo_done = sem("xhi_done"), sem("xlo_done")
        sqa_done, diag_done, row_done, rb_done = sem("sqa_done"), sem("diag_done"), sem("row_done"), sem("rb_done")
        sq_done, ssq_done, ms_done, rstd_done = sem("sq_done"), sem("ssq_done"), sem("ms_done"), sem("rstd_done")
        const_done, zero_done, gain_t, gain_done = sem("const_done"), sem("zero_done"), sem("gain_t"), sem("gain_done")
        gain_cp = sem("gain_cp")
        pool_chain = sem("pool_chain")
        pe_held, pool_held, sp_held, act_held = sem("pe_held"), sem("pool_held"), sem("sp_held"), sem("act_held")
        small_done, w1_done, prep_mm, prep_ev = sem("small_done"), sem("w1_done"), sem("prep_mm"), sem("prep_ev")
        msb_done, ktw_done, tables_done, gw_done = sem("msb_done"), sem("ktw_done"), sem("tables_done"), sem("gw_done")
        ku_done = sem("ku_done")
        zs_done, u_done, e_done, rot_done, turn_done = sem("zs_done"), sem("u_done"), sem("e_done"), sem("rot_done"), sem("turn_done")
        scan_done, un_done, state_done = sem("scan_done"), sem("un_done"), sem("state_done")
        v_done, vsq_done, vss_done, vms_done, vrs_done, vn_done = (
            sem("v_done"), sem("vsq_done"), sem("vss_done"), sem("vms_done"), sem("vrs_done"), sem("vn_done"))
        ug_done, s_done, gm_done = sem("ug_done"), sem("s_done"), sem("gm_done")
        y_done, yg_done, z_done, zb_done, tanh_done, o_done, yt_done = (
            sem("y_done"), sem("yg_done"), sem("z_done"), sem("zb_done"), sem("tanh_done"), sem("o_done"), sem("yt_done"))
        oss_done, oms_done, ors_done, on_done, yT_done = (
            sem("oss_done"), sem("oms_done"), sem("ors_done"), sem("on_done"), sem("yT_done"))
        fin_x, fin_t, fin_y, fin_y1 = sem("fin_x"), sem("fin_t"), sem("fin_y"), sem("fin_y1")

        yh_done, im_done = sem("yh_done"), sem("im_done")

        turned = ((acc[:, 0, :], acc[:, 1, :]), (bank[2][:, :], bank[3][:, :]))
        z_bank = ((bank[2], bank[3]), (bank[0], bank[1]))
        fin_banks = ((bank[0][:, :], bank[1][:, :]), (acc[:, 0, :], acc[:, 1, :]))

        def zs(h):
            return (t1, t2)[h][:].rearrange("p q n -> p (q n)")[:, 0:512]

        def x_fin(k):
            return raw[:, 0, k * L:k * L + L]

        def spread(ap, n):
            return ap.unsqueeze(2).broadcast_to([ap.shape[0], ap.shape[1], n])

        block = stack.enter_context(nc.Block())

        @block.sync
        def _(sp):
            def load(l, c, it, src, view):
                s = raw_slot(c)
                sp.wait_ge(lo_done, raw_free_count(l, c) + it * 6)
                sp.sem_inc(sp_held, 1)
                sp.dma_start(view(raw[:, s, :]), src).then_inc(raw_full[s], 32)

            def load_up(l, c, it, w_in, f):
                base = w_in[l].rearrange("(t p) m -> p t m", p=P)
                s = raw_slot(c)
                sp.wait_ge(lo_done, raw_free_count(l, c) + it * 6)
                sp.sem_inc(sp_held, 1)
                for half in range(2):
                    sp.dma_start(
                        raw[:, s, 1024 * half:1024 * half + 1024].rearrange("p (t m) -> p t m", t=KT),
                        base[:, :, bass.ds(f * P + half * FF, P)]).then_inc(raw_full[s], 16)

            def load_down(l, c, it, w_out, k2):
                src = w_out[l, bass.ds(k2 * 2 * P, 2 * P), :].rearrange("(t p) m -> p t m", p=P)
                load(l, c, it, src, lambda r: r.rearrange("p (t m) -> p t m", t=2))

            def load_ffn(l, c0, w_in, w_out):
                load_up(l, c0, 0, w_in, 0)
                if c0 == 0:
                    load_small(l)
                load_up(l, c0 + 1, 0, w_in, 1)
                load_up(l, c0 + 2, 0, w_in, 2)
                if c0 == 0:
                    load_c(l)
                    load_late(l)
                with sp.Fori(0, 6) as it:
                    for k in range(3):
                        load_up(l, c0 + 3 + k, it, w_in, it * 3 + 3 + k)
                load_up(l, c0 + 21, 0, w_in, 21)
                for k in range(2):
                    load_down(l, c0 + FT + k, 0, w_out, k)
                with sp.Fori(0, 3) as it:
                    for k in range(3):
                        load_down(l, c0 + FT + 2 + k, it, w_out, it * 3 + 2 + k)

            def small(dst, src, full=small_full):
                sp.dma_start(dst, src).then_inc(full, 16)

            def load_small(l):
                small(spk[:, 0, :], a["ssm_a_re"][l].rearrange("(q g) p -> q (g p)", g=2))
                small(spk[:, 1, :], a["ssm_a_im"][l].rearrange("(q g) p -> q (g p)", g=2))
                small(sraw[:, 0:2], a["ssm_log_dt"][l].rearrange("(q g) -> q g", g=2))
                small(sraw[:, 2:34], a["ssm_d"][l].rearrange("(q g) c -> q (g c)", g=2))
                small(sraw[:, 34:98], a["ssm_glu_b"][l].rearrange("(q g) e -> q (g e)", g=2))
                small(bs_raw[:, :], a["gm_b_s"][l])
                small(ws_raw[:, :, :], a["gm_w_s"][l].rearrange("h t s -> t h s"))

            def load_c(l):
                for i, name in enumerate(("ssm_c_re", "ssm_c_im")):
                    for q8 in range(2):
                        for g2 in range(2):
                            small(c_raw[:, i, q8, g2 * ST:(g2 + 1) * ST],
                                  a[name][l].rearrange("(q g) c p -> q g c p", g=2)[8 * q8:8 * q8 + 8, g2], c_full)

            def load_late(l):
                sp.wait_ge(const_done, 2)
                for i, name in enumerate(("ssm_b_re", "ssm_b_im")):
                    small(b_raw[:, i, :, :], a[name][l].rearrange("(q g) p c -> (g p) q c", g=2), late_full)
                small(vg_row[:, :], a["gm_v_gain"][bass.ds(l, 1), :], late_full)
                gl = a["ssm_glu_w"][l].rearrange("(q g) c (f e) -> g f c q e", g=2, f=2)
                for g2 in range(2):
                    for f in range(2):
                        small(gw_c[g2 * CH:(g2 + 1) * CH, :, f, g2 * CH:(g2 + 1) * CH], gl[g2, f], late_full)

            xv = a["x"][0].rearrange("(h n j) d -> j n h d", j=T, n=32)
            for j in range(T):
                for h in range(2):
                    sp.dma_start(x_in[h][32 * j:32 * j + 32, :], xv[j, :, h, :]).then_inc(x_full, 16)
            with sp.Fori(0, DEPTH) as l:
                load_ffn(l, 0, a["ffn1_w_in"], a["ffn1_w_out"])
                for k in range(6):
                    col = (0, 1024, 512)[k // 2]
                    src = a["mix_w_in"][l, (k % 2) * 512:(k % 2) * 512 + 512, col:col + 512]
                    load(l, MIX0 + k, 0, src.rearrange("(t p) m -> p t m", p=P),
                         lambda r: r.rearrange("p (t m) -> p t m", t=4))
                for k in range(4):
                    k2 = (k + 2) % 4
                    load_down(l, MIX0 + 6 + k, 0, a["mix_w_out"], k2)
                load_ffn(l, FFN2, a["ffn2_w_in"], a["ffn2_w_out"])
            ov = out[0].rearrange("(h n j) d -> h j n d", j=T, n=32)
            for h in range(2):
                sp.wait_ge((fin_y, fin_y1)[h], 2)
                for j in range(T):
                    sp.dma_start(ov[h, j], y_out[h][32 * j:32 * j + 32, :]).then_inc(stored, 16)
            sp.wait_ge(stored, 2 * T * 16)

        @block.tensor
        def _(pe):
            mm = nc.tensor.matmul

            def split_ready(l, h, it=0):
                pe.wait_ge(lo_done, l * HALVES + h + 1 + 6 + it * 6)

            def three(o, hi_a, lo_a, hi_b, lo_b, first, last):
                mm(o, hi_a, hi_b, start=first, stop=False)
                mm(o, hi_a, lo_b, start=False, stop=False)
                return mm(o, lo_a, hi_b, start=False, stop=last)

            def up_half(l, c, it, ffn_i, f, half):
                if half == 0:
                    pe.wait_ge(gu_read, l * 2 * FT + ffn_i * FT + max(f + 1, 3) + it * 3)
                o = bank[f % 3]
                h = 2 * c + half
                s = half_slot(h)
                split_ready(l, h, it)
                for k in range(KT):
                    w = slice(k * P, k * P + P)
                    last = three(o[:, half * L:half * L + L], w_hi[:, s, w], w_lo[:, s, w],
                                 x_hi[:, k, :], x_lo[:, k, :], k == 0, k == KT - 1)
                last.then_inc(half_done, 1)

            def up_chunk(l, c, it, ffn_i, f):
                for half in range(2):
                    up_half(l, c, it, ffn_i, f, half)

            def up_first(l, c, ffn_i):
                pe.wait_ge(gu_read, l * 2 * FT + ffn_i * FT + 3)
                for half in range(2):
                    split_ready(l, 2 * c + half)
                for k in range(KT):
                    pe.wait_ge(xlo_done, l * 32 + 24 * ffn_i + k + 1)
                    w = slice(k * P, k * P + P)
                    for half in range(2):
                        s = half_slot(2 * c + half)
                        o = bank[0][:, half * L:half * L + L]
                        mm(o, w_hi[:, s, w], x_hi[:, k, :], start=k == 0 and half == 0, stop=False,
                           skip_group_check=True)
                        mm(o, w_hi[:, s, w], x_lo[:, k, :], start=False, stop=False, skip_group_check=True)
                        last = mm(o, w_lo[:, s, w], x_hi[:, k, :], start=False, stop=k == KT - 1,
                                  skip_group_check=True)
                        if k == KT - 1:
                            last.then_inc(half_done, 1)

            def down_half(l, h, it, hi_b, lo_b, first, last):
                s = half_slot(h)
                split_ready(l, h, it)
                for m in range(KT):
                    w = slice(m * P, m * P + P)
                    o = acc[:, m // 2, (m % 2) * L:(m % 2) * L + L]
                    mm(o, w_hi[:, s, w], hi_b, start=first and m % 2 == 0, stop=False, skip_group_check=True)
                    mm(o, w_hi[:, s, w], lo_b, start=False, stop=False, skip_group_check=True)
                    ins = mm(o, w_lo[:, s, w], hi_b, start=False, stop=last, skip_group_check=True)
                    if m == KT - 1:
                        ins.then_inc(half_done, 1)
                    elif m % 2:
                        ins.then_inc(acc_done, 1)

            def bank3_free(l, k):
                if k:
                    pe.wait_ge(prep_ev, l * PREP + k)
                else:
                    pe.wait_ge(rb_done, l * 2 + 1)

            def norm_sum(done):
                pe.wait_ge(sq_done, done)
                for h in range(2):
                    ins = mm(bank[3][:, h:h + 1], xs2[:, 0, h * P:h * P + P], ones[:, 0:1], start=True, stop=True)
                ins.then_inc(ssq_done, 1)

            def norm_row(l, ffn_i):
                pe.wait_ge(diag_done, l * 4 + 2 * ffn_i + 2)
                mm(bank[3][:, 0:L], ones[:, :], diag, start=True, stop=True).then_inc(row_done, 1)

            def prep_small(l):
                bank3_free(l, 0)
                pe.wait_ge(small_done, l * 2 + 1)
                pe.sem_inc(pe_held, 1)
                for i in range(6):
                    nc.tensor.transpose(bank[3][:, 16 * i:16 * i + 16], spk[:, i, :], ident[0:16, 0:16])
                nc.tensor.transpose(bank[3][:, 96:100], bs_p[:, :], ident[0:4, 0:4]).then_inc(prep_mm, 1)

            def prep_c(l):
                bank3_free(l, 1)
                pe.wait_ge(c_full, l * (C_LOADS * 16) + C_LOADS * 16)
                for i in range(2):
                    for q8 in range(2):
                        ins = nc.tensor.transpose(bank[3][:, (2 * i + q8) * P:(2 * i + q8 + 1) * P],
                                                  c_raw[:, i, q8, :], ident[:, :])
                ins.then_inc(prep_mm, 1)

            def prep_ws(l):
                bank3_free(l, 2)
                pe.wait_ge(small_done, l * 2 + 2)
                for i in range(HEADS):
                    ins = nc.tensor.transpose(bank[3][:, i * P:(i + 1) * P], ws_p[:, i, :], ident[:, :])
                ins.then_inc(prep_mm, 1)

            def prep_gain(l):
                bank3_free(l, 3)
                pe.wait_ge(late_full, l * (LOADS * 16) + LOADS * 16)
                mm(bank[3][:, :], ones[0:1, :], vg_row[:, :], start=True, stop=True).then_inc(prep_mm, 1)

            def prep_group(l, it, g):
                n = it * 2 + g
                pe.wait_ge(prep_ev, l * PREP + 4 + n)
                pe.wait_ge(w1_done, l * 4 + n + 1)
                pe.sem_inc(pe_held, 1)
                for k in range(2):
                    for q in range(4):
                        nc.tensor.transpose(bank[k][:, q * P:(q + 1) * P],
                                            w1[:, k, q].rearrange("p s g c -> p (s g c)"), ident[:, :])
                for q in range(4):
                    for r in range(2):
                        ins = mm(bank[2][:, q * 32:(q + 1) * 32],
                                 w1[:, r, q].rearrange("p s g c -> p (s g c)"),
                                 cw[:, r, bass.ds(n * 4 + q, 1), 0, :, :].rearrange("p q g c -> p (q g c)"),
                                 start=r == 0, stop=r == 1)
                ins.then_inc(prep_mm, 1)

            def ffn(l, ffn_i, c0):
                up_first(l, c0, ffn_i)
                up_half(l, c0 + 1, 0, ffn_i, 1, 0)
                norm_sum(l * 12 + 8 * ffn_i + 4)
                up_half(l, c0 + 1, 0, ffn_i, 1, 1)
                norm_row(l, ffn_i)
                up_chunk(l, c0 + 2, 0, ffn_i, 2)
                if ffn_i == 0:
                    prep_small(l)
                up_chunk(l, c0 + 3, 0, ffn_i, 3)
                if ffn_i == 0:
                    prep_c(l)
                with pe.Fori(0, 6) as it:
                    for k in range(3):
                        up_chunk(l, c0 + 4 + k, it, ffn_i, 4 + k)
                if ffn_i == 0:
                    prep_ws(l)
                base = l * 2 * FT + ffn_i * FT
                pe.wait_ge(hlo_done, base + 20)
                d0 = 2 * (c0 + FT)
                for k in range(4):
                    down_half(l, d0 + k, 0, h_hi[:, k, :], h_lo[:, k, :], k == 0, False)
                    if k == 1 and ffn_i == 0:
                        prep_gain(l)
                pe.wait_ge(hlo_done, base + 23)
                pe.sem_inc(pe_held, 1)
                with pe.Fori(0, 2) as it:
                    for k in range(6):
                        r = bass.ds(it * 6 + 4 + k, 1)
                        down_half(l, d0 + 4 + k, it, h_hi[:, r, :].rearrange("p a c -> p (a c)"),
                                  h_lo[:, r, :].rearrange("p a c -> p (a c)"), False, False)
                        if ffn_i == 0 and k in (1, 4):
                            if k == 1:
                                pe.wait_ge(gu_read, base + FT + 3)
                            prep_group(l, it, k // 3)
                for k in range(6):
                    down_half(l, d0 + 16 + k, 0, h_hi[:, 16 + k, :], h_lo[:, 16 + k, :], False, k == 5)

            def in_half(l, k, half, banks):
                h = 2 * (MIX0 + k) + half
                s = half_slot(h)
                split_ready(l, h)
                for k2 in range(2):
                    kt = (k % 2) * 4 + half * 2 + k2
                    if k < 2:
                        pe.wait_ge(xlo_done, l * 32 + 8 + kt + 1)
                    w = slice(k2 * 512, k2 * 512 + 512)
                    for hh in range(2):
                        t = slice(hh * P, hh * P + P)
                        last = three(bank[banks[hh]][:, :], x_hi[:, kt, t], x_lo[:, kt, t],
                                     w_hi[:, s, w], w_lo[:, s, w], kt == 0, kt == KT - 1)
                last.then_inc(half_done, 1)

            def in_chunk(l, k, banks):
                for half in range(2):
                    in_half(l, k, half, banks)

            pe.sem_inc(half_done, RING - 1)
            pe.wait_ge(const_done, 1)
            pe.wait_ge(gain_full, 16 * 6)
            nc.tensor.transpose(bank[3][:, 0:GAINS], gain_rows[:, :], ident[0:GAINS, 0:GAINS]).then_inc(gain_t, 1)
            pe.wait_ge(x_full, 16 * 2 * T)
            for b in range(NB):
                for k in range(2):
                    for h in range(2):
                        c = (2 * b + k) * P
                        ins = mm(acc[:, b, k * L + h * P:k * L + h * P + P], x_in[h][:, c:c + P], two_ident,
                                 start=True, stop=True)
                if b < NB - 1:
                    ins.then_inc(acc_done, 1)
                else:
                    ins.then_inc(half_done, 1)
            pe.wait_ge(const_done, 2)
            pe.wait_ge(gain_done, 1)

            with pe.Fori(0, DEPTH) as l:
                ffn(l, 0, 0)

                in_chunk(l, 0, (0, 1))
                in_half(l, 1, 0, (0, 1))
                in_half(l, 1, 1, (0, 1))
                norm_sum(l * 12 + 8)
                pe.wait_ge(ms_done, l * 3 + 2)
                in_half(l, 2, 0, (2, 3))
                pe.wait_ge(u_done, l * 2 + 2)
                pe.wait_ge(prep_ev, l * PREP + PREP)
                for r, e in enumerate((e_re, e_im)):
                    for q in range(NQ):
                        ins = mm(e[:, q, :], eb[:, q, r, :], u_blk[:, q].rearrange("p h n -> p (h n)"),
                                 start=True, stop=True)
                ins.then_inc(e_done, 1)
                in_half(l, 2, 1, (2, 3))
                in_chunk(l, 3, (2, 3))
                in_chunk(l, 4, (0, 1))
                in_chunk(l, 5, (0, 1))
                pe.wait_ge(vn_done, l * 8 + 8)
                for i in range(HEADS):
                    ins = mm(bank[2 + i // 2][:, (i % 2) * L:(i % 2) * L + L], ws_t[:, i, :],
                             vn[:, :, i * P:(i + 1) * P], start=True, stop=True)
                ins.then_inc(s_done, 1)

                pe.wait_ge(ug_done, l * 2 + 2)
                pe.wait_ge(ktw_done, l * 10 + 10)

                def y_pass(weights, rows):
                    for q in range(NQ):
                        ins = mm(bank[q // 8][:, (q % 8) * NC:(q % 8 + 1) * NC], weights(q), rows(q),
                                 start=rows is own and q % 8 == 0, stop=rows is im, skip_group_check=True)
                        if rows is im and q % 8 == 7:
                            ins.then_inc(y_done, 1)

                def own(q):
                    return u_blk[:, q].rearrange("p h n -> p (h n)")

                def re(q):
                    return h_re[:, q, 0:NC]

                def im(q):
                    return h_im[:, q, 0:NC]

                y_pass(lambda q: kt_w[:, q].rearrange("p j c -> p (j c)"), own)
                pe.wait_ge(state_done, l + 1)
                pe.sem_inc(pe_held, 1)
                y_pass(lambda q: cw[:, 0, q, 1:T + 1].rearrange("p j g c -> p (j g c)"), re)
                pe.wait_ge(im_done, l + 1)
                pe.sem_inc(pe_held, 1)
                y_pass(lambda q: cw[:, 1, q, 1:T + 1].rearrange("p j g c -> p (j g c)"), im)

                def turn(src, o):
                    for b in range(2):
                        for i in (2 * b, 2 * b + 1):
                            for h in range(2):
                                c = (i % 2) * L + h * P
                                ins = nc.tensor.transpose(o[b][:, c:c + P], src[:, h, i * P:(i + 1) * P], ident[:, :])
                        ins.then_inc(yT_done, 1)

                pe.wait_ge(on_done, l * 4 + 2)
                pe.sem_inc(pe_held, 1)
                turn(vg, turned[0])

                pe.wait_ge(gw_done, l + 1)
                pe.wait_ge(gm_done, l * 4 + 4)
                for hf in range(2):
                    pe.wait_ge(yg_done, l * 2 + hf + 1)
                    for f in range(2):
                        for q in range(8):
                            ins = mm(z_bank[hf][f][:, q * NC:(q + 1) * NC], gw[:, 8 * hf + q, f, :],
                                     t1[:, 8 * hf + q, :], start=True, stop=True)
                    ins.then_inc(z_done, 1)

                def out_chunk(k, first, last):
                    for half in range(2):
                        kt = (4 + 2 * k + half) % KT
                        pe.wait_ge(xlo_done, l * 32 + 16 + (2 * k + half + 1 if k else 4))
                        down_half(l, 2 * (MIX0 + 6 + k) + half, 0, x_hi[:, kt, :], x_lo[:, kt, :],
                                  first and half == 0, last and half == 1)

                out_chunk(0, True, False)
                out_chunk(1, False, False)
                pe.wait_ge(on_done, l * 4 + 4)
                pe.sem_inc(pe_held, 1)
                turn(ug, turned[1])
                out_chunk(2, False, False)
                out_chunk(3, False, True)

                ffn(l, 1, FFN2)

            for k in range(KT):
                pe.wait_ge(fin_x, k + 1)
                for h in range(2):
                    src = x_fin(k)[:, h * P:h * P + P]
                    ins = nc.tensor.transpose(fin_banks[h][k // 4][:, (k % 4) * P:(k % 4 + 1) * P], src, ident[:, :])
            ins.then_inc(fin_t, 1)
            norm_sum(DEPTH * 12 + 4)

        @block.scalar
        def _(act):
            A = nc.scalar.activation

            def split_half(l, h, it=0):
                c = h // 2
                s = raw_slot(c)
                if h % 2 == 0:
                    act.wait_ge(raw_full[s], (l * raw_uses(s, CHUNKS) + raw_uses(s, c) + 1 + it) * 32)
                act.wait_ge(half_done, slot_free_count(l, h) + it * 6)
                A(w_hi[:, half_slot(h), :], raw[:, s, (h % 2) * 1024:(h % 2) * 1024 + 1024],
                  ACT.Copy).then_inc(hi_done, 1)

            def split(l, c, it=0):
                split_half(l, 2 * c, it)
                split_half(l, 2 * c + 1, it)

            def norm_in(l, n, c_next):
                def square(b):
                    if b > 1:
                        act.wait_ge(sq_done, l * 12 + 4 * n + b - 1)
                    A(xsq[b % 2][:, :], x[:, 2 * b:2 * b + 2, :].rearrange("p k c -> p (k c)"),
                      ACT.Square).then_inc(sqa_done, 1)

                for b in range(NB):
                    act.wait_ge(x_done, l * 12 + 4 * n + b + 1)
                    for k in (2 * b, 2 * b + 1):
                        if n == 2 and k == 2:
                            act.wait_ge(half_done, half_count(l, 2 * FFN2 - 1))
                        A(x_hi[:, k, :], x[:, k, :], ACT.Copy,
                          scale=gain[:, n * 8 + k:n * 8 + k + 1]).then_inc(xhi_done, 1)
                    if b == 0 and n == 1:
                        act.wait_ge(tables_done, l + 1)
                    if b < NB - 1:
                        square(b)
                split_half(l, 2 * c_next)
                square(NB - 1)
                split_half(l, 2 * c_next + 1)

            def hidden(l, ffn_i, f, it=None):
                n = l * 2 * FT + ffn_i * FT + f + 1 + (0 if it is None else it * 3)
                act.wait_ge(gate_done, n)
                A(gate_s[:, :], gate_s[:, :], ACT.Silu).then_inc(silu_done, 1)
                act.wait_ge(hid_done, n)
                if it is None:
                    dst = h_hi[:, f, :]
                else:
                    dst = h_hi[:, bass.ds(it * 3 + f, 1), :].rearrange("p a c -> p (a c)")
                A(dst, hid[:, :], ACT.Copy).then_inc(hhi_done, 1)

            def evac(l, k, dst, src, it=0):
                act.wait_ge(prep_mm, l * PREP + k + 1 + it * 3)
                A(dst, src, ACT.Copy).then_inc(prep_ev, 1)

            def prep_group(l, it, g):
                n = it * 2 + g
                q = bass.ds(n * 4, 4)
                act.wait_ge(prep_mm, l * PREP + 5 + n)
                act.sem_inc(act_held, 1)
                for k in range(2):
                    A(eb[:, q, k, :], bank[k][:, :].rearrange("p (q m) -> p q m", q=4), ACT.Copy)
                A(m_sb[:, q, :], bank[2][:, 0:P].rearrange("p (q m) -> p q m", q=4), ACT.Copy).then_inc(prep_ev, 1)

            def ffn(l, ffn_i, c0):
                split(l, c0 + 2)
                act.wait_ge(row_done, l * 2 + ffn_i + 1)
                A(rstd[:, :], bank[3][:, 0:L], ACT.Copy).then_inc(rb_done, 1)
                hidden(l, ffn_i, 0)
                split(l, c0 + 3)
                hidden(l, ffn_i, 1)
                split_half(l, 2 * c0 + 8)
                if ffn_i == 0:
                    evac(l, 0, sv[:, :], bank[3][:, 0:100])
                split_half(l, 2 * c0 + 9)
                hidden(l, ffn_i, 2)
                split_half(l, 2 * c0 + 10)
                if ffn_i == 0:
                    act.wait_ge(prep_mm, l * PREP + 2)
                    A(cd[:, 0, 0].rearrange("p q c -> p (q c)"), bank[3][:, 0:256], ACT.Copy)
                    A(cd[:, 0, 1].rearrange("p q c -> p (q c)"), bank[3][:, 256:512], ACT.Copy,
                      scale=-1.0).then_inc(prep_ev, 1)
                split_half(l, 2 * c0 + 11)
                hidden(l, ffn_i, 3)
                with act.Fori(0, 5) as it:
                    for k in range(3):
                        split(l, c0 + 6 + k, it)
                        hidden(l, ffn_i, 4 + k, it)
                for f in (19, 20):
                    split(l, c0 + f + 2)
                    hidden(l, ffn_i, f)
                split_half(l, 2 * c0 + 46)
                if ffn_i == 0:
                    evac(l, 2, ws_t[:].rearrange("p i (j n) -> p i j n", j=T),
                         bank[3][:, :].rearrange("p (i n j) -> p i j n", i=HEADS, j=T))
                split_half(l, 2 * c0 + 47)
                hidden(l, ffn_i, 21)
                split_half(l, 2 * c0 + 48)
                if ffn_i == 0:
                    evac(l, 3, vgain[:, :], bank[3][:, :])
                split_half(l, 2 * c0 + 49)
                with act.Fori(0, 2) as it:
                    split(l, c0 + 25, it)
                    if ffn_i == 0:
                        prep_group(l, it, 0)
                    split(l, c0 + 26, it)
                    split_half(l, 2 * c0 + 54, it)
                    if ffn_i == 0:
                        prep_group(l, it, 1)
                    split_half(l, 2 * c0 + 55, it)
                split(l, c0 + 31)
                split(l, c0 + 32)

            for i, name in enumerate(("norm_ffn1", "norm_mix", "norm_ffn2", "norm_final")):
                src = a[name] if name == "norm_final" else a[name].rearrange("l d -> (l d)")
                n = src.shape[0] // P
                act.dma_start(gain_rows[i * KT * DEPTH:i * KT * DEPTH + n, :],
                              src.rearrange("(t p) -> t p", p=P)).then_inc(gain_full, 16)
            for i, name in enumerate(("gain_ssm_out", "gain_gm_out")):
                first = GAIN_OUT + i * 4 * DEPTH
                act.dma_start(gain_rows[first:first + 4 * DEPTH, :],
                              a[name].rearrange("l (t p) -> (l t) p", p=P)).then_inc(gain_full, 16)
            act.wait_ge(gain_t, 1)
            A(gains[:, :], bank[3][:, 0:GAINS], ACT.Copy).then_inc(gain_done, 1)
            with act.Fori(0, DEPTH) as l:
                split(l, 0)
                act.wait_ge(gain_cp, l * 2 + 2)
                norm_in(l, 0, 1)
                ffn(l, 0, 0)
                split(l, MIX0)
                norm_in(l, 1, MIX0 + 1)
                split(l, MIX0 + 2)
                act.wait_ge(rstd_done, l * 3 + 2)
                act.wait_ge(half_done, half_count(l, 2 * MIX0 + 3))
                for h in range(2):
                    A(zs(h), bank[h][:, :], ACT.Copy, scale=rstd_c[:, h:h + 1]).then_inc(zs_done, 1)
                split(l, MIX0 + 3)
                split(l, MIX0 + 4)
                act.wait_ge(half_done, half_count(l, 2 * MIX0 + 7))
                for h in range(2):
                    A(vg[:, h, :], bank[2 + h][:, :], ACT.Gelu_apprx_tanh, scale=rstd_c[:, h:h + 1]).then_inc(v_done, 1)
                act.wait_ge(v_done, l * 2 + 2)
                A(vn[:, :, :], vg[:, :, :], ACT.Square).then_inc(vsq_done, 1)
                split(l, MIX0 + 5)
                act.wait_ge(half_done, half_count(l, 2 * MIX0 + 11))
                for h in range(2):
                    A(ug[:, h, :], bank[h][:, :], ACT.Gelu_apprx_tanh, scale=rstd_c[:, h:h + 1]).then_inc(ug_done, 1)

                def row_sums(src, n):
                    for h in range(2):
                        A(xsq[h][:, :], src[:, h, :], ACT.Square,
                          accum_out=oss[:, 2 * n + h:2 * n + h + 1]).then_inc(oss_done, 1)

                split(l, MIX0 + 6)
                split_half(l, 2 * MIX0 + 14)
                act.wait_ge(gm_done, l * 4 + 4)
                row_sums(vg, 0)
                for hf in range(2):
                    act.wait_ge(y_done, l * 2 + hf + 1)
                    A(t1[:, 8 * hf:8 * hf + 8, :].rearrange("p q n -> p (q n)"), bank[hf][:, :],
                      ACT.Gelu_apprx_tanh).then_inc(yg_done, 1)
                for hf in range(2):
                    act.wait_ge(zb_done, l * 4 + 2 * hf + 1)
                    A(t2[:, 8 * hf:8 * hf + 8, :], t2[:, 8 * hf:8 * hf + 8, :], ACT.Tanh,
                      scale=0.5).then_inc(tanh_done, 1)
                split_half(l, 2 * MIX0 + 15)
                act.wait_ge(yt_done, l * 2 + 2)
                act.wait_ge(oss_done, l * 4 + 2)
                row_sums(ug, 1)
                split(l, MIX0 + 8)
                split(l, MIX0 + 9)
                split(l, FFN2)
                norm_in(l, 2, FFN2 + 1)
                ffn(l, 1, FFN2)
            for b in range(NB):
                act.wait_ge(x_done, DEPTH * 12 + b + 1)
                if b > 1:
                    act.wait_ge(sq_done, DEPTH * 12 + b - 1)
                A(xsq[b % 2][:, :], x[:, 2 * b:2 * b + 2, :].rearrange("p k c -> p (k c)"),
                  ACT.Square).then_inc(sqa_done, 1)
            act.wait_ge(rstd_done, 3 * DEPTH + 1)
            act.wait_ge(fin_t, 1)
            for b in range(2):
                A(y_out[1][:, b * 512:b * 512 + 512], fin_banks[1][b], ACT.Copy,
                  scale=rstd_c[:, 1:2]).then_inc(fin_y1, 1)

        @block.vector
        def _(dve):
            TT, TS, STT = nc.vector.tensor_tensor, nc.vector.tensor_scalar, nc.vector.scalar_tensor_tensor

            def split_half(l, h, it=0):
                s = raw_slot(h // 2)
                dve.wait_ge(hi_done, l * HALVES + h + 1 + it * 6)
                TT(w_lo[:, half_slot(h), :], raw[:, s, (h % 2) * 1024:(h % 2) * 1024 + 1024],
                   w_hi[:, half_slot(h), :].bitcast(F32), ALU.subtract).then_inc(lo_done, 1)

            def split(l, c, it=0):
                split_half(l, 2 * c, it)
                split_half(l, 2 * c + 1, it)

            def norm_lo(l, n, k):
                dve.wait_ge(xhi_done, l * 24 + n * 8 + k + 1)
                STT(x_lo[:, k, :], x[:, k, :], gain[:, n * 8 + k:n * 8 + k + 1], x_hi[:, k, :].bitcast(F32),
                    ALU.mult, ALU.subtract).then_inc(xlo_done, 1)

            def residual(l, b, accs, last_half, scale):
                if b < NB - 1:
                    dve.wait_ge(acc_done, l * ACCS + accs + b + 1)
                else:
                    dve.wait_ge(half_done, half_count(l, last_half))
                xb = x[:, 2 * b:2 * b + 2, :].rearrange("p k c -> p (k c)")
                STT(xb, acc[:, b, :], scale, xb, ALU.mult, ALU.add).then_inc(x_done, 1)

            def residual_norm(l, n, accs, last_half, scale, h_next):
                residual(l, 0, accs, last_half, scale)
                split_half(l, h_next)
                for b in range(NB):
                    if b < NB - 1:
                        residual(l, b + 1, accs, last_half, scale)
                    norm_lo(l, n, 2 * b)
                    norm_lo(l, n, 2 * b + 1)

            def mean(l, n):
                dve.wait_ge(ssq_done, l * 3 + n + 1)
                TS(ms_c[:, :], bank[3][:, 0:2], 1.0 / D, EPS, ALU.mult, ALU.add).then_inc(ms_done, 1)

            def norm_diag(l, ffn_i):
                dve.wait_ge(rstd_done, l * 3 + 2 * ffn_i + 1)
                for h in range(2):
                    TS(diag[:, h * P:h * P + P], ident[:, :], rstd_c[:, h:h + 1], None, ALU.mult).then_inc(diag_done, 1)

            def hidden(l, ffn_i, c0, f, it=None):
                step = 0 if it is None else it
                n = l * 2 * FT + ffn_i * FT + f + 1 + step * 3
                dve.wait_ge(half_done, half_count(l, 2 * (c0 + f) + 1) + step * 6)
                if f == 0:
                    dve.wait_ge(rb_done, l * 2 + ffn_i + 1)
                o = bank[f % 3]
                TT(gate_s[:, :], o[:, 0:L], rstd[:, :], ALU.mult).then_inc(gate_done, 1)
                dve.wait_ge(hlo_done, n)
                TT(up_s[:, :], o[:, L:2 * L], rstd[:, :], ALU.mult).then_inc(gu_read, 1)
                dve.wait_ge(silu_done, n)
                dve.wait_ge(gu_read, n + 3)
                TT(hid[:, :], gate_s[:, :], up_s[:, :], ALU.mult).then_inc(hid_done, 1)
                dve.wait_ge(hhi_done, n)
                if it is None:
                    hi, lo = h_hi[:, f, :], h_lo[:, f, :]
                else:
                    r = bass.ds(it * 3 + f, 1)
                    hi, lo = (t[:, r, :].rearrange("p a c -> p (a c)") for t in (h_hi, h_lo))
                TT(lo, hid[:, :], hi.bitcast(F32), ALU.subtract).then_inc(hlo_done, 1)

            def ffn(l, ffn_i, c0):
                split(l, c0 + 1)
                mean(l, 2 * ffn_i)
                norm_diag(l, ffn_i)
                for f in range(3):
                    split(l, c0 + 2 + f)
                    hidden(l, ffn_i, c0, f)
                with dve.Fori(0, 6) as it:
                    for k in range(3):
                        split(l, c0 + 5 + k, it)
                        hidden(l, ffn_i, c0, 3 + k, it)
                split(l, c0 + 23)
                hidden(l, ffn_i, c0, 21)
                with dve.Fori(0, 2) as it:
                    for k in range(3):
                        split(l, c0 + 24 + k, it)
                for k in range(2):
                    split(l, c0 + 30 + k)
                if ffn_i == 0:
                    dve.wait_ge(msb_done, l + 1)
                    for j in range(T):
                        for s in range(j + 1):
                            r = 32 * (T - 1 - (j - s))
                            nc.vector.tensor_copy(kt_w[32 * s:32 * s + 32, :, j, :],
                                                  m_sb[r:r + 32, :, :]).then_inc(ktw_done, 1)
                split(l, c0 + 32)

            dve.sem_inc(lo_done, 6)
            dve.sem_inc(hlo_done, 1)
            dve.sem_inc(gu_read, 3)
            nc.vector.memset(x[:, :, :], 0.0).then_inc(zero_done, 1)
            dve.wait_ge(zero_done, 1)
            with dve.Fori(0, DEPTH) as l:
                dve.wait_ge(gain_done, 1)
                for first, kinds, n, src in ((0, 3, KT, 0), (3 * KT, 2, 4, GAIN_OUT)):
                    nc.vector.tensor_copy(
                        gain[:, first:first + kinds * n].rearrange("p (i l t) -> p i l t", i=kinds, l=1),
                        gains[:, src:src + kinds * n * DEPTH].rearrange("p (i l t) -> p i l t", i=kinds, l=DEPTH)[
                            :, :, bass.ds(l, 1), :]).then_inc(gain_cp, 1)
                dve.wait_ge(gain_cp, l * 2 + 2)
                split_half(l, 0)
                residual_norm(l, 0, 0, -1, 0.5, 1)
                ffn(l, 0, 0)

                split_half(l, 2 * MIX0)
                residual_norm(l, 1, ACC_FFN, 2 * MIX0 - 1, 0.5, 2 * MIX0 + 1)
                split(l, MIX0 + 1)
                split_half(l, 2 * MIX0 + 4)
                mean(l, 1)
                split_half(l, 2 * MIX0 + 5)
                for h in range(2):
                    dve.wait_ge(zs_done, l * 2 + h + 1)
                    nc.vector.transpose(u_blk[:, :, h, :], zs(h).rearrange("p (q c) -> p q c", c=32)).then_inc(u_done, 1)
                split(l, MIX0 + 3)
                dve.wait_ge(e_done, l + 1)
                dve.wait_ge(u_done, l * 2 + 2)
                dve.wait_ge(tables_done, l + 1)
                dve.wait_ge(ku_done, l + 1)
                TT(t1[:, :, :], e_re, cosn[:, :, :], ALU.mult).then_inc(rot_done, 1)
                TT(t3[:, :, :], e_im, sinn[:, :, :], ALU.mult).then_inc(rot_done, 1)
                TT(t2[:, :, :], e_im, cosn[:, :, :], ALU.mult).then_inc(rot_done, 1)
                TT(h_re[:, :, 1:NC + 1], e_re, sinn[:, :, :], ALU.mult).then_inc(rot_done, 1)
                split_half(l, 2 * MIX0 + 8)
                flat = "p q n -> p (q n)"
                dve.wait_ge(turn_done, l * 2 + 1)
                nc.vector.tensor_tensor_scan(t3[:].rearrange(flat), decay[:].rearrange(flat), t1[:].rearrange(flat),
                                             0.0, ALU.mult, ALU.add).then_inc(scan_done, 1)
                split_half(l, 2 * MIX0 + 9)
                dve.wait_ge(turn_done, l * 2 + 2)
                dve.wait_ge(scan_done, l * 2 + 1)
                nc.vector.tensor_tensor_scan(t1[:].rearrange(flat), decay[:].rearrange(flat), t2[:].rearrange(flat),
                                             0.0, ALU.mult, ALU.add).then_inc(scan_done, 1)
                dve.wait_ge(vsq_done, l + 1)
                nc.vector.tensor_reduce(vss[:, :], vn[:].rearrange("p h (i d) -> p (h i) d", d=P), AXX,
                                        ALU.add).then_inc(vss_done, 1)
                dve.wait_ge(vss_done, l + 1)
                TS(vms[:, :], vss[:, :], 1.0 / P, EPS, ALU.mult, ALU.add).then_inc(vms_done, 1)
                split_half(l, 2 * MIX0 + 10)
                dve.wait_ge(scan_done, l * 2 + 2)
                TT(h_re[:, :, 1:NC + 1], t3[:, :, :], cosn[:, :, :], ALU.mult).then_inc(un_done, 1)
                TT(t2[:, :, :], t1[:, :, :], sinn[:, :, :], ALU.mult).then_inc(un_done, 1)
                split_half(l, 2 * MIX0 + 11)
                dve.wait_ge(vrs_done, l + 1)
                dve.wait_ge(prep_ev, l * PREP + PREP)
                for h in range(2):
                    for i in range(HEADS):
                        w = slice(i * P, i * P + P)
                        STT(vn[:, h, w], vg[:, h, w], vrs[:, h * HEADS + i:h * HEADS + i + 1], vgain[:, w],
                            ALU.mult, ALU.mult).then_inc(vn_done, 1)
                TT(h_im[:, :, 1:NC + 1], t3[:, :, :], sinn[:, :, :], ALU.mult).then_inc(un_done, 1)
                dve.wait_ge(un_done, l * 4 + 3)
                TT(t3[:, :, :], t1[:, :, :], cosn[:, :, :], ALU.mult).then_inc(un_done, 1)
                dve.wait_ge(un_done, l * 4 + 4)
                TT(h_im[:, :, 1:NC + 1], h_im[:, :, 1:NC + 1], t3[:, :, :], ALU.add).then_inc(im_done, 1)
                split(l, MIX0 + 6)
                dve.wait_ge(s_done, l + 1)
                dve.wait_ge(ug_done, l * 2 + 2)
                dve.wait_ge(vn_done, l * 8 + 8)
                for i in range(HEADS):
                    w = slice(i * P, i * P + P)
                    STT(vg[:, :, w], bank[2 + i // 2][:, (i % 2) * L:(i % 2) * L + L].rearrange("p (h d) -> p h d", h=2),
                        sv[:, 96 + i:97 + i], ug[:, :, w], ALU.add, ALU.mult).then_inc(gm_done, 1)

                def out_norm(y, n):
                    dve.wait_ge(oss_done, l * 4 + 2 * n + 2)
                    TS(oms[:, 2 * n:2 * n + 2], oss[:, 2 * n:2 * n + 2], 1.0 / 512, EPS, ALU.mult,
                       ALU.add).then_inc(oms_done, 1)
                    dve.wait_ge(ors_done, l * 2 + n + 1)
                    for h in range(2):
                        TS(y[:, h, :], y[:, h, :], ors[:, 2 * n + h:2 * n + h + 1], None, ALU.mult).then_inc(on_done, 1)

                def out_split(first, n, tiles=range(4)):
                    for i in tiles:
                        k = first + i
                        src = turned[n][i // 2][:, (i % 2) * L:(i % 2) * L + L]
                        g = gain[:, 24 + k:25 + k]
                        dve.wait_ge(yT_done, l * 4 + 2 * n + i // 2 + 1)
                        TS(x_hi[:, k, :], src, g, None, ALU.mult).then_inc(yh_done, 1)
                        dve.wait_ge(yh_done, l * 8 + 4 * n + i + 1)
                        STT(x_lo[:, k, :], src, g, x_hi[:, k, :].bitcast(F32), ALU.mult,
                            ALU.subtract).then_inc(xlo_done, 1)

                split_half(l, 2 * MIX0 + 14)
                out_norm(vg, 0)
                out_split(4, 0)
                for hf in range(2):
                    dve.wait_ge(z_done, l * 2 + hf + 1)
                    q = slice(8 * hf, 8 * hf + 8)
                    v = [z_bank[hf][f][:, :].rearrange("p (q n) -> p q n", n=NC) for f in range(2)]
                    TT(t2[:, q, :], v[1], spread(sv[:, 80 + 8 * hf:88 + 8 * hf], NC), ALU.add).then_inc(zb_done, 1)
                    STT(t3[:, q, :], v[0], 0.5, spread(b1h[:, q], NC), ALU.mult, ALU.add).then_inc(zb_done, 1)
                for hf in range(2):
                    dve.wait_ge(tanh_done, l * 2 + hf + 1)
                    dve.wait_ge(zb_done, l * 4 + 2 * hf + 2)
                    q = slice(8 * hf, 8 * hf + 8)
                    STT(t3[:, q, :], t2[:, q, :], 1.0, t3[:, q, :], ALU.add, ALU.mult).then_inc(o_done, 1)
                dve.wait_ge(o_done, l * 2 + 2)
                for h in range(2):
                    nc.vector.transpose(ug[:, h, :].rearrange("p (q c) -> p q c", c=32),
                                        t3[:, :, 32 * h:32 * h + 32]).then_inc(yt_done, 1)
                split_half(l, 2 * MIX0 + 15)
                out_norm(ug, 1)
                split_half(l, 2 * MIX0 + 16)
                out_split(0, 1, (0, 1))
                split_half(l, 2 * MIX0 + 17)
                out_split(0, 1, (2, 3))
                split(l, MIX0 + 9)
                split_half(l, 2 * FFN2)
                residual_norm(l, 2, ACC_MIX, 2 * FFN2 - 1, 1.0, 2 * FFN2 + 1)
                ffn(l, 1, FFN2)
            for b in range(NB):
                residual(DEPTH, b, 0, -1, 0.5)
                dve.wait_ge(x_done, DEPTH * 12 + b + 1)
                for k in (2 * b, 2 * b + 1):
                    TS(x_fin(k), x[:, k, :], gains[:, GAIN_FIN + k:GAIN_FIN + k + 1], None, ALU.mult).then_inc(fin_x, 1)
            dve.wait_ge(ssq_done, 3 * DEPTH + 1)
            TS(ms_c[:, :], bank[3][:, 0:2], 1.0 / D, EPS, ALU.mult, ALU.add).then_inc(ms_done, 1)
            dve.wait_ge(rstd_done, 3 * DEPTH + 1)
            dve.wait_ge(fin_t, 1)
            for b in range(2):
                TS(y_out[0][:, b * 512:b * 512 + 512], fin_banks[0][b], rstd_c[:, 0:1], None,
                   ALU.mult).then_inc(fin_y, 1)

        @block.gpsimd
        def _(pool):
            steps = [0]

            def link(ins):
                steps[0] += 1
                ins.then_inc(pool_chain, 1)
                pool.wait_ge(pool_chain, steps[0])

            def restart():
                steps[0] = 0
                pool.sem_inc(pool_held, 1)
                pool.sem_clear(pool_chain)

            def tt(o, x0, x1, op):
                link(nc.gpsimd.tensor_tensor(o, x0, x1, op))

            def ts(o, x0, s1, s2, op0, op1):
                link(nc.gpsimd.tensor_scalar(o, x0, s1, s2, op0, op1))

            def copy(o, i):
                link(nc.gpsimd.tensor_copy(o, i))

            def inv_sqrt(o, m, done):
                n = neg_half[:, 0:1]
                ins = nc.gpsimd.tensor_tensor(o, m, n.broadcast_to([P, m.shape[1]]), ALU.pow)
                ins.then_inc(done, 1)

            def squares(l, n):
                for b in range(NB):
                    pool.wait_ge(sqa_done, l * 12 + 4 * n + b + 1)
                    lo, hi = xsq[b % 2][:, 0:L], xsq[b % 2][:, L:2 * L]
                    if b == 0:
                        ins = nc.gpsimd.tensor_tensor(xs2[:, 0, :], lo, hi, ALU.add)
                    else:
                        tt(xs2[:, 1, :], lo, hi, ALU.add)
                        ins = nc.gpsimd.tensor_tensor(xs2[:, 0, :], xs2[:, 0, :], xs2[:, 1, :], ALU.add)
                    ins.then_inc(sq_done, 1)
                    pool.wait_ge(sq_done, l * 12 + 4 * n + b + 1)
                    pool.sem_inc(pool_held, 1)

            def cmul(o_re, o_im, a_re, a_im, b_re, b_im, u, v):
                tt(u, a_re, b_re, ALU.mult)
                tt(v, a_im, b_im, ALU.mult)
                tt(o_re, u, v, ALU.subtract)
                tt(u, a_re, b_im, ALU.mult)
                tt(v, a_im, b_re, ALU.mult)
                tt(o_im, u, v, ALU.add)

            def S(i, n=1):
                return sc[:, i:i + n, :].rearrange("p i q -> p (i q)")

            MAGIC = 12582912.0

            def horner(p, z, coefs):
                ts(p, z, coefs[0], coefs[1], ALU.mult, ALU.add)
                for c in coefs[2:]:
                    tt(p, p, z, ALU.mult)
                    ts(p, p, c, None, ALU.add, ALU.bypass)

            def exp(o, arg):
                xx, k, r, t, p = S(17), S(5), S(7), S(18), S(11)
                ts(xx, arg, -200.0, 200.0, ALU.max, ALU.min)
                ts(k, xx, 1.0 / math.log(2.0), MAGIC, ALU.mult, ALU.add)
                ts(k, k, -MAGIC, None, ALU.add, ALU.bypass)
                ts(t, k, -0.693359375, None, ALU.mult, ALU.bypass)
                tt(r, xx, t, ALU.add)
                ts(t, k, 2.12194440e-4, None, ALU.mult, ALU.bypass)
                tt(r, r, t, ALU.add)
                horner(p, r, [1 / 5040, 1 / 720, 1 / 120, 1 / 24, 1 / 6, 0.5, 1.0, 1.0])
                ts(k, k, -127.0, 128.0, ALU.max, ALU.min)
                ts(ki[:, 0:NQ], k, 127.0, 8388608.0, ALU.add, ALU.mult)
                tt(o, p, ki[:, 0:NQ].bitcast(F32), ALU.mult)

            link(nc.gpsimd.memset(ident[:, :], 0.0))
            link(nc.gpsimd.affine_select(out=ident[:, :], in_=ident[:, :], compare_op=ALU.not_equal, fill=1.0,
                                         base=0, pattern=[[-1, P]], channel_multiplier=1))
            link(nc.gpsimd.memset(two_ident, 0.0))
            link(nc.gpsimd.affine_select(out=two_ident, in_=two_ident, compare_op=ALU.not_equal, fill=2.0,
                                         base=0, pattern=[[-1, P]], channel_multiplier=1))
            pool.sem_inc(const_done, 1)
            link(nc.gpsimd.memset(gw_c[:, :, :, :], 0.0))
            link(nc.gpsimd.memset(neg_half[:, :], -0.5))
            link(nc.gpsimd.memset(neg_one[:, :], -1.0))
            nc.gpsimd.memset(ones[:, :], 1.0).then_inc(const_done, 1)
            for t in (w1, cw, kt_w):
                v = t[:].rearrange(("p a b c d e -> p (a b c d e)" if len(t.shape) == 6 else "p a b c -> p (a b c)"))
                link(nc.gpsimd.memset(v, 0.0))
            restart()
            with pool.Fori(0, DEPTH) as l:
                squares(l, 0)
                pool.wait_ge(ms_done, l * 3 + 1)
                inv_sqrt(rstd_c[:, :], ms_c[:, :], rstd_done)
                pool.wait_ge(small_full, l * (LOADS * 16) + LOADS * 16)
                pool.sem_inc(pool_held, 1)
                copy(spk[:, 2, :].rearrange("q (g p) -> q g p", g=2), spread(sraw[:, 0:2], ST))
                for j in range(T):
                    w = slice(32 * j, 32 * j + 32)
                    copy(spk[:, 3, w], sraw[:, 2:34])
                    for f in range(2):
                        copy(spk[:, 4 + f, w].rearrange("q (g e) -> q g e", g=2),
                             sraw[:, 34:98].rearrange("q (g f e) -> q g f e", g=2, f=2)[:, :, f, :])
                ins = nc.gpsimd.tensor_copy(bs_p[:].rearrange("i (j n) -> i j n", j=T),
                                            bs_raw[:].rearrange("i (n j) -> i j n", j=T))
                ins.then_inc(small_done, 1)
                pool.wait_ge(gain_t, 1)
                link(nc.gpsimd.affine_select(out=ws_raw[:, :, :], in_=ws_raw[:, :, :],
                                             compare_op=ALU.is_ge, fill=0.0, base=0,
                                             pattern=[[0, HEADS], [-1, P]], channel_multiplier=1))
                for i in range(HEADS):
                    ins = nc.gpsimd.tensor_copy(ws_p[:, i, :].rearrange("p (j n) -> p j n", j=T),
                                                ws_raw[:, i, :].rearrange("p (n j) -> p j n", j=T))
                    if i < HEADS - 1:
                        link(ins)
                ins.then_inc(small_done, 1)
                pool.wait_ge(prep_ev, l * PREP + 2)
                pool.sem_inc(pool_held, 1)
                are, aim = sv[:, 0:16], sv[:, 16:32]
                ts(b1h[:, :], sv[:, 64:80], 0.5, None, ALU.mult, ALU.bypass)
                exp(S(0), sv[:, 32:48])
                tt(S(1), are, S(0), ALU.mult)
                tt(S(2), aim, S(0), ALU.mult)
                ts(S(3), S(2), 4.0, None, ALU.mult, ALU.bypass)
                exp(S(4), S(1))
                k, r, z, sn, cs, m, t, ca, cb = S(5, 2), S(7, 2), S(9, 2), S(11, 2), S(13, 2), S(15, 2), S(17, 2), S(19, 2), S(21, 2)
                ts(k, S(2, 2), 2.0 / math.pi, MAGIC, ALU.mult, ALU.add)
                ts(k, k, -MAGIC, None, ALU.add, ALU.bypass)
                ts(t, k, -1.5703125, None, ALU.mult, ALU.bypass)
                tt(r, S(2, 2), t, ALU.add)
                ts(t, k, -4.837512969970703125e-4, None, ALU.mult, ALU.bypass)
                tt(r, r, t, ALU.add)
                ts(t, k, -7.54978995489188216e-8, None, ALU.mult, ALU.bypass)
                tt(r, r, t, ALU.add)
                tt(z, r, r, ALU.mult)
                horner(sn, z, [-1.9515295891e-4, 8.3321608736e-3, -1.6666654611e-1])
                tt(sn, sn, z, ALU.mult)
                tt(sn, sn, r, ALU.mult)
                tt(sn, sn, r, ALU.add)
                horner(cs, z, [2.443315711809948e-5, -1.388731625493765e-3, 4.166664568298827e-2])
                tt(cs, cs, z, ALU.mult)
                ts(cs, cs, -0.5, None, ALU.add, ALU.bypass)
                tt(cs, cs, z, ALU.mult)
                ts(cs, cs, 1.0, None, ALU.add, ALU.bypass)
                ts(t, k, 0.25, MAGIC, ALU.mult, ALU.add)
                ts(t, t, -MAGIC, -4.0, ALU.add, ALU.mult)
                tt(m, k, t, ALU.add)
                ts(t, m, -1.0, 0.0, ALU.mult, ALU.max)
                ts(cb, m, 0.0, None, ALU.max, ALU.bypass)
                tt(t, t, cb, ALU.add)
                ts(ca, t, -1.0, 1.0, ALU.mult, ALU.add)
                ts(cb, t, -1.0, 2.0, ALU.mult, ALU.add)
                tt(cb, cb, m, ALU.mult)
                cmul(S(23, 2), S(25, 2), ca, cb, cs, sn, t, m)
                tt(S(27), S(4), S(23), ALU.mult)
                tt(S(28), S(4), S(25), ALU.mult)
                tt(S(29), S(4), S(4), ALU.mult)
                tt(S(29), S(29), S(29), ALU.mult)
                ts(S(35), S(28), -1.0, None, ALU.mult, ALU.bypass)
                ts(S(30), S(27), -1.0, None, ALU.add, ALU.bypass)
                tt(S(33), are, are, ALU.mult)
                tt(S(34), aim, aim, ALU.mult)
                tt(S(33), S(33), S(34), ALU.add)
                ts(S(34), aim, -1.0, None, ALU.mult, ALU.bypass)
                cmul(S(31), S(32), S(30), S(28), are, S(34), S(5), S(6))
                tt(S(33), S(33), neg_one[:, 0:1].broadcast_to([P, NQ]), ALU.pow)
                tt(S(31), S(31), S(33), ALU.mult)
                tt(S(32), S(32), S(33), ALU.mult)
                pool.wait_ge(late_full, l * (LOADS * 16) + LOADS * 16)
                pool.sem_inc(pool_held, 1)
                lr, li, nli = spread(S(27), CH), spread(S(28), CH), spread(S(35), CH)
                u, v = (t_[:, 0:256].rearrange("p (q c) -> p q c", c=CH) for t_ in (pt1, pt2))
                for i in range(T + 1):
                    gen = i % 2
                    if i:
                        cmul(cd[:, gen, 0], cd[:, gen, 1], lr, nli, cd[:, 1 - gen, 0], cd[:, 1 - gen, 1], u, v)
                    for g2 in range(2):
                        rows = slice(ST * g2, ST * g2 + ST)
                        copy(cw[rows, :, :, i, g2, :].rearrange("p r q c -> p (r q) c"),
                             cd[rows, gen].rearrange("p r q c -> p (r q) c"))
                cr, ci = spread(S(31), CH), spread(S(32), CH)

                def bps(r, s):
                    return bp[:, :, r, :, s, :]

                u4, v4 = (t_[:, 0:256].rearrange("p (a q c) -> p a q c", a=4, c=CH) for t_ in (pt1, pt2))

                def four(ap):
                    return ap.rearrange("p (a q) c -> p a q c", a=4)

                b4 = [b_raw[:, r].rearrange("p (a q) c -> p a q c", a=4) for r in range(2)]
                cmul4 = [four(cr), four(ci)]
                cmul(bps(0, 3), bps(1, 3), cmul4[0], cmul4[1], b4[0], b4[1], u4, v4)
                for s in (2, 1, 0):
                    cmul(bps(0, s), bps(1, s), four(lr), four(li), bps(0, s + 1), bps(1, s + 1), u4, v4)
                def make_tables(n, last):
                    if n == 1:
                        link(nc.gpsimd.memset(cosn[:, :, 0:1], 1.0))
                        link(nc.gpsimd.memset(sinn[:, :, 0:1], 0.0))
                        copy(S(0), S(24))
                        copy(S(1), S(26))
                    while n < last:
                        big = [t_[:, 0:NQ * n].rearrange("p (q n) -> p q n", n=n) for t_ in (pt1, pt2)]
                        cmul(cosn[:, :, n:2 * n], sinn[:, :, n:2 * n], spread(S(0), n), spread(S(1), n),
                             cosn[:, :, 0:n], sinn[:, :, 0:n], big[0], big[1])
                        n *= 2
                        if n < NC:
                            cmul(S(2), S(3), S(0), S(1), S(0), S(1), S(5), S(6))
                            copy(S(0), S(2))
                            copy(S(1), S(3))
                    if n == NC:
                        copy(decay[:, :, :], spread(S(29), NC))
                        nc.gpsimd.memset(decay[:, :, 0:1], 0.0).then_inc(tables_done, 1)

                for i in range(4):
                    if i:
                        pool.wait_ge(prep_mm, l * PREP + 4 + i)
                        pool.sem_inc(pool_held, 1)
                    for g2 in range(2):
                        rows = slice(ST * g2, ST * g2 + ST)
                        dst = w1[rows, :, :, :, g2, :].rearrange("p r q s c -> p (r q s) c")
                        ins = nc.gpsimd.tensor_copy(dst, bp[rows, i].rearrange("p r q s c -> p (r q s) c"))
                        if g2:
                            ins.then_inc(w1_done, 1)
                            pool.wait_ge(w1_done, l * 4 + i + 1)
                            pool.sem_inc(pool_held, 1)
                        else:
                            link(ins)
                    if i == 0:
                        make_tables(1, 16)
                    elif i == 1:
                        make_tables(16, 32)
                pool.wait_ge(prep_ev, l * PREP + PREP)
                dg = pt1[96:128, :].rearrange("p (q c) -> p q c", c=32)
                tt(dg, ident[96:128, 96:128].unsqueeze(1).broadcast_to([32, NQ, 32]),
                   spread(sv[96:128, 48:64], 32), ALU.mult)
                nc.gpsimd.tensor_tensor(m_sb[96:128, :, :], m_sb[96:128, :, :], dg, ALU.add).then_inc(msb_done, 1)
                pool.wait_ge(msb_done, l + 1)
                pool.sem_inc(pool_held, 1)
                make_tables(32, NC)
                squares(l, 1)
                pool.wait_ge(ms_done, l * 3 + 2)
                inv_sqrt(rstd_c[:, :], ms_c[:, :], rstd_done)
                def gw_block(j):
                    rows = slice(32 * j, 32 * j + 32)
                    copy(gw[rows, :, :, rows].rearrange("p q f m -> p (q f) m"),
                         gw_c[:].rearrange("p q f m -> p (q f) m"))

                link(nc.gpsimd.memset(h_re[:, :, 0:1], 0.0))
                nc.gpsimd.memset(h_im[:, :, 0:1], 0.0).then_inc(ku_done, 1)
                link(nc.gpsimd.memset(gw[:].rearrange("p q f m -> p (q f m)"), 0.0))
                gw_block(0)
                gw_block(1)
                pool.wait_ge(rot_done, l * 4 + 2)
                nc.gpsimd.tensor_tensor(t1[:, :, :], t1[:, :, :], t3[:, :, :], ALU.add).then_inc(turn_done, 1)
                pool.wait_ge(rot_done, l * 4 + 4)
                nc.gpsimd.tensor_tensor(t2[:, :, :], t2[:, :, :], h_re[:, :, 1:NC + 1], ALU.subtract).then_inc(turn_done, 1)
                pool.wait_ge(vms_done, l + 1)
                inv_sqrt(vrs[:, :], vms[:, :], vrs_done)
                pool.wait_ge(un_done, l * 4 + 2)
                nc.gpsimd.tensor_tensor(h_re[:, :, 1:NC + 1], h_re[:, :, 1:NC + 1], t2[:, :, :],
                                        ALU.subtract).then_inc(state_done, 1)
                pool.wait_ge(state_done, l + 1)
                pool.sem_inc(pool_held, 1)
                gw_block(2)
                gw_block(3)
                pool.sem_inc(gw_done, 1)
                for i in range(2):
                    pool.wait_ge(oms_done, l * 2 + i + 1)
                    inv_sqrt(ors[:, 2 * i:2 * i + 2], oms[:, 2 * i:2 * i + 2], ors_done)
                squares(l, 2)
                pool.wait_ge(ms_done, l * 3 + 3)
                inv_sqrt(rstd_c[:, :], ms_c[:, :], rstd_done)
                restart()
            squares(DEPTH, 0)
            pool.wait_ge(ms_done, DEPTH * 3 + 1)
            inv_sqrt(rstd_c[:, :], ms_c[:, :], rstd_done)


_INS = ["x", "norm_ffn1", "ffn1_w_in", "ffn1_w_out", "norm_mix", "mix_w_in", "ssm_a_re", "ssm_a_im", "ssm_log_dt",
        "ssm_b_re", "ssm_b_im", "ssm_c_re", "ssm_c_im", "ssm_d", "ssm_glu_w", "ssm_glu_b", "gm_v_gain", "gm_w_s",
        "gm_b_s", "gain_ssm_out", "gain_gm_out", "mix_w_out", "norm_ffn2", "ffn2_w_in", "ffn2_w_out", "norm_final"]


def kernel(**inputs):
    import concourse.bacc as bacc
    from concourse.bass_utils import run_bass_kernel_spmd

    nc = bacc.Bacc("TRN2", target_bir_lowering=False, num_devices=1, dynamic_dma_scratch_size=1024)
    arrays = {f"in_{n}": np.ascontiguousarray(inputs[n]) for n in _INS}
    aps = {n: nc.dram_tensor(f"in_{n}", arrays[f"in_{n}"].shape, F32, kind="ExternalInput").ap() for n in _INS}
    out = nc.dram_tensor("out", (1, L, D), F32, kind="ExternalOutput").ap()
    build(nc, aps, out)
    r = run_bass_kernel_spmd(nc, [arrays], core_ids=[0])
    return r.results[0]["out"]
```
